# Optimizing a Trainium2 kernel written in Bass

```python
import math
import jax, jax.numpy as jnp
from jax import lax
import numpy as np

D_MODEL = 1024
BATCH = 1
SEQ = 2048
DEPTH = 1

EPS = 1e-6
GLA_HEADS = 4
GLA_DK = 48
GLA_DV = 96
GLA_QK_WIDTH = GLA_HEADS * GLA_DK
GLA_WIDTH = GLA_HEADS * GLA_DV
GLA_RANK = 16
GLA_GATE_NORM = 16.0
GLA_CHUNK = 64
FOX_HEADS = 6
FOX_DH = 64
FOX_WIDTH = FOX_HEADS * FOX_DH
FOX_BLOCK = 128
MEM_LEN = 256
MEM_HEADS = 4
MEM_DH = 64
MEM_WIDTH = MEM_HEADS * MEM_DH
MIX_WIDTH = GLA_WIDTH + FOX_WIDTH + MEM_WIDTH
IN_SPLITS = (GLA_QK_WIDTH, GLA_QK_WIDTH, GLA_WIDTH, GLA_RANK, GLA_WIDTH,
             FOX_WIDTH, FOX_WIDTH, FOX_WIDTH, FOX_HEADS, FOX_WIDTH,
             MEM_WIDTH, MEM_WIDTH)
IN_COLS = sum(IN_SPLITS)

kernel_name = "hymba_gla_fox_memory_block"

def rmsnorm(x, g):
    xf = x.astype(jnp.float32)
    y = xf * lax.rsqrt(jnp.mean(xf * xf, axis=-1, keepdims=True) + EPS)
    return (y * g.astype(jnp.float32)).astype(x.dtype)

def gla_chunked(q, k, v, log_a):
    B, T, H, K = q.shape
    V = v.shape[-1]
    C = GLA_CHUNK
    N = T // C
    f32 = jnp.float32

    def chunks(a):
        return a.astype(f32).reshape(B, N, C, H, -1).transpose(1, 0, 3, 2, 4)

    qc = chunks(q) * (K ** -0.5)
    kc, vc, gc = chunks(k), chunks(v), chunks(log_a)
    b = jnp.cumsum(gc, axis=3)
    b_last = b[:, :, :, -1:, :]
    q_dec = qc * jnp.exp(b)
    k_dec = kc * jnp.exp(-b)
    k_to_end = kc * jnp.exp(b_last - b)
    causal = jnp.tril(jnp.ones((C, C), f32))
    attn = jnp.einsum('nbhck,nbhsk->nbhcs', q_dec, k_dec) * causal
    o_intra = jnp.einsum('nbhcs,nbhsv->nbhcv', attn, vc)
    kv_chunk = jnp.einsum('nbhsk,nbhsv->nbhkv', k_to_end, vc)
    decay_chunk = jnp.exp(b_last[:, :, :, 0, :])

    def step(S, inp):
        kv_n, dec_n = inp
        return dec_n[..., None] * S + kv_n, S

    _, S_prev = lax.scan(step, jnp.zeros((B, H, K, V), f32), (kv_chunk, decay_chunk))
    o_inter = jnp.einsum('nbhck,nbhkv->nbhcv', q_dec, S_prev)
    o = (o_intra + o_inter).transpose(1, 0, 3, 2, 4).reshape(B, T, H, V)
    return o

def fox_attention(q, k, v, log_f):
    B, T, H, D = q.shape
    nb = T // FOX_BLOCK
    scale = D ** -0.5
    c = jnp.cumsum(log_f.astype(jnp.float32), axis=1).transpose(0, 2, 1)
    kh = k.transpose(0, 2, 1, 3)
    vh = v.transpose(0, 2, 1, 3)
    q_blocks = q.transpose(0, 2, 1, 3).reshape(B, H, nb, FOX_BLOCK, D).transpose(2, 0, 1, 3, 4)
    c_blocks = c.reshape(B, H, nb, FOX_BLOCK).transpose(2, 0, 1, 3)
    starts = jnp.arange(nb, dtype=jnp.int32) * FOX_BLOCK
    key_pos = jnp.arange(T, dtype=jnp.int32)

    def one_block(args):
        qb, cb, start = args
        s = jnp.einsum('bhqd,bhkd->bhqk', qb, kh).astype(jnp.float32) * scale
        s = s + cb[..., :, None] - c[..., None, :]
        q_pos = start + jnp.arange(FOX_BLOCK, dtype=jnp.int32)
        mask = key_pos[None, :] <= q_pos[:, None]
        p = jax.nn.softmax(jnp.where(mask, s, -jnp.inf), axis=-1)
        return jnp.einsum('bhqk,bhkd->bhqd', p.astype(vh.dtype), vh)

    out = lax.map(one_block, (q_blocks, c_blocks, starts))
    return out.transpose(1, 0, 3, 2, 4).reshape(B, T, H * D)

def memory_attention(q, mk, mv):
    B, T, H, D = q.shape
    s = jnp.einsum('bthd,bmhd->bhtm', q, mk).astype(jnp.float32) * (D ** -0.5)
    p = jax.nn.softmax(s, axis=-1)
    o = jnp.einsum('bhtm,bmhd->bthd', p.astype(mv.dtype), mv)
    return o.reshape(B, T, H * D)

def hybrid_layer(x, mem, norm_g, w_in, w_alpha_up, b_alpha, b_forget, gla_norm_g,
                 mem_norm_g, w_mem_kv, w_out):
    B, T, _ = x.shape
    h = rmsnorm(x, norm_g)
    proj = h @ w_in
    idx = [int(i) for i in np.cumsum(IN_SPLITS)[:-1]]
    (g_q, g_k, g_v, g_lr, g_gate, f_q, f_k, f_v, f_fg, f_gate,
     m_q, m_gate) = jnp.split(proj, idx, axis=-1)

    z_alpha = g_lr @ w_alpha_up + b_alpha
    log_a = jax.nn.log_sigmoid(z_alpha.astype(jnp.float32)) / GLA_GATE_NORM
    o_gla = gla_chunked(g_q.reshape(B, T, GLA_HEADS, GLA_DK),
                        g_k.reshape(B, T, GLA_HEADS, GLA_DK),
                        g_v.reshape(B, T, GLA_HEADS, GLA_DV),
                        log_a.reshape(B, T, GLA_HEADS, GLA_DK))
    o_gla = rmsnorm(o_gla, gla_norm_g).reshape(B, T, GLA_WIDTH).astype(x.dtype)
    o_gla = o_gla * jax.nn.silu(g_gate)

    log_f = jax.nn.log_sigmoid((f_fg + b_forget).astype(jnp.float32))
    o_fox = fox_attention(f_q.reshape(B, T, FOX_HEADS, FOX_DH),
                          f_k.reshape(B, T, FOX_HEADS, FOX_DH),
                          f_v.reshape(B, T, FOX_HEADS, FOX_DH), log_f)
    o_fox = o_fox.astype(x.dtype) * jax.nn.silu(f_gate)

    mkv = rmsnorm(mem, mem_norm_g) @ w_mem_kv
    M = mem.shape[1]
    mk, mv = jnp.split(mkv, 2, axis=-1)
    o_mem = memory_attention(m_q.reshape(B, T, MEM_HEADS, MEM_DH),
                             mk.reshape(B, M, MEM_HEADS, MEM_DH),
                             mv.reshape(B, M, MEM_HEADS, MEM_DH))
    o_mem = o_mem.astype(x.dtype) * jax.nn.silu(m_gate)

    mixed = jnp.concatenate([o_gla, o_fox, o_mem], axis=-1)
    return x + mixed @ w_out

def setup_inputs(seed: int = 0) -> dict:
    key = jax.random.key(seed)
    ks = jax.random.split(key, 14)
    f32 = jnp.float32
    nrm = lambda k, s: jax.random.normal(k, s, f32)
    return {
        "x": nrm(ks[0], (BATCH, SEQ, D_MODEL)),
        "mem": nrm(ks[1], (BATCH, MEM_LEN, D_MODEL)),
        "norm_g": 1.0 + 0.02 * nrm(ks[2], (DEPTH, D_MODEL)),
        "w_in": nrm(ks[3], (DEPTH, D_MODEL, IN_COLS)) * D_MODEL ** -0.5,
        "w_alpha_up": nrm(ks[4], (DEPTH, GLA_RANK, GLA_QK_WIDTH)) * GLA_RANK ** -0.5,
        "b_alpha": 0.1 * nrm(ks[5], (DEPTH, GLA_QK_WIDTH)),
        "b_forget": 2.0 + 0.5 * nrm(ks[6], (DEPTH, FOX_HEADS)),
        "gla_norm_g": 1.0 + 0.02 * nrm(ks[7], (DEPTH, GLA_DV)),
        "mem_norm_g": 1.0 + 0.02 * nrm(ks[8], (DEPTH, D_MODEL)),
        "w_mem_kv": nrm(ks[9], (DEPTH, D_MODEL, 2 * MEM_WIDTH)) * D_MODEL ** -0.5,
        "w_out": nrm(ks[10], (DEPTH, MIX_WIDTH, D_MODEL)) * MIX_WIDTH ** -0.5,
        "final_norm_g": 1.0 + 0.02 * nrm(ks[11], (D_MODEL,)),
    }

def reference(x, mem, norm_g, w_in, w_alpha_up, b_alpha, b_forget, gla_norm_g,
              mem_norm_g, w_mem_kv, w_out, final_norm_g):
    h = x
    for layer in range(DEPTH):
        h = hybrid_layer(h, mem, norm_g[layer], w_in[layer], w_alpha_up[layer],
                         b_alpha[layer], b_forget[layer], gla_norm_g[layer],
                         mem_norm_g[layer], w_mem_kv[layer], w_out[layer])
    return rmsnorm(h, final_norm_g)


_drawn_inputs = setup_inputs


def setup_inputs(seed=0):
    import zlib

    import numpy as np

    out = dict(_drawn_inputs(seed))
    spreads = {}
    factors = {'norm_g': 3.728,
     'b_alpha': 3.483,
     'gla_norm_g': 8.0,
     'mem_norm_g': 8.0,
     'final_norm_g': 2.829}
    for name, (base, spread) in spreads.items():
        noise = np.random.default_rng([zlib.crc32(name.encode()), seed]).standard_normal(out[name].shape)
        drawn = base * np.exp(spread * noise) if base else spread * noise
        out[name] = __import__('jax').numpy.asarray(drawn.astype(out[name].dtype))
    for name, factor in factors.items():
        out[name] = (out[name] * factor).astype(out[name].dtype)
    return out
```

```python
import concourse.bass as bass
from concourse import mybir
from contextlib import ExitStack

F32 = mybir.dt.float32
F32R = mybir.dt.float32r
BF16 = mybir.dt.bfloat16
ALU = mybir.AluOpType
ACT = mybir.ActivationFunctionType
AX = mybir.AxisListType

P = 128
D = 1024
T = 2048
M = 256
KT = D // P
TT = T // P
EPS = 1e-6
CH = 512
NCH = T // CH

GLA_H, GLA_DK, GLA_DV, GLA_R, GLA_C, GLA_GATE = 4, 48, 96, 16, 64, 16.0
FOX_H, DH = 6, 64
MEM_H = 4
MIX_T = 8

TOK_C = FOX_H * DH + FOX_H + GLA_R
FGLR = FOX_H + GLA_R
NSPLIT, NGATE, NRAW = 8, 8, 6
NCOL = NSPLIT + NGATE + NRAW

IN = [192, 192, 384, 16, 384, 384, 384, 384, 6, 384, 256, 256]
OFF = [sum(IN[:i]) for i in range(len(IN) + 1)]
G_Q, G_K, G_V, G_LR, G_GATE, F_Q, F_K, F_V, F_FG, F_GATE, M_Q, M_GATE = OFF[:-1]

HI, LO = 0, 1
PASSES = [(HI, HI), (HI, LO), (LO, HI)]


class Scratch:

    def __init__(self, nc):
        def dram(name, shape, dt):
            return nc.dram_tensor(name, shape, dt).ap()
        self.split = dram("scr_split", [NSPLIT, 2, P, T], F32)
        self.gates = dram("scr_gates", [NGATE, P, T], F32)
        self.raw = dram("scr_raw", [NRAW * P, T], F32)
        self.fox_v = dram("scr_fox_v", [FOX_H, P, TT, 2 * DH], F32)
        self.mem_k = dram("scr_mem_k", [2, 2, P, M], F32)
        self.mem_v = dram("scr_mem_v", [MEM_H, P, 2, 2 * DH], F32)
        self.lr = dram("scr_lr", [GLA_R, T], F32)
        self.crow = dram("scr_crow", [4, FOX_H, T], F32)
        self.mix = dram("scr_mix", [2, TT, P, MIX_T, P], F32)


class Pools:

    def __init__(self, nc, ctx, tag, clears=False):
        self.nc, self.ctx, self.tag = nc, ctx, tag
        self.cleared = [] if clears else None
        if clears:
            ctx.callback(self.clear)

    def clear(self):
        self.nc.clear_and_free_semaphores(self.cleared)
        self.nc.all_engine_barrier()

    def sb(self, name, shape, dt=F32):
        return self.ctx.enter_context(self.nc.sbuf_tensor(f"{self.tag}_{name}", shape, dt))

    def ps(self, name, shape, dt=F32):
        return self.ctx.enter_context(self.nc.psum_tensor(f"{self.tag}_{name}", shape, dt))

    def sem(self, name):
        if self.cleared is None:
            return self.ctx.enter_context(self.nc.semaphore(f"{self.tag}_{name}"))
        sem = self.nc.alloc_semaphore(f"{self.tag}_{name}")
        self.cleared.append(sem)
        return sem


def constants(nc, k):
    ident = k.sb("ident", [P, P])
    ident_b = k.sb("ident_b", [P, P], BF16)
    fox_mask = k.sb("fox_mask", [P, P], BF16)
    gla_mask = k.sb("gla_mask", [P, 4, P])
    made = k.sem("made")
    with nc.Block() as block:
        @block.gpsimd
        def _(pool):
            pool.memset(ident[:, :], 0.0).then_inc(made, 1)
            pool.memset(ident_b[:, :], 0.0).then_inc(made, 1)
            pool.memset(fox_mask[:, :], 0.0).then_inc(made, 1)
            pool.memset(gla_mask[:, :, :], 1.0).then_inc(made, 1)
            pool.wait_ge(made, 4)
            for m in (ident, ident_b):
                pool.affine_select(out=m[:, :], in_=m[:, :], compare_op=ALU.not_equal, fill=1.0,
                                   base=0, pattern=[[-1, P]], channel_multiplier=1).then_inc(made, 1)
            pool.affine_select(out=fox_mask[:, :], in_=fox_mask[:, :], compare_op=ALU.is_ge, fill=-1e38,
                               base=0, pattern=[[-1, P]], channel_multiplier=1).then_inc(made, 1)
            pool.affine_select(out=gla_mask[:, :, :], in_=gla_mask[:, :, :], compare_op=ALU.is_ge, fill=0.0,
                               base=0, pattern=[[0, 4], [1, P]], channel_multiplier=-1).then_inc(made, 1)
            pool.wait_ge(made, 8)
            pool.memset(gla_mask[0:GLA_C, :, GLA_C:P], 0.0).then_inc(made, 1)
            pool.wait_ge(made, 9)
    return ident, ident_b, fox_mask, gla_mask


def memory_keys_values(nc, scr, ident, mem, mem_norm_g, w_mem_kv):
    MT = M // P
    KV = 2 * MEM_H * DH
    ctx = ExitStack()
    with ctx:
        k = Pools(nc, ctx, "mem")
        x = k.sb("x", [P, MT, D])
        g = k.sb("g", [P, D])
        xn = k.sb("xn", [P, MT, D])
        sq = k.sb("sq", [P, D])
        ss = k.sb("ss", [P, MT])
        ms = k.sb("ms", [P, MT])
        root = k.sb("root", [P, MT])
        rstd = k.sb("rstd", [P, MT])
        xT = [k.sb(f"xT{i}", [P, KT, M], F32R) for i in (HI, LO)]
        w = k.sb("w", [P, KT, KV])
        wp = [k.sb(f"w{i}", [P, KT, KV], F32R) for i in (HI, LO)]
        kst = [k.sb(f"k{i}", [P, MT, M], F32R) for i in (HI, LO)]
        vst = k.sb("v", [P, MT, MEM_H, 2, DH], F32R)
        tps = [k.ps(f"tps{i}", [P, 4, P]) for i in range(4)]
        kps = [k.ps(f"kps{i}", [P, CH]) for i in range(MT)]
        vps = [k.ps(f"vps{i}", [P, CH]) for i in range(MT)]
        loaded, w_loaded, squared, mean_done, root_done, rstd_done, normed = map(
            k.sem, "loaded w_loaded squared mean_done root_done rstd_done normed".split())
        transposed, hi_done, lo_done, w_hi, w_lo, k_done, v_done, ev_hi, ev_lo, stored = map(
            k.sem, "transposed hi_done lo_done w_hi w_lo k_done v_done ev_hi ev_lo stored".split())
        with nc.Block() as block:
            @block.sync
            def _(sp):
                sp.dma_start(x[:, :, :], mem[0].rearrange("(t p) d -> p t d", p=P)).then_inc(loaded, 16)
                sp.dma_start(g[:, :], mem_norm_g[0].partition_broadcast(P)).then_inc(loaded, 16)
                sp.dma_start(w[:, :, :], w_mem_kv[0].rearrange("(k p) n -> p k n", p=P)).then_inc(w_loaded, 16)
                for i in range(MT):
                    sp.wait_ge(ev_lo, i + 1)
                    for part in (HI, LO):
                        sp.dma_start(scr.mem_k[i, part], kst[part][:, i, :].bitcast(F32)).then_inc(stored, 16)
                for t in range(MT):
                    sp.wait_ge(ev_lo, MT + t + 1)
                    sp.dma_start(scr.mem_v[:, :, t, :].rearrange("h p c -> p h c"),
                                 vst[:, t, :, :, :].rearrange("p h a c -> p h (a c)").bitcast(F32)).then_inc(stored, 16)
                sp.wait_ge(stored, 16 * 3 * MT)

            @block.scalar
            def _(act):
                act.wait_ge(loaded, 32)
                for t in range(MT):
                    if t:
                        act.wait_ge(squared, t)
                    nc.scalar.activation(sq[:, :], x[:, t, :], ACT.Square,
                                         accum_out=ss[:, t:t + 1]).then_inc(squared, 1)
                act.wait_ge(mean_done, 1)
                nc.scalar.activation(root[:, :], ms[:, :], ACT.Sqrt).then_inc(root_done, 1)
                for t in range(MT):
                    for c in range(2):
                        act.wait_ge(transposed, 2 * t + c + 1)
                        nc.scalar.activation(xT[HI][:, 4 * c:4 * c + 4, t * P:(t + 1) * P],
                                             tps[2 * t + c][:, :, :], ACT.Copy).then_inc(hi_done, 1)
                for i in range(MT):
                    act.wait_ge(k_done, i + 1)
                    nc.scalar.activation(kst[HI][:, i, :], kps[i][:, 0:M], ACT.Copy).then_inc(ev_hi, 1)
                for t in range(MT):
                    act.wait_ge(v_done, t + 1)
                    nc.scalar.activation(vst[:, t, :, HI, :],
                                         vps[t][:, 0:M].rearrange("p (h c) -> p h c", c=DH),
                                         ACT.Copy).then_inc(ev_hi, 1)

            @block.vector
            def _(dve):
                dve.wait_ge(squared, MT)
                nc.vector.tensor_scalar(ms[:, :], ss[:, :], 1.0 / D, EPS, ALU.mult, ALU.add).then_inc(mean_done, 1)
                dve.wait_ge(root_done, 1)
                nc.vector.reciprocal(rstd[:, :], root[:, :]).then_inc(rstd_done, 1)
                dve.wait_ge(rstd_done, 1)
                dve.wait_ge(loaded, 32)
                for t in range(MT):
                    nc.vector.scalar_tensor_tensor(xn[:, t, :], x[:, t, :], rstd[:, t:t + 1], g[:, :],
                                                   ALU.mult, ALU.mult).then_inc(normed, 1)
                for t in range(MT):
                    for c in range(2):
                        dve.wait_ge(hi_done, 2 * t + c + 1)
                        nc.vector.tensor_tensor(xT[LO][:, 4 * c:4 * c + 4, t * P:(t + 1) * P],
                                                tps[2 * t + c][:, :, :],
                                                xT[HI][:, 4 * c:4 * c + 4, t * P:(t + 1) * P].bitcast(F32),
                                                ALU.subtract).then_inc(lo_done, 1)
                for i in range(MT):
                    dve.wait_ge(ev_hi, i + 1)
                    nc.vector.tensor_tensor(kst[LO][:, i, :], kps[i][:, 0:M], kst[HI][:, i, :].bitcast(F32),
                                            ALU.subtract).then_inc(ev_lo, 1)
                for t in range(MT):
                    dve.wait_ge(ev_hi, MT + t + 1)
                    nc.vector.tensor_tensor(vst[:, t, :, LO, :],
                                            vps[t][:, 0:M].rearrange("p (h c) -> p h c", c=DH),
                                            vst[:, t, :, HI, :].bitcast(F32), ALU.subtract).then_inc(ev_lo, 1)

            @block.gpsimd
            def _(pool):
                pool.wait_ge(w_loaded, 16)
                for q in range(4):
                    s = slice(2 * q, 2 * q + 2)
                    nc.gpsimd.tensor_copy(wp[HI][:, s, :], w[:, s, :]).then_inc(w_hi, 1)
                    pool.wait_ge(w_hi, q + 1)
                    nc.gpsimd.tensor_tensor(wp[LO][:, s, :], w[:, s, :], wp[HI][:, s, :].bitcast(F32),
                                            ALU.subtract).then_inc(w_lo, 1)

            @block.tensor
            def _(pe):
                for t in range(MT):
                    pe.wait_ge(normed, t + 1)
                    for c in range(2):
                        for j in range(4):
                            kk = 4 * c + j
                            mm = nc.tensor.transpose(tps[2 * t + c][:, j, :], xn[:, t, kk * P:(kk + 1) * P],
                                                     ident[:, :])
                        mm.then_inc(transposed, 1)
                pe.wait_ge(lo_done, 2 * MT)
                pe.wait_ge(w_lo, 4)
                for i in range(MT):
                    for kk in range(KT):
                        for n, (a, b) in enumerate(PASSES):
                            mm = nc.tensor.matmul(kps[i][:, 0:M], wp[a][:, kk, i * P:(i + 1) * P], xT[b][:, kk, :],
                                                  start=(kk == 0 and n == 0), stop=(kk == KT - 1 and n == 2))
                    mm.then_inc(k_done, 1)
                for t in range(MT):
                    for kk in range(KT):
                        for n, (a, b) in enumerate(PASSES):
                            mm = nc.tensor.matmul(vps[t][:, 0:M], xT[a][:, kk, t * P:(t + 1) * P],
                                                  wp[b][:, kk, M:2 * M],
                                                  start=(kk == 0 and n == 0), stop=(kk == KT - 1 and n == 2))
                    mm.then_inc(v_done, 1)


def project_tokens(nc, scr, ident, hT, fglr, x, norm_g, w_tok):
    V = FOX_H * DH
    x_t = x[0].rearrange("(t p) d -> t p d", p=P)
    ctx = ExitStack()
    with ctx:
        k = Pools(nc, ctx, "tok", clears=True)
        g = k.sb("g", [P, D])
        xin = [k.sb(f"xin{s}", [P, D]) for s in range(2)]
        xn = k.sb("xn", [P, D])
        st = k.sb("st", [P, 4])
        w_raw = [k.sb(f"wraw{s}", [P, TOK_C]) for s in range(2)]
        w = [k.sb(f"w{i}", [P, KT, TOK_C], F32R) for i in (HI, LO)]
        slot = [[k.sb(f"slot{s}{i}", [P, KT, P], F32R) for i in (HI, LO)] for s in range(2)]
        vst = [k.sb(f"vst{s}", [P, FOX_H, 2, DH], F32R) for s in range(2)]
        tps = [k.ps(f"tps{c}", [P, 4, P]) for c in range(2)]
        mps = [k.ps(f"mps{s}", [P, CH]) for s in range(2)]
        junk = k.ps("junk", [P, 2 * CH])
        (g_loaded, x_loaded0, x_loaded1, w_loaded0, w_loaded1, w_hi, w_lo, squared, mean_done, root_done, rstd_done,
         normed, transposed, hi_done, lo_done, kept, multiplied, v_hi, v_lo, v_stored0, v_stored1, pool_goes) = map(
            k.sem, ("g_loaded x_loaded0 x_loaded1 w_loaded0 w_loaded1 w_hi w_lo squared mean_done root_done rstd_done "
                    "normed transposed hi_done lo_done kept multiplied v_hi v_lo v_stored0 v_stored1 pool_goes").split())
        x_loaded, w_loaded, v_stored = (x_loaded0, x_loaded1), (w_loaded0, w_loaded1), (v_stored0, v_stored1)

        def steps(eng, step):
            for t in (0, 1):
                step(0, t, True, True)
            with eng.Fori(1, TT // 2 - 1) as h:
                for s in range(2):
                    step(h, s, True, True)
            step(TT // 2 - 1, 0, True, False)
            step(TT // 2 - 1, 1, False, False)

        with nc.Block() as block:
            @block.sync
            def _(sp):
                for t in range(2):
                    sp.dma_start(xin[t][:, :], x_t[t]).then_inc(x_loaded[t], 16)
                sp.dma_start(g[:, :], norm_g[0].partition_broadcast(P)).then_inc(g_loaded, 16)
                for kk in range(KT):
                    if kk >= 2:
                        sp.wait_ge(w_lo, kk - 1)
                    sp.dma_start(w_raw[kk % 2][:, :], w_tok[:, kk, :]).then_inc(w_loaded[kk % 2], 16)

                def step(h, s, _, more):
                    t = 2 * h + s
                    if more:
                        sp.wait_ge(normed, t + 1)
                        sp.dma_start(xin[s][:, :], x_t[bass.ds(t + 2, 1)].rearrange("a p d -> (a p) d")
                                     ).then_inc(x_loaded[s], 16)
                    sp.wait_ge(v_lo, t + 1)
                    sp.dma_start(scr.fox_v[:, :, bass.ds(t, 1), :].rearrange("h p a c -> p h (a c)"),
                                 vst[s][:, :, :, :].rearrange("p h a c -> p h (a c)").bitcast(F32)).then_inc(v_stored[s], 16)
                steps(sp, step)
                for s in range(2):
                    sp.wait_ge(v_stored[s], 16 * TT // 2)

            def normalise_act(act, h, s):
                t = 2 * h + s
                act.wait_ge(x_loaded[s], 16 * (h + 1))
                nc.scalar.activation(junk[:, :], xin[s][:, :], ACT.Square, accum_out=st[:, 0:1]).then_inc(squared, 1)
                act.wait_ge(mean_done, t + 1)
                nc.scalar.activation(st[:, 2:3], st[:, 1:2], ACT.Sqrt).then_inc(root_done, 1)

            def high_part(act, h, s):
                t = 2 * h + s
                for c in range(2):
                    act.wait_ge(transposed, 2 * t + c + 1)
                    nc.scalar.activation(slot[s][HI][:, 4 * c:4 * c + 4, :], tps[c][:, :, :],
                                         ACT.Copy).then_inc(hi_done, 1)

            @block.scalar
            def _(act):
                normalise_act(act, 0, 0)
                high_part(act, 0, 0)
                normalise_act(act, 0, 1)

                def step(h, s, one_more, two_more):
                    t = 2 * h + s
                    if one_more:
                        act.wait_ge(multiplied, t)
                        act.wait_ge(kept, t)
                        high_part(act, h + s, 1 - s)
                    if two_more:
                        normalise_act(act, h + 1, s)
                    act.wait_ge(multiplied, t + 1)
                    act.wait_ge(v_stored[s], 16 * h)
                    nc.scalar.activation(vst[s][:, :, HI, :], mps[s][:, 0:V].rearrange("p (h c) -> p h c", c=DH),
                                         ACT.Copy).then_inc(v_hi, 1)
                steps(act, step)

            def normalise_dve(dve, h, s):
                t = 2 * h + s
                dve.wait_ge(squared, t + 1)
                nc.vector.tensor_scalar(st[:, 1:2], st[:, 0:1], 1.0 / D, EPS, ALU.mult, ALU.add
                                        ).then_inc(mean_done, 1)
                dve.wait_ge(root_done, t + 1)
                nc.vector.reciprocal(st[:, 3:4], st[:, 2:3]).then_inc(rstd_done, 1)
                dve.wait_ge(rstd_done, t + 1)
                dve.wait_ge(transposed, 2 * t)
                nc.vector.scalar_tensor_tensor(xn[:, :], xin[s][:, :], st[:, 3:4], g[:, :],
                                               ALU.mult, ALU.mult).then_inc(normed, 1)

            def low_part(dve, h, s):
                t = 2 * h + s
                for c in range(2):
                    dve.wait_ge(hi_done, 2 * t + c + 1)
                    nc.vector.tensor_tensor(slot[s][LO][:, 4 * c:4 * c + 4, :], tps[c][:, :, :],
                                            slot[s][HI][:, 4 * c:4 * c + 4, :].bitcast(F32),
                                            ALU.subtract).then_inc(lo_done, 1)

            @block.vector
            def _(dve):
                dve.wait_ge(g_loaded, 16)
                normalise_dve(dve, 0, 0)
                low_part(dve, 0, 0)
                normalise_dve(dve, 0, 1)

                def step(h, s, one_more, two_more):
                    t = 2 * h + s
                    if one_more:
                        low_part(dve, h + s, 1 - s)
                    if two_more:
                        normalise_dve(dve, h + 1, s)
                    dve.wait_ge(v_hi, t + 1)
                    nc.vector.tensor_copy(fglr[:, bass.ds(t, 1), :].rearrange("p a c -> p (a c)"),
                                          mps[s][:, V:TOK_C])
                    nc.vector.tensor_tensor(vst[s][:, :, LO, :], mps[s][:, 0:V].rearrange("p (h c) -> p h c", c=DH),
                                            vst[s][:, :, HI, :].bitcast(F32), ALU.subtract).then_inc(v_lo, 1)
                steps(dve, step)

            @block.gpsimd
            def _(pool):
                for kk in range(KT):
                    pool.wait_ge(w_loaded[kk % 2], 16 * (kk // 2 + 1))
                    nc.gpsimd.tensor_copy(w[HI][:, kk, :], w_raw[kk % 2][:, :]).then_inc(w_hi, 1)
                    pool.wait_ge(w_hi, kk + 1)
                    nc.gpsimd.tensor_tensor(w[LO][:, kk, :], w_raw[kk % 2][:, :], w[HI][:, kk, :].bitcast(F32),
                                            ALU.subtract).then_inc(w_lo, 1)
                with pool.Fori(0, TT // 2) as h:
                    for s in range(2):
                        t = 2 * h + s
                        pool.wait_ge(lo_done, 2 * t + 2)
                        pool.sem_inc(pool_goes, 1)
                        nc.gpsimd.tensor_copy(hT[HI][:, :, bass.ds(t * P, P)], slot[s][HI][:, :, :].bitcast(F32))
                        nc.gpsimd.tensor_copy(hT[LO][:, :, bass.ds(t * P, P)], slot[s][LO][:, :, :].bitcast(F32)
                                              ).then_inc(kept, 1)
                pool.wait_ge(kept, TT)

            @block.tensor
            def _(pe):
                def transposes(h, s, first=False):
                    t = 2 * h + s
                    pe.wait_ge(normed, t + 1)
                    for c in range(2):
                        if not first:
                            pe.wait_ge(lo_done, 2 * t - 1 + c)
                        for j in range(4):
                            kk = 4 * c + j
                            mm = nc.tensor.transpose(tps[c][:, j, :], xn[:, kk * P:(kk + 1) * P], ident[:, :])
                        mm.then_inc(transposed, 1)
                transposes(0, 0, True)

                def step(h, s, one_more, _):
                    t = 2 * h + s
                    if one_more:
                        transposes(h + s, 1 - s)
                    pe.wait_ge(lo_done, 2 * t + 2)
                    if isinstance(h, int) and h == 0:
                        pe.wait_ge(w_lo, KT)
                    else:
                        pe.wait_ge(v_lo, t - 1)
                    for kk in range(KT):
                        for n, (a, b) in enumerate(PASSES):
                            mm = nc.tensor.matmul(mps[s][:, 0:TOK_C], slot[s][a][:, kk, :], w[b][:, kk, :],
                                                  start=(kk == 0 and n == 0), stop=(kk == KT - 1 and n == 2))
                    mm.then_inc(multiplied, 1)
                steps(pe, step)


def project_columns(nc, scr, ident, hT, fglr, w_cols, b_forget):
    R = 8
    ctx = ExitStack()
    with ctx:
        k = Pools(nc, ctx, "col")
        w_raw = [k.sb(f"wraw{s}", [P, KT, P]) for s in range(2)]
        w = [[k.sb(f"w{s}{i}", [P, KT, P], F32R) for i in (HI, LO)] for s in range(2)]
        stage = [[k.sb(f"stage{s}{i}", [P, CH], F32R) for i in (HI, LO)] for s in range(2)]
        plain = [k.sb(f"plain{s}", [P, CH]) for s in range(2)]
        rT = k.sb("rT", [FGLR, T])
        f = rT[0:FOX_H, :]
        a = k.sb("a", [FOX_H, T])
        parts = [k.sb(f"part{i}", [FOX_H, T], F32R) for i in range(2)]
        bf = k.sb("bf", [FOX_H, 1])
        cps = [k.ps(f"cps{c}", [P, CH]) for c in range(NCH)]
        rps = k.ps("rps", [P, T])
        (w_loaded0, w_loaded1, w_hi, w_lo, projected, hi_done, bank_free, gate_done, raw_done,
         stored0, stored1, rows_loaded, rows_t, rows_copied, act_rows, dve_rows, pool_rows, rows_stored, pool_goes) = map(
            k.sem, ("w_loaded0 w_loaded1 w_hi w_lo projected hi_done bank_free gate_done raw_done "
                    "stored0 stored1 rows_loaded rows_t rows_copied act_rows dve_rows pool_rows rows_stored pool_goes").split())
        w_loaded, stored = (w_loaded0, w_loaded1), (stored0, stored1)
        split_st = 16 * 2 * 2
        plain_st = 16 * 2
        base_plain = NSPLIT * split_st

        with nc.Block() as block:
            @block.sync
            def _(sp):
                sp.dma_start(w_raw[0][:, :, :], w_cols[0]).then_inc(w_loaded[0], 16)

                def load_next(j, s):
                    sp.wait_ge(w_lo, j)
                    sp.dma_start(w_raw[1 - s][:, :, :],
                                 w_cols[bass.ds(j + 1, 1)].rearrange("a p k c -> (a p) k c")
                                 ).then_inc(w_loaded[1 - s], 16)

                def store_split(j):
                    for c in range(NCH):
                        sp.wait_ge(bank_free, 4 * j + c + 5)
                        for i in (HI, LO):
                            dst = scr.split[bass.ds(j, 1), i, :, c * CH:(c + 1) * CH]
                            sp.dma_start(dst.rearrange("a p t -> (a p) t"), stage[c % 2][i][:, :].bitcast(F32)
                                         ).then_inc(stored[c % 2], 16)

                def store_plain(j, dst, first):
                    for c in range(NCH):
                        sp.wait_ge(bank_free, 4 * j + c + 5)
                        d = dst[bass.ds(j - first, 1), :, c * CH:(c + 1) * CH].rearrange("a p t -> (a p) t")
                        sp.dma_start(d, plain[c % 2][:, :]).then_inc(stored[c % 2], 16)

                with sp.Fori(0, NSPLIT // 2) as h:
                    for s in range(2):
                        load_next(2 * h + s, s)
                        store_split(2 * h + s)
                with sp.Fori(NSPLIT // 2, (NSPLIT + NGATE) // 2) as h:
                    for s in range(2):
                        load_next(2 * h + s, s)
                        store_plain(2 * h + s, scr.gates, NSPLIT)
                raw = scr.raw.rearrange("(a p) t -> a p t", p=P)
                with sp.Fori((NSPLIT + NGATE) // 2, NCOL // 2 - 1) as h:
                    for s in range(2):
                        load_next(2 * h + s, s)
                        store_plain(2 * h + s, raw, NSPLIT + NGATE)
                load_next(NCOL - 2, 0)
                store_plain(NCOL - 2, raw, NSPLIT + NGATE)
                store_plain(NCOL - 1, raw, NSPLIT + NGATE)
                for s in range(2):
                    sp.wait_ge(stored[s], base_plain + (NGATE + NRAW) * plain_st)

            @block.gpsimd
            def _(pool):
                pool.dma_start(bf[:, :], b_forget.rearrange("a h -> h a")).then_inc(rows_loaded, 16)

                def split(h, s):
                    j = 2 * h + s
                    pool.wait_ge(w_loaded[s], 16 * (h + 1))
                    pool.sem_inc(pool_goes, 1)
                    nc.gpsimd.tensor_copy(w[s][HI][:, :, :], w_raw[s][:, :, :]).then_inc(w_hi, 1)
                    pool.wait_ge(w_hi, j + 1)
                    nc.gpsimd.tensor_tensor(w[s][LO][:, :, :], w_raw[s][:, :, :], w[s][HI][:, :, :].bitcast(F32),
                                            ALU.subtract).then_inc(w_lo, 1)
                for s in range(2):
                    split(0, s)
                pool.wait_ge(rows_copied, 1)
                pool.dma_start(scr.lr, rT[FOX_H:FGLR, :]).then_inc(rows_stored, 16)
                pool.wait_ge(dve_rows, 4)
                nc.gpsimd.tensor_scalar(f, f, float(R), 1.0, ALU.mult, ALU.mult).then_inc(pool_rows, 1)
                pool.wait_ge(pool_rows, 1)
                nc.gpsimd.tensor_copy(parts[HI][:, :], f).then_inc(pool_rows, 1)
                pool.wait_ge(pool_rows, 2)
                nc.gpsimd.tensor_tensor(parts[LO][:, :], f, parts[HI][:, :].bitcast(F32), ALU.subtract
                                        ).then_inc(pool_rows, 1)
                pool.wait_ge(pool_rows, 3)
                for i in (HI, LO):
                    pool.dma_start(scr.crow[i], parts[i][:, :].bitcast(F32)).then_inc(rows_stored, 16)
                pool.wait_ge(rows_stored, 48)
                for i in (HI, LO):
                    nc.gpsimd.tensor_scalar(parts[i][:, :], parts[i][:, :].bitcast(F32), -1.0, 1.0,
                                            ALU.mult, ALU.mult).then_inc(pool_rows, 1)
                pool.wait_ge(pool_rows, 5)
                for i in (HI, LO):
                    pool.dma_start(scr.crow[2 + i], parts[i][:, :].bitcast(F32)).then_inc(rows_stored, 16)
                pool.wait_ge(rows_stored, 80)
                with pool.Fori(1, NCOL // 2) as h:
                    for s in range(2):
                        pool.wait_ge(projected, 4 * (2 * h + s - 1))
                        split(h, s)

            @block.tensor
            def _(pe):
                for t in range(TT):
                    mm = nc.tensor.transpose(rps[0:FGLR, t * P:(t + 1) * P], fglr[:, t, :], ident[:, :])
                mm.then_inc(rows_t, 1)
                with pe.Fori(0, NCOL // 2) as h:
                    for s in range(2):
                        j = 2 * h + s
                        pe.wait_ge(w_lo, j + 1)
                        for c in range(NCH):
                            pe.wait_ge(bank_free, 4 * j + c + 1)
                            for kk in range(KT):
                                for n, (a_, b_) in enumerate(PASSES):
                                    mm = nc.tensor.matmul(cps[c][:, :], w[s][a_][:, kk, :],
                                                          hT[b_][:, kk, c * CH:(c + 1) * CH],
                                                          start=(kk == 0 and n == 0), stop=(kk == KT - 1 and n == 2))
                            mm.then_inc(projected, 1)

            @block.scalar
            def _(act):
                act.wait_ge(rows_t, 1)
                nc.scalar.activation(rT[:, :], rps[0:FGLR, :], ACT.Copy).then_inc(rows_copied, 1)
                act.wait_ge(dve_rows, 1)
                nc.scalar.activation(a[:, :], f, ACT.Abs).then_inc(act_rows, 1)
                act.wait_ge(act_rows, 1)
                nc.scalar.activation(a[:, :], a[:, :], ACT.Exp, scale=-1.0).then_inc(act_rows, 1)
                act.wait_ge(act_rows, 2)
                nc.scalar.activation(a[:, :], a[:, :], ACT.Ln, bias=1.0).then_inc(act_rows, 1)

                with act.Fori(0, NSPLIT // 2) as h:
                    for s in range(2):
                        for c in range(NCH):
                            j = 2 * h + s
                            act.wait_ge(projected, 4 * j + c + 1)
                            act.wait_ge(stored[c % 2], j * split_st + (c // 2) * 32)
                            nc.scalar.activation(stage[c % 2][HI][:, :], cps[c][:, :], ACT.Copy).then_inc(hi_done, 1)
                act.wait_ge(bank_free, 4 * NSPLIT + 4)
                with act.Fori(NSPLIT // 2, (NSPLIT + NGATE) // 2) as h:
                    for s in range(2):
                        for c in range(NCH):
                            j = 2 * h + s
                            act.wait_ge(projected, 4 * j + c + 1)
                            act.wait_ge(stored[c % 2], base_plain + (j - NSPLIT) * plain_st + (c // 2) * 16)
                            nc.scalar.activation(plain[c % 2][:, :], cps[c][:, :], ACT.Silu).then_inc(bank_free, 1)

            @block.vector
            def _(dve):
                dve.sem_inc(bank_free, 4)
                dve.wait_ge(rows_copied, 1)
                dve.wait_ge(rows_loaded, 16)
                nc.vector.tensor_scalar(f, rT[0:FOX_H, :], bf[:, 0:1], None, ALU.add).then_inc(dve_rows, 1)
                dve.wait_ge(dve_rows, 1)
                dve.wait_ge(act_rows, 3)
                nc.vector.scalar_tensor_tensor(f, f, 0.0, a[:, :], ALU.min, ALU.subtract
                                               ).then_inc(dve_rows, 1)
                dve.wait_ge(dve_rows, 2)
                nc.vector.memset(a[:, :], -3e38).then_inc(dve_rows, 1)
                dve.wait_ge(dve_rows, 3)
                nc.vector.tensor_tensor_scan(f, f, a[:, :], 0.0, ALU.add, ALU.max).then_inc(dve_rows, 1)
                with dve.Fori(0, NSPLIT // 2) as h:
                    for s in range(2):
                        for c in range(NCH):
                            j = 2 * h + s
                            dve.wait_ge(hi_done, 4 * j + c + 1)
                            nc.vector.tensor_tensor(stage[c % 2][LO][:, :], cps[c][:, :],
                                                    stage[c % 2][HI][:, :].bitcast(F32), ALU.subtract
                                                    ).then_inc(bank_free, 1)
                dve.wait_ge(bank_free, 4 * (NSPLIT + NGATE) + 4)
                with dve.Fori((NSPLIT + NGATE) // 2, NCOL // 2) as h:
                    for s in range(2):
                        for c in range(NCH):
                            j = 2 * h + s
                            dve.wait_ge(projected, 4 * j + c + 1)
                            dve.wait_ge(stored[c % 2], base_plain + (j - NSPLIT) * plain_st + (c // 2) * 16)
                            nc.vector.tensor_copy(plain[c % 2][:, :], cps[c][:, :]).then_inc(bank_free, 1)




def gated_linear_attention(nc, scr, ident, gla_mask, w_alpha_up, b_alpha, gla_norm_g):
    NG, GT = T // CH, CH
    NS = T // P
    ST = CH // P
    HB = 64
    KR = HB + GLA_DK
    W2 = 2 * GLA_DV
    GV = GLA_H * GLA_DV
    RING = 6
    PAIRS = 2
    QKW = GLA_H * GLA_DK
    ctx = ExitStack()
    with ctx:
        k = Pools(nc, ctx, "gla")
        pair_tiles = lambda name, shape, dt=F32: [[k.sb(f"{name}{s}{p}", shape, dt) for p in range(PAIRS)]
                                                  for s in range(2)]
        q, kk = pair_tiles("q", [KR, GT]), pair_tiles("k", [KR, GT])
        qd, kd, kte = (pair_tiles(n, [KR, GT]) for n in ("qd", "kd", "kte"))
        qpad = pair_tiles("qpad", [KR, 2, GT])
        dec = pair_tiles("dec", [KR, GT // GLA_C])
        v = [k.sb(f"v{s}", [GLA_DV, GLA_H, GT]) for s in range(2)]
        lr = [k.sb(f"lr{s}", [GLA_R, GT]) for s in range(2)]
        gate = [k.sb(f"gate{s}", [P, 3, GT]) for s in range(2)]
        keep = k.sb("keep", [KR, GT])
        zabs, la, b, tail, ep, em, ee = (k.sb(n, [KR, GT]) for n in "zabs la b tail ep em ee".split())
        wup = [k.sb(f"wup{p}", [GLA_R, KR]) for p in range(PAIRS)]
        bup = [k.sb(f"bup{p}", [KR, 1]) for p in range(PAIRS)]
        gn = k.sb("gn", [P, 3])
        vt = [k.sb(f"vt{s}", [P, GV]) for s in range(2)]
        vz = k.sb("vz", [P, 2, GV])
        kt = k.sb("kt", [P, PAIRS * KR])
        am = [k.sb(f"am{s}", [P, GLA_H * P]) for s in range(2)]
        S = [[k.sb(f"S{r}{p}", [KR, W2]) for p in range(PAIRS)] for r in range(RING)]
        sqj = k.sb("sqj", [P, GLA_DV])
        ss, ms, rstd, half = (k.sb(n, [P, GLA_H]) for n in ("ss", "ms", "rstd", "half"))
        on = [k.sb(f"on{s}", [P, GV]) for s in range(2)]
        mx = k.sb("mx", [P, 3, P])
        mst = [[k.sb(f"mst{s}{i}", [P, 3, P], F32R) for i in (HI, LO)] for s in range(2)]
        zps = k.ps("zps", [P, CH])
        vps = k.ps("vps", [P, CH])
        kps = k.ps("kps", [P, CH])
        aps = k.ps("aps", [P, CH])
        kvps = [k.ps(f"kvps{p}", [P, CH]) for p in range(PAIRS)]
        ops = k.ps("ops", [P, CH])
        otps = k.ps("otps", [P, CH])
        (k_decayed, qpad_done, pads, w_loaded, cleared, qk_loaded0, qk_loaded1, v_loaded0, v_loaded1, gate_loaded0, gate_loaded1, z_done, abs_done,
         min_done, exp_done, ln_done, la_done, scan_done, ep_done, em_done, tail_done, ee_done, qd_done, prep_done,
         gate_ready) = map(
            k.sem, ("k_decayed qpad_done pads w_loaded cleared qk_loaded0 qk_loaded1 v_loaded0 v_loaded1 gate_loaded0 gate_loaded1 z_done "
                    "abs_done min_done exp_done ln_done la_done scan_done ep_done em_done tail_done ee_done qd_done "
                    "prep_done gate_ready").split())
        (vT_done, kT_done, attn_done, kv_done, o_done, oT_done, v_copied, k_copied, masked, state_done, squared,
         ms_done, rstd_done, on_done, mixed, mix_hi, mix_lo, stored0, stored1) = map(
            k.sem, ("vT_done kT_done attn_done kv_done o_done oT_done v_copied k_copied masked state_done squared "
                    "ms_done rstd_done on_done mixed mix_hi mix_lo stored0 stored1").split())
        qk_loaded, v_loaded, gate_loaded = (qk_loaded0, qk_loaded1), (v_loaded0, v_loaded1), (gate_loaded0, gate_loaded1)
        stored = (stored0, stored1)
        QK_DMAS = 16 * (4 * PAIRS + 1)

        def pieces(g, n):
            if g + 1 < NG:
                yield g + 1, n // 2, n % 2

        def first_pieces():
            for p in range(PAIRS):
                for part in range(2):
                    yield 0, p, part

        with nc.Block() as block:
            @block.sync
            def _(sp):
                sp.wait_ge(pads, 2 * PAIRS)
                for p in range(PAIRS):
                    for e in range(2):
                        c = (2 * p + e) * GLA_DK
                        sp.dma_start(wup[p][:, HB * e:HB * e + GLA_DK], w_alpha_up[0, :, c:c + GLA_DK]
                                     ).then_inc(w_loaded, 16)
                ch = 0
                while ch < GV:
                    n = min(P - ch % P, GLA_DV - ch % GLA_DV)
                    sp.dma_start(gn[ch % P:ch % P + n, ch // P:ch // P + 1],
                                 gla_norm_g[0:1, ch % GLA_DV:ch % GLA_DV + n].rearrange("a n -> n a")
                                 ).then_inc(w_loaded, 16)
                    ch += n

                def load_qk(g):
                    s, cols = g % 2, slice(g * GT, (g + 1) * GT)
                    if g == 0:
                        sp.wait_ge(cleared, 8)
                    if g >= 2:
                        sp.wait_ge(prep_done, PAIRS * (g - 1))
                    for p in range(PAIRS):
                        for e in range(2):
                            r = (2 * p + e) * GLA_DK
                            rows = slice(HB * e, HB * e + GLA_DK)
                            sp.dma_start(q[s][p][rows, :], scr.raw[r:r + GLA_DK, cols]).then_inc(qk_loaded[s], 16)
                            sp.dma_start(kk[s][p][rows, :], scr.raw[QKW + r:QKW + r + GLA_DK, cols]
                                         ).then_inc(qk_loaded[s], 16)
                    sp.dma_start(lr[s][:, :], scr.lr[:, cols]).then_inc(qk_loaded[s], 16)

                def load_v(g):
                    s, cols = g % 2, slice(g * GT, (g + 1) * GT)
                    if g >= 2:
                        sp.wait_ge(vT_done, ST * (g - 1))
                    sp.dma_start(v[s][:, :, :], scr.raw[2 * QKW:2 * QKW + GV, cols].rearrange("(h d) t -> d h t", d=GLA_DV)
                                 ).then_inc(v_loaded[s], 16)

                def load_gate(g):
                    s, cols = g % 2, slice(g * GT, (g + 1) * GT)
                    if g >= 2:
                        sp.wait_ge(mixed, ST * (g - 1))
                    sp.dma_start(gate[s][:, :, :], scr.gates[0:3, :, cols].rearrange("j p t -> p j t")
                                 ).then_inc(gate_loaded[s], 16)

                def store(N):
                    sp.wait_ge(mix_lo, N + 1)
                    for i in (HI, LO):
                        sp.dma_start(scr.mix[i, N, :, 0:3, :], mst[N % 2][i][:, :, :].bitcast(F32)
                                     ).then_inc(stored[N % 2], 16)
                for g in range(2):
                    load_qk(g)
                    load_v(g)
                    load_gate(g)
                for g in range(NG):
                    for n in range(ST):
                        if g * ST + n >= 2:
                            store(g * ST + n - 2)
                        if n == 0 and g + 2 < NG:
                            load_qk(g + 2)
                        if n == 0 and 2 <= g + 1 < NG:
                            load_v(g + 1)
                        if n == 2 and 2 <= g + 1 < NG:
                            load_gate(g + 1)
                store(NS - 2)
                store(NS - 1)
                for s in range(2):
                    sp.wait_ge(stored[s], 16 * NS)

            @block.tensor
            def _(pe):
                def prep(g, p, part):
                    u = PAIRS * g + p
                    if part:
                        return
                    if p == 0:
                        pe.wait_ge(qk_loaded[g % 2], QK_DMAS * (g // 2 + 1))
                    if u:
                        pe.wait_ge(min_done, u)
                        pe.wait_ge(abs_done, u)
                    nc.tensor.matmul(zps[0:KR, :], wup[p][:, :], lr[g % 2][:, :], start=True, stop=True
                                     ).then_inc(z_done, 1)
                pe.wait_ge(cleared, 10)
                pe.wait_ge(w_loaded, 16 * 14)
                for x in first_pieces():
                    prep(*x)

                def outputs(N):
                    s, c0 = (N // ST) % 2, (N % ST) * P
                    if N:
                        pe.wait_ge(on_done, N)
                    pe.wait_ge(masked, N + 1)
                    for p in range(PAIRS):
                        o = ops[:, p * W2:(p + 1) * W2]
                        for e in range(2):
                            m = 2 * N + e
                            if m:
                                pe.wait_ge(state_done, 2 * PAIRS * (m - 1) + 2 * p + 2)
                            nc.tensor.matmul(o[GLA_C * e:GLA_C * (e + 1), :],
                                             qd[s][p][:, c0 + GLA_C * e:c0 + GLA_C * (e + 1)], S[m % RING][p][:, :],
                                             start=True, stop=False, skip_group_check=True)
                        for e in range(2):
                            h = 2 * p + e
                            mm = nc.tensor.matmul(o[:, e * GLA_DV:(e + 1) * GLA_DV], am[N % 2][:, h * P:(h + 1) * P],
                                                  vt[N % 2][:, h * GLA_DV:(h + 1) * GLA_DV],
                                                  start=False, stop=True, skip_group_check=True)
                    mm.then_inc(o_done, 1)

                def transposed_outputs(N):
                    pe.wait_ge(on_done, N + 1)
                    if N:
                        pe.wait_ge(mixed, N)
                    for j in range(3):
                        mm = nc.tensor.transpose(otps[:, j * P:(j + 1) * P], on[N % 2][:, j * P:(j + 1) * P], ident[:, :])
                    mm.then_inc(oT_done, 1)

                for g in range(NG):
                    s = g % 2
                    for n in range(ST):
                        N, cols = g * ST + n, slice(n * P, (n + 1) * P)
                        if n == 0:
                            pe.wait_ge(v_loaded[s], 16 * (g // 2 + 1))
                            pe.wait_ge(prep_done, PAIRS * (g + 1))
                        if N:
                            pe.wait_ge(v_copied, 3 * N)
                        for h in range(GLA_H):
                            mm = nc.tensor.transpose(vps[:, h * GLA_DV:(h + 1) * GLA_DV], v[s][:, h, cols],
                                                     ident[0:GLA_DV, 0:GLA_DV])
                        mm.then_inc(vT_done, 1)
                        if N:
                            pe.wait_ge(k_copied, N)
                        for p in range(PAIRS):
                            mm = nc.tensor.transpose(kps[:, p * KR:(p + 1) * KR], kte[s][p][:, cols], ident[0:KR, 0:KR])
                        mm.then_inc(kT_done, 1)
                        if N:
                            pe.wait_ge(masked, N)
                        for p in range(PAIRS):
                            mm = nc.tensor.matmul(aps[:, p * 2 * P:(p + 1) * 2 * P], kd[s][p][:, cols],
                                                  qpad[s][p][:, :, cols], start=True, stop=True)
                        mm.then_inc(attn_done, 1)
                        if N:
                            outputs(N - 1)
                        pe.wait_ge(v_copied, 3 * (N + 1))
                        pe.wait_ge(k_copied, N + 1)
                        for p in range(PAIRS):
                            if N:
                                pe.wait_ge(state_done, 4 * PAIRS * (N - 1) + 2 * PAIRS + 2 * p + 2)
                            nc.tensor.matmul(kvps[p][0:KR, 0:2 * W2], kt[:, p * KR:(p + 1) * KR],
                                             vz[:, :, p * W2:(p + 1) * W2], start=True, stop=True
                                             ).then_inc(kv_done, 1)
                        if N >= 2:
                            transposed_outputs(N - 2)
                        for x in pieces(g, n):
                            prep(*x)
                outputs(NS - 1)
                transposed_outputs(NS - 2)
                transposed_outputs(NS - 1)

            @block.scalar
            def _(act):
                def prep(g, p, part):
                    u = PAIRS * g + p
                    if part == 0:
                        act.wait_ge(z_done, u + 1)
                        if u:
                            act.wait_ge(la_done, u)
                        nc.scalar.activation(zabs[:, :], zps[0:KR, :], ACT.Abs, bias=bup[p][:, 0:1]).then_inc(abs_done, 1)
                        act.wait_ge(abs_done, u + 1)
                        nc.scalar.activation(zabs[:, :], zabs[:, :], ACT.Exp, scale=-1.0).then_inc(exp_done, 1)
                        act.wait_ge(exp_done, u + 1)
                        nc.scalar.activation(zabs[:, :], zabs[:, :], ACT.Ln, bias=1.0).then_inc(ln_done, 1)
                    else:
                        act.wait_ge(scan_done, u + 1)
                        if u:
                            act.wait_ge(prep_done, u)
                        gs = 1.0 / GLA_GATE
                        nc.scalar.activation(ep[:, :], b[:, :], ACT.Exp, scale=gs).then_inc(ep_done, 1)
                        nc.scalar.activation(em[:, :], b[:, :], ACT.Exp, scale=-gs).then_inc(em_done, 1)
                        act.wait_ge(tail_done, u + 1)
                        nc.scalar.activation(ee[:, :], tail[:, :], ACT.Exp, scale=gs).then_inc(ee_done, 1)
                act.wait_ge(pads, 2 * PAIRS)
                for p in range(PAIRS):
                    for e in range(2):
                        c = (2 * p + e) * GLA_DK
                        act.dma_start(bup[p][HB * e:HB * e + GLA_DK, :],
                                      b_alpha[0:1, c:c + GLA_DK].rearrange("a n -> n a")).then_inc(w_loaded, 16)
                act.wait_ge(w_loaded, 16 * 14)
                act.wait_ge(cleared, 10)
                for x in first_pieces():
                    prep(*x)

                def squares(N):
                    act.wait_ge(o_done, N + 1)
                    if N:
                        act.wait_ge(ms_done, N)
                    for h in range(GLA_H):
                        nc.scalar.activation(sqj[:, :], ops[:, h * GLA_DV:(h + 1) * GLA_DV], ACT.Square,
                                             accum_out=ss[:, h:h + 1]).then_inc(squared, 1)
                        act.wait_ge(squared, GLA_H * N + h + 1)

                for g in range(NG):
                    for n in range(ST):
                        N = g * ST + n
                        act.wait_ge(vT_done, N + 1)
                        if N >= 2:
                            act.wait_ge(o_done, N - 1)
                        nc.scalar.activation(vt[N % 2][:, :], vps[:, 0:GV], ACT.Copy).then_inc(v_copied, 1)
                        if N:
                            act.wait_ge(kv_done, PAIRS * N)
                        for e in range(2):
                            rows = slice(GLA_C * e, GLA_C * (e + 1))
                            nc.scalar.activation(vz[rows, e, :], vps[rows, 0:GV], ACT.Copy).then_inc(v_copied, 1)
                        act.wait_ge(kT_done, N + 1)
                        nc.scalar.activation(kt[:, :], kps[:, 0:PAIRS * KR], ACT.Copy).then_inc(k_copied, 1)
                        if N:
                            squares(N - 1)
                        for x in pieces(g, n):
                            prep(*x)
                squares(NS - 1)

            @block.vector
            def _(dve):
                def prep(g, p, part):
                    u, s = PAIRS * g + p, g % 2
                    if part == 0:
                        dve.wait_ge(z_done, u + 1)
                        dve.wait_ge(abs_done, u + 1)
                        if u:
                            dve.wait_ge(scan_done, u)
                        nc.vector.tensor_scalar(la[:, :], zps[0:KR, :], bup[p][:, 0:1], 0.0, ALU.add, ALU.min
                                                ).then_inc(min_done, 1)
                        dve.wait_ge(min_done, u + 1)
                        dve.wait_ge(ln_done, u + 1)
                        nc.vector.tensor_tensor(la[:, :], la[:, :], zabs[:, :], ALU.subtract).then_inc(la_done, 1)
                        dve.wait_ge(la_done, u + 1)
                        if u:
                            dve.wait_ge(em_done, u)
                            dve.wait_ge(tail_done, u)
                        nc.vector.tensor_tensor_scan(b[:, :], keep[:, :], la[:, :], 0.0, ALU.mult, ALU.add
                                                     ).then_inc(scan_done, 1)
                    else:
                        dve.wait_ge(scan_done, u + 1)
                        if u:
                            dve.wait_ge(ee_done, u)
                        bc = b[:, :].rearrange("p (n c) -> p n c", c=GLA_C)
                        nc.vector.tensor_tensor(tail[:, :].rearrange("p (n c) -> p n c", c=GLA_C),
                                                bc[:, :, GLA_C - 1:GLA_C].to_broadcast([KR, GT // GLA_C, GLA_C]), bc,
                                                ALU.subtract).then_inc(tail_done, 1)
                        dve.wait_ge(ep_done, u + 1)
                        if g >= 2:
                            dve.wait_ge(o_done, ST * (g - 1))
                            dve.wait_ge(attn_done, ST * (g - 1))
                        nc.vector.scalar_tensor_tensor(qd[s][p][:, :], q[s][p][:, :], GLA_DK ** -0.5, ep[:, :],
                                                       ALU.mult, ALU.mult).then_inc(qd_done, 1)
                        dve.wait_ge(qd_done, u + 1)
                        for e in range(2):
                            rows = slice(HB * e, HB * e + GLA_DK)
                            nc.vector.tensor_copy(qpad[s][p][rows, e, :], qd[s][p][rows, :]).then_inc(qpad_done, 1)
                dve.wait_ge(cleared, 10)
                dve.wait_ge(w_loaded, 16 * 14)
                dve.wait_ge(qk_loaded[0], QK_DMAS)
                for x in first_pieces():
                    prep(*x)

                def normed(N):
                    dve.wait_ge(squared, GLA_H * (N + 1))
                    nc.vector.tensor_scalar(ms[:, :], ss[:, :], 1.0 / GLA_DV, EPS, ALU.mult, ALU.add).then_inc(ms_done, 1)
                    dve.wait_ge(rstd_done, N + 1)
                    if N >= 2:
                        dve.wait_ge(oT_done, N - 1)
                    nc.vector.tensor_tensor(on[N % 2][:, :].rearrange("p (h d) -> p h d", d=GLA_DV),
                                            ops[:, 0:GV].rearrange("p (h d) -> p h d", d=GLA_DV),
                                            rstd[:, :].unsqueeze(2).to_broadcast([P, GLA_H, GLA_DV]), ALU.mult
                                            ).then_inc(on_done, 1)

                def gated(N):
                    g, c0 = N // ST, (N % ST) * P
                    dve.wait_ge(oT_done, N + 1)
                    dve.wait_ge(gate_ready, 3 * (g + 1))
                    if N:
                        dve.wait_ge(mix_lo, N)
                    nc.vector.tensor_tensor(mx[:, :, :], otps[:, 0:3 * P].rearrange("p (j t) -> p j t", t=P),
                                            gate[g % 2][:, :, c0:c0 + P], ALU.mult).then_inc(mixed, 1)

                for g in range(NG):
                    s = g % 2
                    if g + 1 < NG:
                        dve.wait_ge(qk_loaded[(g + 1) % 2], QK_DMAS * ((g + 1) // 2 + 1))
                    for n in range(ST):
                        N = g * ST + n
                        dve.wait_ge(attn_done, N + 1)
                        if N >= 2:
                            dve.wait_ge(o_done, N - 1)
                        nc.vector.tensor_tensor(am[N % 2][:, :], aps[:, :], gla_mask[:, :, :].rearrange("p h t -> p (h t)"),
                                                ALU.mult).then_inc(masked, 1)
                        if N:
                            normed(N - 1)
                        if n == 0:
                            dve.wait_ge(prep_done, PAIRS * (g + 1))
                        for e in range(2):
                            m = 2 * N + e
                            for p in range(PAIRS):
                                if e == 0:
                                    dve.wait_ge(kv_done, PAIRS * N + p + 1)
                                if m:
                                    dve.wait_ge(state_done, 2 * PAIRS * (m - 1) + 2 * p + 2)
                                for a in range(2):
                                    rows = slice(HB * a, HB * a + GLA_DK)
                                    cols = slice(a * GLA_DV, (a + 1) * GLA_DV)
                                    nc.vector.scalar_tensor_tensor(
                                        S[(m + 1) % RING][p][rows, cols], S[m % RING][p][rows, cols],
                                        dec[s][p][rows, 2 * n + e:2 * n + e + 1],
                                        kvps[p][rows, e * W2 + a * GLA_DV:e * W2 + (a + 1) * GLA_DV],
                                        ALU.mult, ALU.add).then_inc(state_done, 1)
                        if N >= 2:
                            gated(N - 2)
                        for x in pieces(g, n):
                            prep(*x)
                normed(NS - 1)
                gated(NS - 2)
                gated(NS - 1)

            @block.gpsimd
            def _(pool):
                for p in range(PAIRS):
                    pool.memset(wup[p][:, :], 0.0).then_inc(pads, 1)
                    pool.memset(bup[p][:, :], 0.0).then_inc(pads, 1)
                for s in range(2):
                    for p in range(PAIRS):
                        pool.memset(q[s][p][:, :], 0.0).then_inc(cleared, 1)
                        pool.memset(kk[s][p][:, :], 0.0).then_inc(cleared, 1)
                for p in range(PAIRS):
                    pool.memset(qpad[0][p][:, :, :], 0.0)
                    pool.memset(qpad[1][p][:, :, :], 0.0)
                    for r in range(RING):
                        pool.memset(S[r][p][:, :], 0.0)
                pool.memset(vz[:, :, :], 0.0)
                pool.memset(half[:, :], -0.5)
                pool.memset(keep[:, :], 1.0).then_inc(cleared, 1)
                pool.wait_ge(cleared, 9)
                pool.memset(keep[:, :].rearrange("p (n c) -> p n c", c=GLA_C)[:, :, 0:1], 0.0).then_inc(cleared, 1)
                pool.wait_ge(cleared, 10)

                def prep(g, p, part):
                    u, s = PAIRS * g + p, g % 2
                    if part == 0:
                        return
                    if p == 0:
                        pool.wait_ge(qk_loaded[s], QK_DMAS * (g // 2 + 1))
                    if g >= 2:
                        pool.wait_ge(attn_done, ST * (g - 1))
                        pool.wait_ge(kT_done, ST * (g - 1))
                        pool.wait_ge(state_done, 4 * PAIRS * ST * (g - 1))
                    pool.wait_ge(em_done, u + 1)
                    nc.gpsimd.tensor_tensor(kd[s][p][:, :], kk[s][p][:, :], em[:, :], ALU.mult).then_inc(k_decayed, 1)
                    pool.wait_ge(ee_done, u + 1)
                    nc.gpsimd.tensor_tensor(kte[s][p][:, :], kk[s][p][:, :], ee[:, :], ALU.mult).then_inc(k_decayed, 1)
                    pool.wait_ge(k_decayed, 2 * u + 2)
                    pool.wait_ge(qpad_done, 2 * u + 2)
                    nc.gpsimd.tensor_copy(dec[s][p][:, :].unsqueeze(2),
                                          ep[:, :].rearrange("p (n c) -> p n c", c=GLA_C)[:, :, GLA_C - 1:GLA_C]
                                          ).then_inc(prep_done, 1)

                def gates(g):
                    s = g % 2
                    pool.wait_ge(w_loaded, 16 * 14)
                    pool.wait_ge(gate_loaded[s], 16 * (g // 2 + 1))
                    for j in range(3):
                        nc.gpsimd.tensor_scalar(gate[s][:, j, :], gate[s][:, j, :], gn[:, j:j + 1], 1.0,
                                                ALU.mult, ALU.mult).then_inc(gate_ready, 1)
                for x in first_pieces():
                    prep(*x)
                gates(0)

                def rstds(N):
                    pool.wait_ge(ms_done, N + 1)
                    if N:
                        pool.wait_ge(on_done, N)
                    nc.gpsimd.tensor_tensor(rstd[:, :], ms[:, :], half[:, :], ALU.pow).then_inc(rstd_done, 1)

                def split(N):
                    pool.wait_ge(mixed, N + 1)
                    if N >= 2:
                        pool.wait_ge(stored[N % 2], 32 * (N // 2))
                    nc.gpsimd.tensor_copy(mst[N % 2][HI][:, :, :], mx[:, :, :]).then_inc(mix_hi, 1)
                    pool.wait_ge(mix_hi, N + 1)
                    nc.gpsimd.tensor_tensor(mst[N % 2][LO][:, :, :], mx[:, :, :], mst[N % 2][HI][:, :, :].bitcast(F32),
                                            ALU.subtract).then_inc(mix_lo, 1)
                for g in range(NG):
                    for n in range(ST):
                        N = g * ST + n
                        if N:
                            rstds(N - 1)
                        if N >= 2:
                            split(N - 2)
                        if n == 3 and g + 1 < NG:
                            gates(g + 1)
                        for x in pieces(g, n):
                            prep(*x)
                rstds(NS - 1)
                split(NS - 2)
                split(NS - 1)


class Ring:

    def __init__(self, it, per):
        self.it, self.per = it, per

    def at(self, n):
        return self.it * self.per + n


def softmax_attention(nc, scr, ident, ident_b, mask, fox):
    tag = "fox" if fox else "att"
    W = T if fox else M
    NB = W // P
    NG = T // CH
    ROUNDS = (FOX_H if fox else MEM_H) // 2
    SCALE = DH ** -0.5
    QT = CH // P
    AUX = DH

    def score_units(hd, g):
        for i in range(CH // P):
            if fox:
                for c in range(g + 1):
                    yield hd, g, i, c, CH if c < g else P * (i + 1)
            else:
                yield hd, g, i, 0, W

    def key_units(hd, g):
        for j in range(4 * (g + 1) if fox else NB):
            yield hd, g, j, max(0, j - 4 * g) if fox else 0

    turns = [(hd, g) for hd in range(2) for g in range(NG)]
    keys_of = lambda g: CH * (g + 1) if fox else W
    ctx = ExitStack()
    with ctx:
        k = Pools(nc, ctx, tag)
        qa, qb = ([k.sb(f"{n}{e}", [P, T], F32R) for e in range(2)] for n in ("qa", "qb"))
        ka, kb = ([k.sb(f"{n}{e}", [P, W], F32R) for e in range(2)] for n in ("ka", "kb"))
        v = [k.sb(f"v{e}", [P, NB, 2 * DH], F32R) for e in range(2)]
        prob = [k.sb(f"prob{b}", [P, QT, W]) for b in range(2)]
        pT = [[k.sb(f"pT{b}{i}", [P, CH], F32R) for i in (HI, LO)] for b in range(2)]
        nmax = [k.sb(f"nmax{b}", [P, CH // P, 4]) for b in range(2)]
        nm = [k.sb(f"nm{b}", [P, CH // P]) for b in range(2)]
        rsum = [k.sb(f"rsum{b}", [P, CH // P]) for b in range(2)]
        rinv = [k.sb(f"rinv{b}", [P, CH // P]) for b in range(2)]
        gate = [k.sb(f"gate{b}", [DH, CH]) for b in range(2)]
        low, o1, o2 = k.sb("low", [DH, CH]), k.sb("o1", [DH, CH]), k.sb("o2", [DH, CH])
        zero = k.sb("zero", [DH, CH])
        om = [[k.sb(f"om{b}{i}", [DH, CH], F32R) for i in (HI, LO)] for b in range(2)]
        sps = [k.ps(f"sps{b}", [P, CH]) for b in range(2)]
        tps = [k.ps(f"tps{b}", [P, CH]) for b in range(3)]
        ops = [k.ps(f"ops{b}", [P, CH]) for b in range(2)]
        rps = k.ps("rps", [P, CH])
        names = ("cleared ones qkv_loaded gate_loaded0 gate_loaded1 scored negated maxed expd transposed pt_hi pt_lo "
                 "weighed inverted spread low_done added scaled gated o_hi o_lo stored0 stored1 sp_goes").split()
        (cleared, ones, qkv_loaded, gate_loaded0, gate_loaded1, scored, negated, maxed, expd, transposed, pt_hi, pt_lo,
         weighed, inverted, spread, low_done, added, scaled, gated, o_hi, o_lo, stored0, stored1, sp_goes) = map(k.sem, names)
        gate_loaded, stored = (gate_loaded0, gate_loaded1), (stored0, stored1)

        n_scores = sum(len(list(score_units(*t))) for t in turns)
        n_keys = sum(len(list(key_units(*t))) for t in turns)
        n_turns = len(turns)
        LOADS = 16 * 2 * (11 if fox else 7)

        def at_turn(t):
            return (sum(len(list(score_units(*x))) for x in turns[:t]),
                    sum(len(list(key_units(*x))) for x in turns[:t]))

        def plan(t):
            units = list(key_units(*turns[t]))
            ahead = list(score_units(*turns[t + 1])) if t + 1 < n_turns else []
            done, tiles, out = 0, 0, []
            for m in range(len(units)):
                upto = min(len(ahead), -(-len(ahead) * (m + 1) * 4 // (3 * len(units))))
                ready = upto * QT // len(ahead) if ahead else 0
                out.append((units[m], list(range(done, upto)), list(range(tiles, ready))))
                done, tiles = upto, ready
            return ahead, out

        def ends(t, m):
            return t >= 1 and m == 1

        with nc.Block() as block:
            @block.sync
            def _(sp):
                sp.wait_ge(cleared, 5 if fox else 4)
                with sp.Fori(0, ROUNDS) as r:
                    sp.wait_ge(weighed, r * n_keys)
                    sp.sem_inc(sp_goes, 1)
                    sp.wait_ge(gated, r * n_turns)
                    sp.sem_inc(sp_goes, 1)
                    qt = r if fox else r + 3
                    for e in range(2):
                        rows = slice(DH * e, DH * (e + 1))

                        def part(tile, i, rows=rows):
                            return scr.split[bass.ds(tile, 1), i, rows, :].rearrange("a p t -> (a p) t")

                        def key(i, rows=rows):
                            if fox:
                                return part(r + 5, i)
                            return scr.mem_k[bass.ds(r, 1), i, rows, :].rearrange("a p t -> (a p) t")
                        top, bottom = slice(0, DH), slice(DH, P)
                        loads = [(qa[e][top, :], part(qt, HI)), (qa[e][bottom, :], part(qt, LO)),
                                 (ka[e][top, :], key(LO)), (ka[e][bottom, :], key(HI)),
                                 (qb[e][top, :], part(qt, HI)), (kb[e][top, :], key(HI))]
                        if fox:
                            for i in range(2):
                                c = scr.crow[i, bass.ds(2 * r + e, 1), :]
                                loads.append((qb[e][AUX + 2 + i:AUX + 3 + i, :], c))
                                loads.append((kb[e][AUX + i:AUX + i + 1, :], scr.crow[2 + i, bass.ds(2 * r + e, 1), :]))
                        vs = (scr.fox_v if fox else scr.mem_v)[bass.ds(2 * r + e, 1)].rearrange("a p b c -> (a p) b c")
                        loads.append((v[e][:, :, :], vs))
                        for dst, src in loads:
                            sp.dma_start(dst.bitcast(F32), src).then_inc(qkv_loaded, 16)
                    def load_gate(t):
                        e, g = turns[t]
                        if t >= 2:
                            sp.wait_ge(gated, r * n_turns + t - 1)
                            sp.sem_inc(sp_goes, 1)
                        src = scr.gates[bass.ds(r + (3 if fox else 6), 1), DH * e:DH * (e + 1), g * CH:(g + 1) * CH]
                        sp.dma_start(gate[t % 2][:, :], src.rearrange("a p t -> (a p) t")
                                     ).then_inc(gate_loaded[t % 2], 16)
                    load_gate(0)
                    load_gate(1)
                    for t, (e, g) in enumerate(turns):
                        sp.wait_ge(o_lo, r * n_turns + t + 1)
                        sp.sem_inc(sp_goes, 1)
                        for i in (HI, LO):
                            dst = scr.mix[i, 4 * g:4 * g + 4, DH * e:DH * (e + 1), bass.ds(r + (3 if fox else 6), 1), :]
                            sp.dma_start(dst.rearrange("a p b t -> p a (b t)"),
                                         om[t % 2][i][:, :].rearrange("p (a t) -> p a t", t=P).bitcast(F32)
                                         ).then_inc(stored[t % 2], 16)
                        if t + 2 < n_turns:
                            load_gate(t + 2)
                for b in range(2):
                    sp.wait_ge(stored[b], 16 * ROUNDS * n_turns)

            @block.tensor
            def _(pe):
                with pe.Fori(0, ROUNDS) as r:
                    S, K, G, E = Ring(r, n_scores), Ring(r, n_keys), Ring(r, n_turns), Ring(r, QT * n_turns)
                    pe.wait_ge(qkv_loaded, (r + 1) * LOADS)
                    pe.wait_ge(o_lo, r * n_turns)

                    def scores(u, n):
                        e, g, i, c, w = u
                        if n >= 2:
                            pe.wait_ge(negated, S.at(n - 1))
                        qcols = slice((4 * g + i) * P, (4 * g + i + 1) * P)
                        wide = max(w, 2 * P)
                        kcols = slice(c * CH, c * CH + wide)
                        diagonal = fox and c == g
                        nc.tensor.matmul(sps[n % 2][:, 0:wide], qa[e][:, qcols], ka[e][:, kcols],
                                         start=True, stop=False)
                        if diagonal:
                            nc.tensor.matmul(sps[n % 2][:, w - P:w], ident_b[:, :], mask[:, :],
                                             start=False, stop=False, skip_group_check=True)
                        mm = nc.tensor.matmul(sps[n % 2][:, 0:wide], qb[e][:, qcols], kb[e][:, kcols],
                                              start=False, stop=True)
                        mm.then_inc(scored, 1)

                    def transposes(u, n, t, q0):
                        e, g, j, i0 = u
                        if n >= 3:
                            pe.wait_ge(pt_lo, K.at(n - 2))
                        if q0:
                            pe.wait_ge(expd, E.at(QT * (t + 1)))
                        for i in range(i0, 4):
                            mm = nc.tensor.transpose(tps[n % 3][:, i * P:(i + 1) * P],
                                                     prob[t % 2][:, i, j * P:(j + 1) * P], ident[:, :])
                        mm.then_inc(transposed, 1)

                    def weigh(u, n, t, first, last):
                        e, g, j, i0 = u
                        if first and t >= 2:
                            pe.wait_ge(added, G.at(t - 1))
                        for i in (HI, LO):
                            if i == HI:
                                pe.wait_ge(pt_hi, K.at(n + 1))
                            else:
                                pe.wait_ge(pt_lo, K.at(n + 1))
                            mm = nc.tensor.matmul(ops[t % 2][:, i0 * P:CH], v[e][:, j, :], pT[n % 2][i][:, i0 * P:CH],
                                                  start=(first and i == HI), stop=(last and i == LO),
                                                  skip_group_check=True)
                        mm.then_inc(weighed, 1)

                    def spread_sums(t):
                        pe.wait_ge(inverted, G.at(t + 1))
                        if t:
                            pe.wait_ge(scaled, G.at(t))
                        for i in range(4):
                            mm = nc.tensor.matmul(rps[0:DH, i * P:(i + 1) * P],
                                                  rinv[t % 2][:, i:i + 1].to_broadcast([P, DH]), ident[:, :],
                                                  start=True, stop=True)
                        mm.then_inc(spread, 1)

                    for n, u in enumerate(score_units(*turns[0])):
                        scores(u, n)
                    before = None
                    for t in range(n_turns):
                        k0, s1 = at_turn(t)[1], at_turn(t + 1)[0]
                        ahead, steps = plan(t)
                        for m, (u, made, _) in enumerate(steps):
                            transposes(u, k0 + m, t, m == 0)
                            for a in made:
                                scores(ahead[a], s1 + a)
                            if before:
                                weigh(*before)
                            before = (u, k0 + m, t, m == 0, m == len(steps) - 1)
                            if ends(t, m):
                                spread_sums(t - 1)
                    weigh(*before)
                    spread_sums(n_turns - 1)

            @block.scalar
            def _(act):
                with act.Fori(0, ROUNDS) as r:
                    K, G, E = Ring(r, n_keys), Ring(r, n_turns), Ring(r, QT * n_turns)

                    def exponentials(t, i):
                        w = keys_of(turns[t][1]) - (CH - P * (i + 1) if fox else 0)
                        act.wait_ge(maxed, E.at(QT * t + i + 1))
                        nc.scalar.activation(prob[t % 2][:, i, 0:w], prob[t % 2][:, i, 0:w], ACT.Exp,
                                             bias=nm[t % 2][:, i:i + 1], scale=-1.0,
                                             accum_out=rsum[t % 2][:, i:i + 1]).then_inc(expd, 1)

                    def pt_high(u, n):
                        e, g, j, i0 = u
                        act.wait_ge(transposed, K.at(n + 1))
                        act.wait_ge(weighed, K.at(max(n - 1, 0)))
                        nc.scalar.activation(pT[n % 2][HI][:, i0 * P:CH], tps[n % 3][:, i0 * P:CH], ACT.Copy
                                             ).then_inc(pt_hi, 1)

                    def low_half(t):
                        act.wait_ge(weighed, K.at(at_turn(t + 1)[1]))
                        act.wait_ge(added, G.at(t))
                        nc.scalar.activation(low[:, :], ops[t % 2][DH:P, :], ACT.Copy).then_inc(low_done, 1)

                    for i in range(QT):
                        exponentials(0, i)
                    for t in range(n_turns):
                        k0 = at_turn(t)[1]
                        for m, (u, _, tiles) in enumerate(plan(t)[1]):
                            pt_high(u, k0 + m)
                            for i in tiles:
                                exponentials(t + 1, i)
                            if ends(t, m):
                                low_half(t - 1)
                    low_half(n_turns - 1)

            @block.vector
            def _(dve):
                with dve.Fori(0, ROUNDS) as r:
                    S, K, G, E = Ring(r, n_scores), Ring(r, n_keys), Ring(r, n_turns), Ring(r, QT * n_turns)

                    def negate(u, n, t):
                        e, g, i, c, w = u
                        dve.wait_ge(scored, S.at(n + 1))
                        if t >= 2 and i == 0 and c == 0:
                            dve.wait_ge(transposed, K.at(at_turn(t - 1)[1]))
                        nc.vector.tensor_scalar(prob[t % 2][:, i, c * CH:c * CH + w], sps[n % 2][:, 0:w], -SCALE, None,
                                                ALU.mult, ALU.min, accum_out=nmax[t % 2][:, i, c:c + 1]
                                                ).then_inc(negated, 1)
                        if c == (g if fox else 0):
                            dve.wait_ge(negated, S.at(n + 1))
                            nc.vector.tensor_reduce(nm[t % 2][:, i:i + 1], nmax[t % 2][:, i, 0:c + 1], AX.X, ALU.min
                                                    ).then_inc(maxed, 1)

                    def pt_low(u, n):
                        e, g, j, i0 = u
                        dve.wait_ge(pt_hi, K.at(n + 1))
                        nc.vector.tensor_tensor(pT[n % 2][LO][:, i0 * P:CH], tps[n % 3][:, i0 * P:CH],
                                                pT[n % 2][HI][:, i0 * P:CH].bitcast(F32), ALU.subtract
                                                ).then_inc(pt_lo, 1)

                    def invert(t):
                        dve.wait_ge(expd, E.at(QT * (t + 1)))
                        if t >= 2:
                            dve.wait_ge(spread, G.at(t - 1))
                        nc.vector.reciprocal(rinv[t % 2][:, :], rsum[t % 2][:, :]).then_inc(inverted, 1)

                    def scale(t):
                        dve.wait_ge(scaled, G.at(t))
                        dve.wait_ge(low_done, G.at(t + 1))
                        nc.vector.tensor_tensor(o1[:, :], ops[t % 2][0:DH, :], low[:, :], ALU.add).then_inc(added, 1)
                        dve.wait_ge(added, G.at(t + 1))
                        dve.wait_ge(spread, G.at(t + 1))
                        dve.wait_ge(o_lo, G.at(t))
                        nc.vector.tensor_tensor(o2[:, :], rps[0:DH, :], o1[:, :], ALU.mult).then_inc(scaled, 1)

                    for n, u in enumerate(score_units(*turns[0])):
                        negate(u, n, 0)
                    for t in range(n_turns):
                        k0, s1 = at_turn(t)[1], at_turn(t + 1)[0]
                        ahead, steps = plan(t)
                        invert(t)
                        for m, (u, made, _) in enumerate(steps):
                            for a in made:
                                negate(ahead[a], s1 + a, t + 1)
                            pt_low(u, k0 + m)
                            if ends(t, m):
                                scale(t - 1)
                    scale(n_turns - 1)

            @block.gpsimd
            def _(pool):
                for e in range(2):
                    pool.memset(qb[e][:, :].bitcast(F32), 0.0).then_inc(cleared, 1)
                    pool.memset(kb[e][:, :].bitcast(F32), 0.0).then_inc(cleared, 1)
                pool.memset(zero[:, :], 0.0).then_inc(ones, 1)
                if fox:
                    pool.wait_ge(cleared, 4)
                    for e in range(2):
                        pool.memset(qb[e][AUX:AUX + 2, :].bitcast(F32), 1.0).then_inc(ones, 1)
                        pool.memset(kb[e][AUX:AUX + 4, :].bitcast(F32), 1.0).then_inc(ones, 1)
                    pool.wait_ge(ones, 5)
                    pool.sem_inc(cleared, 1)
                with pool.Fori(0, ROUNDS) as r:
                    G = Ring(r, n_turns)
                    for t in range(n_turns):
                        b = t % 2
                        pool.wait_ge(gate_loaded[b], 16 * (r * (n_turns // 2) + t // 2 + 1))
                        pool.wait_ge(scaled, G.at(t + 1))
                        nc.gpsimd.tensor_tensor(o2[:, :], o2[:, :], gate[b][:, :], ALU.mult).then_inc(gated, 1)
                        pool.wait_ge(gated, G.at(t + 1))
                        pool.wait_ge(stored[b], 32 * (r * (n_turns // 2) + t // 2))
                        nc.gpsimd.tensor_tensor(om[b][HI][:, :], o2[:, :], zero[:, :], ALU.add).then_inc(o_hi, 1)
                        pool.wait_ge(o_hi, G.at(t + 1))
                        nc.gpsimd.tensor_tensor(om[b][LO][:, :], o2[:, :], om[b][HI][:, :].bitcast(F32),
                                                ALU.subtract).then_inc(o_lo, 1)


def project_out(nc, scr, out, x, w_out, final_norm_g):
    x_t = x[0].rearrange("(t p) d -> t p d", p=P)
    out_t = out[0].rearrange("(t p) d -> t p d", p=P)
    NC = D // CH
    ctx = ExitStack()
    with ctx:
        k = Pools(nc, ctx, "out")
        g = k.sb("g", [P, D])
        w_raw = [k.sb(f"wraw{s}", [P, D]) for s in range(2)]
        w = [k.sb(f"w{i}", [P, MIX_T, D], F32R) for i in (HI, LO)]
        mix = [[k.sb(f"mix{s}{i}", [P, MIX_T, P], F32R) for i in (HI, LO)] for s in range(2)]
        xin, y, o = ([k.sb(f"{n}{s}", [P, D]) for s in range(2)] for n in ("x", "y", "o"))
        junk = k.sb("junk", [P, D])
        st = k.sb("st", [P, 4])
        yps = [k.ps(f"yps{s}", [P, NC, CH]) for s in range(2)]
        names = ("g_loaded w_loaded0 w_loaded1 w_hi w_lo mix_loaded0 mix_loaded1 x_loaded0 x_loaded1 projected added "
                 "squared mean_done root_done rstd_done normed stored0 stored1 sp_goes").split()
        (g_loaded, w_loaded0, w_loaded1, w_hi, w_lo, mix_loaded0, mix_loaded1, x_loaded0, x_loaded1, projected, added,
         squared, mean_done, root_done, rstd_done, normed, stored0, stored1, sp_goes) = map(k.sem, names)
        w_loaded, mix_loaded = (w_loaded0, w_loaded1), (mix_loaded0, mix_loaded1)
        x_loaded, stored = (x_loaded0, x_loaded1), (stored0, stored1)
        with nc.Block() as block:
            @block.sync
            def _(sp):
                def load(t, s):
                    for i in (HI, LO):
                        sp.dma_start(mix[s][i][:, :, :].bitcast(F32),
                                     scr.mix[i, bass.ds(t, 1)].rearrange("a p k t -> (a p) k t")
                                     ).then_inc(mix_loaded[s], 16)
                    sp.dma_start(xin[s][:, :], x_t[bass.ds(t, 1)].rearrange("a p d -> (a p) d")
                                 ).then_inc(x_loaded[s], 16)
                for kk in range(MIX_T):
                    if kk >= 2:
                        sp.wait_ge(w_lo, kk - 1)
                    sp.dma_start(w_raw[kk % 2][:, :], w_out[0, kk * P:(kk + 1) * P, :]).then_inc(w_loaded[kk % 2], 16)
                    if kk == 1:
                        load(0, 0)
                load(1, 1)
                sp.dma_start(g[:, :], final_norm_g.rearrange("(a d) -> a d", a=1)[0].partition_broadcast(P)
                             ).then_inc(g_loaded, 16)
                with sp.Fori(1, TT // 2) as h:
                    for s in range(2):
                        t = 2 * h + s
                        sp.wait_ge(projected, t - 1)
                        sp.sem_inc(sp_goes, 1)
                        sp.wait_ge(added, t - 1)
                        sp.sem_inc(sp_goes, 1)
                        load(t, s)

            @block.gpsimd
            def _(pool):
                for kk in range(MIX_T):
                    pool.wait_ge(w_loaded[kk % 2], 16 * (kk // 2 + 1))
                    nc.gpsimd.tensor_copy(w[HI][:, kk, :], w_raw[kk % 2][:, :]).then_inc(w_hi, 1)
                    pool.wait_ge(w_hi, kk + 1)
                    nc.gpsimd.tensor_tensor(w[LO][:, kk, :], w_raw[kk % 2][:, :], w[HI][:, kk, :].bitcast(F32),
                                            ALU.subtract).then_inc(w_lo, 1)

            @block.tensor
            def _(pe):
                def tile(h, s, first):
                    t = 2 * h + s
                    pe.wait_ge(mix_loaded[s], 32 * (h + 1))
                    if not first:
                        pe.wait_ge(added, t - 1)
                    for kk in range(MIX_T):
                        if first and s == 0:
                            pe.wait_ge(w_lo, kk + 1)
                        for n, (a, b) in enumerate(PASSES):
                            for c in range(NC):
                                mm = nc.tensor.matmul(yps[s][:, c, :], mix[s][a][:, kk, :],
                                                      w[b][:, kk, c * CH:(c + 1) * CH],
                                                      start=(kk == 0 and n == 0), stop=(kk == MIX_T - 1 and n == 2))
                    mm.then_inc(projected, 1)
                for s in range(2):
                    tile(0, s, True)
                with pe.Fori(1, TT // 2) as h:
                    for s in range(2):
                        tile(h, s, False)

            @block.vector
            def _(dve):
                dve.wait_ge(g_loaded, 16)
                with dve.Fori(0, TT // 2) as h:
                    for s in range(2):
                        t = 2 * h + s
                        dve.wait_ge(x_loaded[s], 16 * (h + 1))
                        dve.wait_ge(projected, t + 1)
                        nc.vector.tensor_tensor(y[s][:, :], yps[s][:, :, :].rearrange("p c n -> p (c n)"), xin[s][:, :],
                                                ALU.add).then_inc(added, 1)
                        dve.wait_ge(squared, t + 1)
                        nc.vector.tensor_scalar(st[:, 1:2], st[:, 0:1], 1.0 / D, EPS, ALU.mult, ALU.add
                                                ).then_inc(mean_done, 1)
                        dve.wait_ge(root_done, t + 1)
                        nc.vector.reciprocal(st[:, 3:4], st[:, 2:3]).then_inc(rstd_done, 1)
                        dve.wait_ge(rstd_done, t + 1)
                        dve.wait_ge(stored[s], 16 * h)
                        nc.vector.scalar_tensor_tensor(o[s][:, :], y[s][:, :], st[:, 3:4], g[:, :], ALU.mult, ALU.mult
                                                       ).then_inc(normed, 1)

            @block.scalar
            def _(act):
                with act.Fori(0, TT // 2) as h:
                    for s in range(2):
                        t = 2 * h + s
                        act.wait_ge(added, t + 1)
                        nc.scalar.activation(junk[:, :], y[s][:, :], ACT.Square, accum_out=st[:, 0:1]).then_inc(squared, 1)
                        act.wait_ge(mean_done, t + 1)
                        nc.scalar.activation(st[:, 2:3], st[:, 1:2], ACT.Sqrt).then_inc(root_done, 1)
                        act.wait_ge(normed, t + 1)
                        act.dma_start(out_t[bass.ds(t, 1)].rearrange("a p d -> (a p) d"), o[s][:, :]
                                      ).then_inc(stored[s], 16)
                for s in range(2):
                    act.wait_ge(stored[s], 16 * (TT // 2))


def hymba_block(nc, out, x, mem, norm_g, w_cols, w_tok, w_alpha_up, b_alpha, b_forget, gla_norm_g, mem_norm_g,
                w_mem_kv, w_out, final_norm_g):
    scr = Scratch(nc)
    ctx = ExitStack()
    with ctx:
        k = Pools(nc, ctx, "all")
        ident, ident_b, fox_mask, gla_mask = constants(nc, k)
        memory_keys_values(nc, scr, ident, mem, mem_norm_g, w_mem_kv)
        h_ctx = ExitStack()
        with h_ctx:
            kh = Pools(nc, h_ctx, "h")
            hT = [kh.sb(f"T{i}", [P, KT, T], F32R) for i in (HI, LO)]
            fglr = kh.sb("fglr", [P, TT, FGLR])
            project_tokens(nc, scr, ident, hT, fglr, x, norm_g, w_tok)
            project_columns(nc, scr, ident, hT, fglr, w_cols, b_forget)
        gated_linear_attention(nc, scr, ident, gla_mask, w_alpha_up, b_alpha, gla_norm_g)
        softmax_attention(nc, scr, ident, ident_b, fox_mask, fox=False)
        softmax_attention(nc, scr, ident, ident_b, fox_mask, fox=True)
        project_out(nc, scr, out, x, w_out, final_norm_g)


_OUTS = [((1, T, D), "float32")]


def laid_out(inputs):
    import numpy as np

    a = {n: np.ascontiguousarray(inputs[n]) for n in (
        "x", "mem", "norm_g", "w_alpha_up", "b_alpha", "b_forget", "gla_norm_g", "mem_norm_g", "w_mem_kv",
        "w_out", "final_norm_g")}
    w = np.ascontiguousarray(inputs["w_in"])[0].reshape(KT, P, -1)
    starts = ([F_Q + P * i for i in range(3)] + [M_Q + P * i for i in range(2)] + [F_K + P * i for i in range(3)]
              + [G_GATE + P * i for i in range(3)] + [F_GATE + P * i for i in range(3)]
              + [M_GATE + P * i for i in range(2)] + [G_Q + P * i for i in range(6)])
    a["w_cols"] = np.ascontiguousarray(np.stack([w[:, :, c:c + P].transpose(1, 0, 2) for c in starts]))
    tok = np.concatenate([w[:, :, F_V:F_V + 384], w[:, :, F_FG:F_FG + FOX_H], w[:, :, G_LR:G_LR + GLA_R]], axis=2)
    a["w_tok"] = np.ascontiguousarray(tok.transpose(1, 0, 2))
    return a


def kernel(**inputs):
    import numpy as np
    import concourse.bacc as bacc
    from concourse.bass_utils import run_bass_kernel_spmd

    nc = bacc.Bacc("TRN2", target_bir_lowering=False, num_devices=1)
    arrays, args = {}, {}
    for name, a in laid_out(inputs).items():
        arrays[f"in_{name}"] = a
        args[name] = nc.dram_tensor(f"in_{name}", a.shape, mybir.dt.from_np(a.dtype), kind="ExternalInput").ap()
    shape, dtype = _OUTS[0]
    out = nc.dram_tensor("out_0", shape, mybir.dt.from_np(np.dtype(dtype)), kind="ExternalOutput").ap()
    hymba_block(nc, out=out, **args)
    r = run_bass_kernel_spmd(nc, [arrays], core_ids=[0])
    return r.results[0]["out_0"]
```

```python
import concourse.bass as bass
from concourse import mybir
from contextlib import ExitStack

F32 = mybir.dt.float32
F32R = mybir.dt.float32r
BF16 = mybir.dt.bfloat16
ALU = mybir.AluOpType
ACT = mybir.ActivationFunctionType
AX = mybir.AxisListType

P = 128
D = 1024
T = 2048
M = 256
KT = D // P
TT = T // P
EPS = 1e-6
CH = 512
NCH = T // CH

GLA_H, GLA_DK, GLA_DV, GLA_R, GLA_C, GLA_GATE = 4, 48, 96, 16, 64, 16.0
FOX_H, DH = 6, 64
MEM_H = 4
MIX_T = 8

TOK_C = FOX_H * DH + FOX_H + GLA_R
FGLR = FOX_H + GLA_R
NSPLIT, NGATE, NRAW = 8, 8, 6
NCOL = NSPLIT + NGATE + NRAW

IN = [192, 192, 384, 16, 384, 384, 384, 384, 6, 384, 256, 256]
OFF = [sum(IN[:i]) for i in range(len(IN) + 1)]
G_Q, G_K, G_V, G_LR, G_GATE, F_Q, F_K, F_V, F_FG, F_GATE, M_Q, M_GATE = OFF[:-1]

HI, LO = 0, 1
PASSES = [(HI, HI), (HI, LO), (LO, HI)]


class Scratch:

    def __init__(self, nc):
        def dram(name, shape, dt):
            return nc.dram_tensor(name, shape, dt).ap()
        self.split = dram("scr_split", [NSPLIT, 2, P, T], F32)
        self.gates = dram("scr_gates", [NGATE, P, T], F32)
        self.raw = dram("scr_raw", [NRAW * P, T], F32)
        self.fox_v = dram("scr_fox_v", [FOX_H, P, TT, 2 * DH], F32)
        self.mem_k = dram("scr_mem_k", [2, 2, P, M], F32)
        self.mem_v = dram("scr_mem_v", [MEM_H, P, 2, 2 * DH], F32)
        self.lr = dram("scr_lr", [GLA_R, T], F32)
        self.crow = dram("scr_crow", [4, FOX_H, T], F32)
        self.mix = dram("scr_mix", [2, TT, P, MIX_T, P], F32)


class Pools:

    def __init__(self, nc, ctx, tag, clears=False):
        self.nc, self.ctx, self.tag = nc, ctx, tag
        self.cleared = [] if clears else None
        if clears:
            ctx.callback(self.clear)

    def clear(self):
        self.nc.clear_and_free_semaphores(self.cleared)
        self.nc.all_engine_barrier()

    def sb(self, name, shape, dt=F32):
        return self.ctx.enter_context(self.nc.sbuf_tensor(f"{self.tag}_{name}", shape, dt))

    def ps(self, name, shape, dt=F32):
        return self.ctx.enter_context(self.nc.psum_tensor(f"{self.tag}_{name}", shape, dt))

    def sem(self, name):
        if self.cleared is None:
            return self.ctx.enter_context(self.nc.semaphore(f"{self.tag}_{name}"))
        sem = self.nc.alloc_semaphore(f"{self.tag}_{name}")
        self.cleared.append(sem)
        return sem


def constants(nc, k):
    ident = k.sb("ident", [P, P])
    ident_b = k.sb("ident_b", [P, P], BF16)
    fox_mask = k.sb("fox_mask", [P, P], BF16)
    gla_mask = k.sb("gla_mask", [P, 4, P])
    made = k.sem("made")
    with nc.Block() as block:
        @block.gpsimd
        def _(pool):
            pool.memset(ident[:, :], 0.0).then_inc(made, 1)
            pool.memset(ident_b[:, :], 0.0).then_inc(made, 1)
            pool.memset(fox_mask[:, :], 0.0).then_inc(made, 1)
            pool.memset(gla_mask[:, :, :], 1.0).then_inc(made, 1)
            pool.wait_ge(made, 4)
            for m in (ident, ident_b):
                pool.affine_select(out=m[:, :], in_=m[:, :], compare_op=ALU.not_equal, fill=1.0,
                                   base=0, pattern=[[-1, P]], channel_multiplier=1).then_inc(made, 1)
            pool.affine_select(out=fox_mask[:, :], in_=fox_mask[:, :], compare_op=ALU.is_ge, fill=-1e38,
                               base=0, pattern=[[-1, P]], channel_multiplier=1).then_inc(made, 1)
            pool.affine_select(out=gla_mask[:, :, :], in_=gla_mask[:, :, :], compare_op=ALU.is_ge, fill=0.0,
                               base=0, pattern=[[0, 4], [1, P]], channel_multiplier=-1).then_inc(made, 1)
            pool.wait_ge(made, 8)
            pool.memset(gla_mask[0:GLA_C, :, GLA_C:P], 0.0).then_inc(made, 1)
            pool.wait_ge(made, 9)
    return ident, ident_b, fox_mask, gla_mask


def memory_keys_values(nc, scr, ident, tokens, mem, mem_norm_g, w_mem_kv):
    MT = M // P
    KV = 2 * MEM_H * DH
    QUARTERS = 4
    QK = KT // QUARTERS
    ctx = ExitStack()
    with ctx:
        k = Pools(nc, ctx, "mem", clears=True)
        x, g, xn, sq = k.sb("x", [P, MT, D]), k.sb("g", [P, D]), k.sb("xn", [P, MT, D]), k.sb("sq", [P, D])
        xT = [k.sb(f"xT{i}", [P, KT, M], F32R) for i in (HI, LO)]
        w = k.sb("w", [P, KT, KV])
        wp = [k.sb(f"w{i}", [P, KT, KV], F32R) for i in (HI, LO)]
        kst = [k.sb(f"k{i}", [P, MT, M], F32R) for i in (HI, LO)]
        vst = k.sb("v", [P, MT, MEM_H, 2, DH], F32R)
        ss, ms, rstd, half = (k.sb(n, [P, MT]) for n in ("ss", "ms", "rstd", "half"))
        tps = [k.ps(f"tps{i}", [P, 4, P]) for i in range(2)]
        kps, vps = k.ps("kps", [P, MT, M]), k.ps("vps", [P, MT, M])
        loaded, w_loaded, filled, squared, mean_done, rstd_done, normed = map(
            k.sem, "loaded w_loaded filled squared mean_done rstd_done normed".split())
        transposed, hi_done, lo_done, w_hi, w_lo, k_done, v_done, ev_hi, ev_lo, stored = map(
            k.sem, "transposed hi_done lo_done w_hi w_lo k_done v_done ev_hi ev_lo stored".split())

        def columns(i):
            t, c = divmod(i, 2)
            return slice(4 * c, 4 * c + 4), slice(t * P, (t + 1) * P)

        with nc.Block() as block:
            @block.sync
            def _(sp):
                sp.dma_start(x[:, :, :], mem[0].rearrange("(t p) d -> p t d", p=P)).then_inc(loaded, 16)
                sp.dma_start(g[:, :], mem_norm_g[0].partition_broadcast(P)).then_inc(loaded, 16)
                sp.dma_start(w[:, :, :], w_mem_kv[0].rearrange("(k p) n -> p k n", p=P)).then_inc(w_loaded, 16)
                tokens.first_loads(sp)
                sp.wait_ge(ev_lo, 1)
                for i in range(MT):
                    for part in (HI, LO):
                        sp.dma_start(scr.mem_k[i, part], kst[part][:, i, :].bitcast(F32)).then_inc(stored, 16)
                for t in range(MT):
                    sp.wait_ge(ev_lo, t + 2)
                    sp.dma_start(scr.mem_v[:, :, t, :].rearrange("h p c -> p h c"),
                                 vst[:, t, :, :, :].rearrange("p h a c -> p h (a c)").bitcast(F32)).then_inc(stored, 16)
                sp.wait_ge(stored, 16 * 3 * MT)

            @block.scalar
            def _(act):
                act.wait_ge(loaded, 32)
                for t in range(MT):
                    if t:
                        act.wait_ge(squared, t)
                    nc.scalar.activation(sq[:, :], x[:, t, :], ACT.Square,
                                         accum_out=ss[:, t:t + 1]).then_inc(squared, 1)

                def weights_high(q):
                    act.wait_ge(w_loaded, 16)
                    ks = slice(QK * q, QK * (q + 1))
                    nc.scalar.activation(wp[HI][:, ks, :], w[:, ks, :], ACT.Copy).then_inc(w_hi, 1)

                for i in range(2 * MT):
                    if i % 2 == 0:
                        weights_high(i)
                        weights_high(i + 1)
                    act.wait_ge(transposed, i + 1)
                    ks, cols = columns(i)
                    nc.scalar.activation(xT[HI][:, ks, cols], tps[i % 2][:, :, :], ACT.Copy).then_inc(hi_done, 1)
                tokens.squares(act, 0, 0)
                act.wait_ge(k_done, MT)
                nc.scalar.activation(kst[HI][:, :, :], kps[:, :, :], ACT.Copy).then_inc(ev_hi, 1)
                tokens.high_part(act, 0, 0)
                tokens.squares(act, 0, 1)
                act.wait_ge(v_done, MT)
                for t in range(MT):
                    nc.scalar.activation(vst[:, t, :, HI, :], vps[:, t, :].rearrange("p (h c) -> p h c", c=DH),
                                         ACT.Copy).then_inc(ev_hi, 1)

            @block.vector
            def _(dve):
                dve.wait_ge(squared, MT)
                nc.vector.tensor_scalar(ms[:, :], ss[:, :], 1.0 / D, EPS, ALU.mult, ALU.add).then_inc(mean_done, 1)
                dve.wait_ge(loaded, 32)
                dve.wait_ge(rstd_done, 1)
                for t in range(MT):
                    nc.vector.scalar_tensor_tensor(xn[:, t, :], x[:, t, :], rstd[:, t:t + 1], g[:, :],
                                                   ALU.mult, ALU.mult).then_inc(normed, 1)

                def weights_low(q):
                    dve.wait_ge(w_hi, q + 1)
                    ks = slice(QK * q, QK * (q + 1))
                    nc.vector.tensor_tensor(wp[LO][:, ks, :], w[:, ks, :], wp[HI][:, ks, :].bitcast(F32),
                                            ALU.subtract).then_inc(w_lo, 1)

                for i in range(2 * MT):
                    if i % 2 == 0:
                        weights_low(i)
                        weights_low(i + 1)
                    dve.wait_ge(hi_done, i + 1)
                    ks, cols = columns(i)
                    nc.vector.tensor_tensor(xT[LO][:, ks, cols], tps[i % 2][:, :, :], xT[HI][:, ks, cols].bitcast(F32),
                                            ALU.subtract).then_inc(lo_done, 1)
                tokens.normalise(dve, 0, 0)
                dve.wait_ge(ev_hi, 1)
                nc.vector.tensor_tensor(kst[LO][:, :, :], kps[:, :, :], kst[HI][:, :, :].bitcast(F32),
                                        ALU.subtract).then_inc(ev_lo, 1)
                tokens.low_part(dve, 0, 0)
                tokens.normalise(dve, 0, 1)
                dve.wait_ge(ev_hi, 1 + MT)
                for t in range(MT):
                    nc.vector.tensor_tensor(vst[:, t, :, LO, :], vps[:, t, :].rearrange("p (h c) -> p h c", c=DH),
                                            vst[:, t, :, HI, :].bitcast(F32), ALU.subtract).then_inc(ev_lo, 1)

            @block.gpsimd
            def _(pool):
                pool.memset(half[:, :], -0.5).then_inc(filled, 1)
                pool.memset(tokens.half[:, :], -0.5).then_inc(filled, 1)
                pool.wait_ge(filled, 2)
                pool.wait_ge(mean_done, 1)
                nc.gpsimd.tensor_tensor(rstd[:, :], ms[:, :], half[:, :], ALU.pow).then_inc(rstd_done, 1)
                for kk in range(KT):
                    tokens.split_weights(pool, kk)
                    if kk == KT // 2 - 1:
                        tokens.rstds(pool, 0, 0)
                    if kk == KT - 2:
                        tokens.rstds(pool, 0, 1)

            @block.tensor
            def _(pe):
                for i in range(2 * MT):
                    t, c = divmod(i, 2)
                    pe.wait_ge(normed, t + 1)
                    if i >= 2:
                        pe.wait_ge(lo_done, i - 1)
                    for j in range(4):
                        kk = 4 * c + j
                        mm = nc.tensor.transpose(tps[c][:, j, :], xn[:, t, kk * P:(kk + 1) * P], ident[:, :])
                    mm.then_inc(transposed, 1)
                pe.wait_ge(lo_done, 2 * MT)
                for i in range(MT):
                    for kk in range(KT):
                        pe.wait_ge(w_lo, kk // QK + 1)
                        for n, (a, b) in enumerate(PASSES):
                            mm = nc.tensor.matmul(kps[:, i, :], wp[a][:, kk, i * P:(i + 1) * P], xT[b][:, kk, :],
                                                  start=(kk == 0 and n == 0), stop=(kk == KT - 1 and n == 2))
                    mm.then_inc(k_done, 1)
                tokens.transposes(pe, 0, 0, first=True)
                for t in range(MT):
                    for kk in range(KT):
                        for n, (a, b) in enumerate(PASSES):
                            mm = nc.tensor.matmul(vps[:, t, :], xT[a][:, kk, t * P:(t + 1) * P],
                                                  wp[b][:, kk, M:2 * M],
                                                  start=(kk == 0 and n == 0), stop=(kk == KT - 1 and n == 2))
                    mm.then_inc(v_done, 1)


class TokenStage:

    RAW = 4

    def __init__(self, nc, ctx, ctx_steps, scr, ident, x, norm_g, w_tok):
        self.nc, self.scr, self.ident, self.norm_g, self.w_tok = nc, scr, ident, norm_g, w_tok
        self.x_t = x[0].rearrange("(t p) d -> t p d", p=P)
        k = Pools(nc, ctx, "tok")
        self.g = k.sb("g", [P, D])
        self.xin = [k.sb(f"xin{s}", [P, D]) for s in range(2)]
        self.xn = k.sb("xn", [P, D])
        self.ssq, self.mean, self.rstd, self.half = (k.sb(n, [P, 1]) for n in ("ssq", "mean", "rstd", "half"))
        self.raws = k.sb("wraw", [P, T])
        self.w_raw = [self.raws[:, TOK_C * s:TOK_C * (s + 1)] for s in range(self.RAW)]
        self.w = [k.sb(f"w{i}", [P, KT, TOK_C], F32R) for i in (HI, LO)]
        self.slot = [[k.sb(f"slot{s}{i}", [P, KT, P], F32R) for i in (HI, LO)] for s in range(2)]
        k = Pools(nc, ctx_steps, "tok", clears=True)
        self.tps = [k.ps(f"tps{c}", [P, 4, P]) for c in range(2)]
        self.junk = k.ps("junk", [P, 2 * CH])
        (self.g_loaded, self.w_hi, self.w_lo, self.squared, self.mean_done, self.rstd_done, self.normed,
         self.transposed, self.hi_done, self.lo_done) = map(
            k.sem, "g_loaded w_hi w_lo squared mean_done rstd_done normed transposed hi_done lo_done".split())
        self.x_loaded = [k.sem(f"x_loaded{s}") for s in range(2)]
        self.w_loaded = [k.sem(f"w_loaded{s}") for s in range(self.RAW)]

    def first_loads(self, sp):
        for t in range(2):
            sp.dma_start(self.xin[t][:, :], self.x_t[t]).then_inc(self.x_loaded[t], 16)
            if t == 0:
                sp.dma_start(self.g[:, :], self.norm_g[0].partition_broadcast(P)).then_inc(self.g_loaded, 16)
        for kk in range(KT):
            if kk >= self.RAW:
                sp.wait_ge(self.w_lo, kk - self.RAW + 1)
            sp.dma_start(self.w_raw[kk % self.RAW][:, :], self.w_tok[:, kk, :]
                         ).then_inc(self.w_loaded[kk % self.RAW], 16)

    def split_weights(self, pool, kk):
        raw, hi = self.w_raw[kk % self.RAW], self.w[HI][:, kk, :]
        pool.wait_ge(self.w_loaded[kk % self.RAW], 16 * (kk // self.RAW + 1))
        pool.tensor_copy(hi, raw[:, :]).then_inc(self.w_hi, 1)
        pool.wait_ge(self.w_hi, kk + 1)
        pool.tensor_tensor(self.w[LO][:, kk, :], raw[:, :], hi.bitcast(F32), ALU.subtract).then_inc(self.w_lo, 1)

    def squares(self, act, h, s):
        t = 2 * h + s
        act.wait_ge(self.x_loaded[s], 16 * (h + 1))
        act.wait_ge(self.mean_done, t)
        act.activation(self.junk[:, :], self.xin[s][:, :], ACT.Square, accum_out=self.ssq[:, :]
                       ).then_inc(self.squared, 1)

    def rstds(self, pool, h, s):
        t = 2 * h + s
        pool.wait_ge(self.mean_done, t + 1)
        pool.wait_ge(self.normed, t)
        pool.tensor_tensor(self.rstd[:, :], self.mean[:, :], self.half[:, :], ALU.pow).then_inc(self.rstd_done, 1)

    def normalise(self, dve, h, s):
        t = 2 * h + s
        dve.wait_ge(self.squared, t + 1)
        dve.tensor_scalar(self.mean[:, :], self.ssq[:, :], 1.0 / D, EPS, ALU.mult, ALU.add).then_inc(self.mean_done, 1)
        dve.wait_ge(self.transposed, 2 * t)
        dve.wait_ge(self.g_loaded, 16)
        dve.wait_ge(self.rstd_done, t + 1)
        dve.scalar_tensor_tensor(self.xn[:, :], self.xin[s][:, :], self.rstd[:, :], self.g[:, :],
                                 ALU.mult, ALU.mult).then_inc(self.normed, 1)

    def transposes(self, pe, h, s, first=False):
        t = 2 * h + s
        pe.wait_ge(self.normed, t + 1)
        for c in range(2):
            if not first:
                pe.wait_ge(self.lo_done, 2 * t - 1 + c)
            for j in range(4):
                kk = 4 * c + j
                mm = pe.transpose(self.tps[c][:, j, :], self.xn[:, kk * P:(kk + 1) * P], self.ident[:, :])
            mm.then_inc(self.transposed, 1)

    def high_part(self, act, h, s):
        t = 2 * h + s
        for c in range(2):
            act.wait_ge(self.transposed, 2 * t + c + 1)
            act.activation(self.slot[s][HI][:, 4 * c:4 * c + 4, :], self.tps[c][:, :, :], ACT.Copy
                           ).then_inc(self.hi_done, 1)

    def low_part(self, dve, h, s):
        t = 2 * h + s
        for c in range(2):
            dve.wait_ge(self.hi_done, 2 * t + c + 1)
            dve.tensor_tensor(self.slot[s][LO][:, 4 * c:4 * c + 4, :], self.tps[c][:, :, :],
                              self.slot[s][HI][:, 4 * c:4 * c + 4, :].bitcast(F32), ALU.subtract
                              ).then_inc(self.lo_done, 1)


def project_tokens(nc, scr, tk, hT, fglr):
    V = FOX_H * DH
    slot, w = tk.slot, tk.w
    ctx = ExitStack()
    with ctx:
        k = Pools(nc, ctx, "tok2", clears=True)
        vst = [k.sb(f"vst{s}", [P, FOX_H, 2, DH], F32R) for s in range(2)]
        mps = [k.ps(f"mps{s}", [P, CH]) for s in range(2)]
        (kept_hi, kept_lo, multiplied, v_hi, v_lo, v_stored0, v_stored1, pool_goes, act_goes) = map(
            k.sem, "kept_hi kept_lo multiplied v_hi v_lo v_stored0 v_stored1 pool_goes act_goes".split())
        v_stored = (v_stored0, v_stored1)

        def steps(eng, step):
            for t in (0, 1):
                step(0, t, True, True)
            with eng.Fori(1, TT // 2 - 1) as h:
                for s in range(2):
                    step(h, s, True, True)
            step(TT // 2 - 1, 0, True, False)
            step(TT // 2 - 1, 1, False, False)

        with nc.Block() as block:
            @block.sync
            def _(sp):
                def store(t, s):
                    sp.wait_ge(v_lo, t + 1)
                    sp.dma_start(scr.fox_v[:, :, bass.ds(t, 1), :].rearrange("h p a c -> p h (a c)"),
                                 vst[s][:, :, :, :].rearrange("p h a c -> p h (a c)").bitcast(F32)).then_inc(v_stored[s], 16)

                def step(h, s, _, more):
                    t = 2 * h + s
                    if more:
                        sp.wait_ge(tk.normed, t + 1)
                        sp.dma_start(tk.xin[s][:, :], tk.x_t[bass.ds(t + 2, 1)].rearrange("a p d -> (a p) d")
                                     ).then_inc(tk.x_loaded[s], 16)
                    if not (isinstance(h, int) and t == 0):
                        store(t - 1, 1 - s)
                steps(sp, step)
                store(TT - 1, 1)
                for s in range(2):
                    sp.wait_ge(v_stored[s], 16 * TT // 2)

            @block.scalar
            def _(act):
                def keep_high(h, s):
                    t = 2 * h + s
                    act.wait_ge(tk.hi_done, 2 * t + 2)
                    act.sem_inc(act_goes, 1)
                    nc.scalar.activation(hT[HI][:, :, bass.ds(t * P, P)], slot[s][HI][:, :, :].bitcast(F32), ACT.Copy
                                         ).then_inc(kept_hi, 1)
                keep_high(0, 0)

                def step(h, s, one_more, two_more):
                    t = 2 * h + s
                    if one_more:
                        act.wait_ge(multiplied, t)
                        act.wait_ge(kept_hi, t)
                        act.wait_ge(kept_lo, t)
                        tk.high_part(nc.scalar, h + s, 1 - s)
                    if two_more:
                        tk.squares(nc.scalar, h + 1, s)
                    if one_more:
                        keep_high(h + s, 1 - s)
                    act.wait_ge(multiplied, t + 1)
                    act.wait_ge(v_stored[s], 16 * h)
                    nc.scalar.activation(vst[s][:, :, HI, :], mps[s][:, 0:V].rearrange("p (h c) -> p h c", c=DH),
                                         ACT.Copy).then_inc(v_hi, 1)
                steps(act, step)

            @block.vector
            def _(dve):
                def step(h, s, one_more, two_more):
                    t = 2 * h + s
                    if one_more:
                        tk.low_part(nc.vector, h + s, 1 - s)
                    if two_more:
                        tk.normalise(nc.vector, h + 1, s)
                    dve.wait_ge(v_hi, t + 1)
                    nc.vector.tensor_copy(fglr[:, bass.ds(t, 1), :].rearrange("p a c -> p (a c)"),
                                          mps[s][:, V:TOK_C])
                    nc.vector.tensor_tensor(vst[s][:, :, LO, :], mps[s][:, 0:V].rearrange("p (h c) -> p h c", c=DH),
                                            vst[s][:, :, HI, :].bitcast(F32), ALU.subtract).then_inc(v_lo, 1)
                steps(dve, step)

            @block.gpsimd
            def _(pool):
                def keep_low(h, s):
                    t = 2 * h + s
                    pool.wait_ge(tk.lo_done, 2 * t + 2)
                    pool.sem_inc(pool_goes, 1)
                    nc.gpsimd.tensor_copy(hT[LO][:, :, bass.ds(t * P, P)], slot[s][LO][:, :, :].bitcast(F32)
                                          ).then_inc(kept_lo, 1)
                keep_low(0, 0)

                def step(h, s, one_more, two_more):
                    if two_more:
                        tk.rstds(nc.gpsimd, h + 1, s)
                    if one_more:
                        keep_low(h + s, 1 - s)
                steps(pool, step)
                pool.wait_ge(kept_lo, TT)

            @block.tensor
            def _(pe):
                def step(h, s, one_more, _):
                    t = 2 * h + s
                    if one_more:
                        tk.transposes(nc.tensor, h + s, 1 - s)
                    pe.wait_ge(tk.lo_done, 2 * t + 2)
                    if isinstance(h, int) and h == 0:
                        pe.wait_ge(tk.w_lo, KT)
                    else:
                        pe.wait_ge(v_lo, t - 1)
                    for kk in range(KT):
                        for n, (a, b) in enumerate(PASSES):
                            mm = nc.tensor.matmul(mps[s][:, 0:TOK_C], slot[s][a][:, kk, :], w[b][:, kk, :],
                                                  start=(kk == 0 and n == 0), stop=(kk == KT - 1 and n == 2))
                    mm.then_inc(multiplied, 1)
                steps(pe, step)


def project_columns(nc, scr, ident, tk, hT, fglr, w_cols, b_forget):
    R = 8
    ctx = ExitStack()
    with ctx:
        k = Pools(nc, ctx, "col")
        w_raw = [tile[:, :].rearrange("p (k c) -> p k c", c=P) for tile in tk.xin]
        w = tk.slot
        both = [tile[:, :, :].rearrange("p k c -> p (k c)") for tile in tk.w]
        stage = [[both[i][:, T + CH * s:T + CH * (s + 1)] for i in (HI, LO)] for s in range(2)]
        plain = [tk.xn[:, CH * s:CH * (s + 1)] for s in range(2)]
        rT = k.sb("rT", [FGLR, T])
        f = rT[0:FOX_H, :]
        a = tk.raws[0:FOX_H, :]
        parts = [both[i][0:FOX_H, 0:T] for i in (HI, LO)]
        bf = k.sb("bf", [FOX_H, 1])
        cps = [k.ps(f"cps{c}", [P, CH]) for c in range(NCH)]
        rps = k.ps("rps", [P, T])
        (w_loaded0, w_loaded1, w_hi, w_lo, projected, hi_done, bank_free, gate_done, raw_done,
         stored0, stored1, rows_loaded, rows_t, rows_copied, act_rows, dve_rows, pool_rows, rows_stored, pool_goes) = map(
            k.sem, ("w_loaded0 w_loaded1 w_hi w_lo projected hi_done bank_free gate_done raw_done "
                    "stored0 stored1 rows_loaded rows_t rows_copied act_rows dve_rows pool_rows rows_stored pool_goes").split())
        w_loaded, stored = (w_loaded0, w_loaded1), (stored0, stored1)
        split_st = 16 * 2 * 2
        plain_st = 16 * 2
        base_plain = NSPLIT * split_st

        with nc.Block() as block:
            @block.sync
            def _(sp):
                sp.dma_start(w_raw[0][:, :, :], w_cols[0]).then_inc(w_loaded[0], 16)

                def load_next(j, s):
                    sp.wait_ge(w_lo, j)
                    sp.dma_start(w_raw[1 - s][:, :, :],
                                 w_cols[bass.ds(j + 1, 1)].rearrange("a p k c -> (a p) k c")
                                 ).then_inc(w_loaded[1 - s], 16)

                def store_split(j):
                    for c in range(NCH):
                        sp.wait_ge(bank_free, 4 * j + c + 5)
                        for i in (HI, LO):
                            dst = scr.split[bass.ds(j, 1), i, :, c * CH:(c + 1) * CH]
                            sp.dma_start(dst.rearrange("a p t -> (a p) t"), stage[c % 2][i][:, :].bitcast(F32)
                                         ).then_inc(stored[c % 2], 16)

                def store_plain(j, dst, first):
                    for c in range(NCH):
                        sp.wait_ge(bank_free, 4 * j + c + 5)
                        d = dst[bass.ds(j - first, 1), :, c * CH:(c + 1) * CH].rearrange("a p t -> (a p) t")
                        sp.dma_start(d, plain[c % 2][:, :]).then_inc(stored[c % 2], 16)

                with sp.Fori(0, NSPLIT // 2) as h:
                    for s in range(2):
                        load_next(2 * h + s, s)
                        store_split(2 * h + s)
                with sp.Fori(NSPLIT // 2, (NSPLIT + NGATE) // 2) as h:
                    for s in range(2):
                        load_next(2 * h + s, s)
                        store_plain(2 * h + s, scr.gates, NSPLIT)
                raw = scr.raw.rearrange("(a p) t -> a p t", p=P)
                with sp.Fori((NSPLIT + NGATE) // 2, NCOL // 2 - 1) as h:
                    for s in range(2):
                        load_next(2 * h + s, s)
                        store_plain(2 * h + s, raw, NSPLIT + NGATE)
                load_next(NCOL - 2, 0)
                store_plain(NCOL - 2, raw, NSPLIT + NGATE)
                store_plain(NCOL - 1, raw, NSPLIT + NGATE)
                for s in range(2):
                    sp.wait_ge(stored[s], base_plain + (NGATE + NRAW) * plain_st)

            @block.gpsimd
            def _(pool):
                pool.dma_start(bf[:, :], b_forget.rearrange("a h -> h a")).then_inc(rows_loaded, 16)

                def split(h, s):
                    j = 2 * h + s
                    pool.wait_ge(w_loaded[s], 16 * (h + 1))
                    pool.sem_inc(pool_goes, 1)
                    nc.gpsimd.tensor_copy(w[s][HI][:, :, :], w_raw[s][:, :, :]).then_inc(w_hi, 1)
                    pool.wait_ge(w_hi, j + 1)
                    nc.gpsimd.tensor_tensor(w[s][LO][:, :, :], w_raw[s][:, :, :], w[s][HI][:, :, :].bitcast(F32),
                                            ALU.subtract).then_inc(w_lo, 1)
                for s in range(2):
                    split(0, s)
                pool.wait_ge(rows_copied, 1)
                pool.dma_start(scr.lr, rT[FOX_H:FGLR, :]).then_inc(rows_stored, 16)
                pool.wait_ge(dve_rows, 4)
                nc.gpsimd.tensor_scalar(f, f, float(R), 1.0, ALU.mult, ALU.mult).then_inc(pool_rows, 1)
                pool.wait_ge(pool_rows, 1)
                nc.gpsimd.tensor_copy(parts[HI][:, :], f).then_inc(pool_rows, 1)
                pool.wait_ge(pool_rows, 2)
                nc.gpsimd.tensor_tensor(parts[LO][:, :], f, parts[HI][:, :].bitcast(F32), ALU.subtract
                                        ).then_inc(pool_rows, 1)
                pool.wait_ge(pool_rows, 3)
                for i in (HI, LO):
                    pool.dma_start(scr.crow[i], parts[i][:, :].bitcast(F32)).then_inc(rows_stored, 16)
                pool.wait_ge(rows_stored, 48)
                for i in (HI, LO):
                    nc.gpsimd.tensor_scalar(parts[i][:, :], parts[i][:, :].bitcast(F32), -1.0, 1.0,
                                            ALU.mult, ALU.mult).then_inc(pool_rows, 1)
                pool.wait_ge(pool_rows, 5)
                for i in (HI, LO):
                    pool.dma_start(scr.crow[2 + i], parts[i][:, :].bitcast(F32)).then_inc(rows_stored, 16)
                pool.wait_ge(rows_stored, 80)
                with pool.Fori(1, NCOL // 2) as h:
                    for s in range(2):
                        pool.wait_ge(projected, 4 * (2 * h + s - 1))
                        split(h, s)

            @block.tensor
            def _(pe):
                for t in range(TT):
                    mm = nc.tensor.transpose(rps[0:FGLR, t * P:(t + 1) * P], fglr[:, t, :], ident[:, :])
                mm.then_inc(rows_t, 1)
                with pe.Fori(0, NCOL // 2) as h:
                    for s in range(2):
                        j = 2 * h + s
                        pe.wait_ge(w_lo, j + 1)
                        for c in range(NCH):
                            pe.wait_ge(bank_free, 4 * j + c + 1)
                            for kk in range(KT):
                                for n, (a_, b_) in enumerate(PASSES):
                                    mm = nc.tensor.matmul(cps[c][:, :], w[s][a_][:, kk, :],
                                                          hT[b_][:, kk, c * CH:(c + 1) * CH],
                                                          start=(kk == 0 and n == 0), stop=(kk == KT - 1 and n == 2))
                            mm.then_inc(projected, 1)

            @block.scalar
            def _(act):
                act.wait_ge(rows_t, 1)
                nc.scalar.activation(rT[:, :], rps[0:FGLR, :], ACT.Copy).then_inc(rows_copied, 1)
                act.wait_ge(dve_rows, 1)
                nc.scalar.activation(a[:, :], f, ACT.Abs).then_inc(act_rows, 1)
                act.wait_ge(act_rows, 1)
                nc.scalar.activation(a[:, :], a[:, :], ACT.Exp, scale=-1.0).then_inc(act_rows, 1)
                act.wait_ge(act_rows, 2)
                nc.scalar.activation(a[:, :], a[:, :], ACT.Ln, bias=1.0).then_inc(act_rows, 1)

                with act.Fori(0, NSPLIT // 2) as h:
                    for s in range(2):
                        for c in range(NCH):
                            j = 2 * h + s
                            act.wait_ge(projected, 4 * j + c + 1)
                            act.wait_ge(stored[c % 2], j * split_st + (c // 2) * 32)
                            nc.scalar.activation(stage[c % 2][HI][:, :], cps[c][:, :], ACT.Copy).then_inc(hi_done, 1)
                act.wait_ge(bank_free, 4 * NSPLIT + 4)
                with act.Fori(NSPLIT // 2, (NSPLIT + NGATE) // 2) as h:
                    for s in range(2):
                        for c in range(NCH):
                            j = 2 * h + s
                            act.wait_ge(projected, 4 * j + c + 1)
                            act.wait_ge(stored[c % 2], base_plain + (j - NSPLIT) * plain_st + (c // 2) * 16)
                            nc.scalar.activation(plain[c % 2][:, :], cps[c][:, :], ACT.Silu).then_inc(bank_free, 1)

            @block.vector
            def _(dve):
                dve.sem_inc(bank_free, 4)
                dve.wait_ge(rows_copied, 1)
                dve.wait_ge(rows_loaded, 16)
                nc.vector.tensor_scalar(f, rT[0:FOX_H, :], bf[:, 0:1], None, ALU.add).then_inc(dve_rows, 1)
                dve.wait_ge(dve_rows, 1)
                dve.wait_ge(act_rows, 3)
                nc.vector.scalar_tensor_tensor(f, f, 0.0, a[:, :], ALU.min, ALU.subtract
                                               ).then_inc(dve_rows, 1)
                dve.wait_ge(dve_rows, 2)
                nc.vector.memset(a[:, :], -3e38).then_inc(dve_rows, 1)
                dve.wait_ge(dve_rows, 3)
                nc.vector.tensor_tensor_scan(f, f, a[:, :], 0.0, ALU.add, ALU.max).then_inc(dve_rows, 1)
                with dve.Fori(0, NSPLIT // 2) as h:
                    for s in range(2):
                        for c in range(NCH):
                            j = 2 * h + s
                            dve.wait_ge(hi_done, 4 * j + c + 1)
                            nc.vector.tensor_tensor(stage[c % 2][LO][:, :], cps[c][:, :],
                                                    stage[c % 2][HI][:, :].bitcast(F32), ALU.subtract
                                                    ).then_inc(bank_free, 1)
                dve.wait_ge(bank_free, 4 * (NSPLIT + NGATE) + 4)
                with dve.Fori((NSPLIT + NGATE) // 2, NCOL // 2) as h:
                    for s in range(2):
                        for c in range(NCH):
                            j = 2 * h + s
                            dve.wait_ge(projected, 4 * j + c + 1)
                            dve.wait_ge(stored[c % 2], base_plain + (j - NSPLIT) * plain_st + (c // 2) * 16)
                            nc.vector.tensor_copy(plain[c % 2][:, :], cps[c][:, :]).then_inc(bank_free, 1)




def gated_linear_attention(nc, scr, ident, gla_mask, w_alpha_up, b_alpha, gla_norm_g):
    NG, GT = T // CH, CH
    NS = T // P
    ST = CH // P
    HB = 64
    KR = HB + GLA_DK
    W2 = 2 * GLA_DV
    GV = GLA_H * GLA_DV
    RING = 6
    PAIRS = 2
    QKW = GLA_H * GLA_DK
    ctx = ExitStack()
    with ctx:
        k = Pools(nc, ctx, "gla")
        pair_tiles = lambda name, shape, dt=F32: [[k.sb(f"{name}{s}{p}", shape, dt) for p in range(PAIRS)]
                                                  for s in range(2)]
        q, kk = pair_tiles("q", [KR, GT]), pair_tiles("k", [KR, GT])
        qd, kd, kte = (pair_tiles(n, [KR, GT]) for n in ("qd", "kd", "kte"))
        qpad = pair_tiles("qpad", [KR, 2, GT])
        dec = pair_tiles("dec", [KR, GT // GLA_C])
        v = [k.sb(f"v{s}", [GLA_DV, GLA_H, GT]) for s in range(2)]
        lr = [k.sb(f"lr{s}", [GLA_R, GT]) for s in range(2)]
        gate = [k.sb(f"gate{s}", [P, 3, GT]) for s in range(2)]
        keep = k.sb("keep", [KR, GT])
        zabs, la, b, tail, ep, em, ee = (k.sb(n, [KR, GT]) for n in "zabs la b tail ep em ee".split())
        wup = [k.sb(f"wup{p}", [GLA_R, KR]) for p in range(PAIRS)]
        bup = [k.sb(f"bup{p}", [KR, 1]) for p in range(PAIRS)]
        gn = k.sb("gn", [P, 3])
        vt = [k.sb(f"vt{s}", [P, GV]) for s in range(2)]
        vz = k.sb("vz", [P, 2, GV])
        kt = k.sb("kt", [P, PAIRS * KR])
        am = [k.sb(f"am{s}", [P, GLA_H * P]) for s in range(2)]
        S = [[k.sb(f"S{r}{p}", [KR, W2]) for p in range(PAIRS)] for r in range(RING)]
        sqj = k.sb("sqj", [P, GLA_DV])
        ss, ms, rstd, half = (k.sb(n, [P, GLA_H]) for n in ("ss", "ms", "rstd", "half"))
        on = [k.sb(f"on{s}", [P, GV]) for s in range(2)]
        mx, zero = k.sb("mx", [P, 3, P]), k.sb("zero", [P, 3, P])
        mst = [[k.sb(f"mst{s}{i}", [P, 3, P], F32R) for i in (HI, LO)] for s in range(2)]
        zps = k.ps("zps", [P, CH])
        vps = k.ps("vps", [P, CH])
        kps = k.ps("kps", [P, CH])
        aps = k.ps("aps", [P, CH])
        kvps = [k.ps(f"kvps{p}", [P, CH]) for p in range(PAIRS)]
        ops = k.ps("ops", [P, CH])
        otps = k.ps("otps", [P, CH])
        (k_decayed, qpad_done, pads, w_loaded, cleared, qk_loaded0, qk_loaded1, v_loaded0, v_loaded1, gate_loaded0, gate_loaded1, z_done, abs_done,
         min_done, exp_done, ln_done, la_done, scan_done, ep_done, em_done, tail_done, ee_done, qd_done, prep_done,
         gate_ready) = map(
            k.sem, ("k_decayed qpad_done pads w_loaded cleared qk_loaded0 qk_loaded1 v_loaded0 v_loaded1 gate_loaded0 gate_loaded1 z_done "
                    "abs_done min_done exp_done ln_done la_done scan_done ep_done em_done tail_done ee_done qd_done "
                    "prep_done gate_ready").split())
        (vT_done, kT_done, attn_done, kv_done, o_done, oT_done, v_copied, k_copied, masked, state_done, squared,
         ms_done, rstd_done, on_done, mixed, mix_hi, mix_lo, stored0, stored1) = map(
            k.sem, ("vT_done kT_done attn_done kv_done o_done oT_done v_copied k_copied masked state_done squared "
                    "ms_done rstd_done on_done mixed mix_hi mix_lo stored0 stored1").split())
        qk_loaded, v_loaded, gate_loaded = (qk_loaded0, qk_loaded1), (v_loaded0, v_loaded1), (gate_loaded0, gate_loaded1)
        stored = (stored0, stored1)
        QK_DMAS = 16 * (4 * PAIRS + 1)

        def pieces(g, n):
            if g + 1 < NG:
                for piece in ((0,), (1, 2), (3,), ())[n]:
                    yield g + 1, piece // 2, piece % 2

        def first_pieces():
            for p in range(PAIRS):
                for part in range(2):
                    yield 0, p, part

        with nc.Block() as block:
            @block.sync
            def _(sp):
                sp.wait_ge(pads, 2 * PAIRS)
                for p in range(PAIRS):
                    for e in range(2):
                        c = (2 * p + e) * GLA_DK
                        sp.dma_start(wup[p][:, HB * e:HB * e + GLA_DK], w_alpha_up[0, :, c:c + GLA_DK]
                                     ).then_inc(w_loaded, 16)
                ch = 0
                while ch < GV:
                    n = min(P - ch % P, GLA_DV - ch % GLA_DV)
                    sp.dma_start(gn[ch % P:ch % P + n, ch // P:ch // P + 1],
                                 gla_norm_g[0:1, ch % GLA_DV:ch % GLA_DV + n].rearrange("a n -> n a")
                                 ).then_inc(w_loaded, 16)
                    ch += n

                def load_qk(g):
                    s, cols = g % 2, slice(g * GT, (g + 1) * GT)
                    if g == 0:
                        sp.wait_ge(cleared, 8)
                    if g >= 2:
                        sp.wait_ge(prep_done, PAIRS * (g - 1))
                    for p in range(PAIRS):
                        for e in range(2):
                            r = (2 * p + e) * GLA_DK
                            rows = slice(HB * e, HB * e + GLA_DK)
                            sp.dma_start(q[s][p][rows, :], scr.raw[r:r + GLA_DK, cols]).then_inc(qk_loaded[s], 16)
                            sp.dma_start(kk[s][p][rows, :], scr.raw[QKW + r:QKW + r + GLA_DK, cols]
                                         ).then_inc(qk_loaded[s], 16)
                    sp.dma_start(lr[s][:, :], scr.lr[:, cols]).then_inc(qk_loaded[s], 16)

                def load_v(g):
                    s, cols = g % 2, slice(g * GT, (g + 1) * GT)
                    if g >= 2:
                        sp.wait_ge(vT_done, ST * (g - 1))
                    sp.dma_start(v[s][:, :, :], scr.raw[2 * QKW:2 * QKW + GV, cols].rearrange("(h d) t -> d h t", d=GLA_DV)
                                 ).then_inc(v_loaded[s], 16)

                def load_gate(g):
                    s, cols = g % 2, slice(g * GT, (g + 1) * GT)
                    if g >= 2:
                        sp.wait_ge(mixed, ST * (g - 1))
                    sp.dma_start(gate[s][:, :, :], scr.gates[0:3, :, cols].rearrange("j p t -> p j t")
                                 ).then_inc(gate_loaded[s], 16)

                def store(N):
                    sp.wait_ge(mix_lo, N + 1)
                    for i in (HI, LO):
                        sp.dma_start(scr.mix[i, N, :, 0:3, :], mst[N % 2][i][:, :, :].bitcast(F32)
                                     ).then_inc(stored[N % 2], 16)
                for g in range(2):
                    load_qk(g)
                    load_v(g)
                    load_gate(g)
                for g in range(NG):
                    for n in range(ST):
                        if g * ST + n >= 2:
                            store(g * ST + n - 2)
                        if n == 0 and g + 2 < NG:
                            load_qk(g + 2)
                        if n == 0 and 2 <= g + 1 < NG:
                            load_v(g + 1)
                        if n == 2 and 2 <= g + 1 < NG:
                            load_gate(g + 1)
                store(NS - 2)
                store(NS - 1)
                for s in range(2):
                    sp.wait_ge(stored[s], 16 * NS)

            @block.tensor
            def _(pe):
                def prep(g, p, part):
                    u = PAIRS * g + p
                    if part:
                        return
                    if p == 0:
                        pe.wait_ge(qk_loaded[g % 2], QK_DMAS * (g // 2 + 1))
                    if u:
                        pe.wait_ge(min_done, u)
                        pe.wait_ge(abs_done, u)
                    nc.tensor.matmul(zps[0:KR, :], wup[p][:, :], lr[g % 2][:, :], start=True, stop=True
                                     ).then_inc(z_done, 1)
                pe.wait_ge(cleared, 10)
                pe.wait_ge(w_loaded, 16 * 14)
                for x in first_pieces():
                    prep(*x)

                def outputs(N):
                    s, c0 = (N // ST) % 2, (N % ST) * P
                    if N:
                        pe.wait_ge(on_done, N)
                    pe.wait_ge(masked, N + 1)
                    for p in range(PAIRS):
                        o = ops[:, p * W2:(p + 1) * W2]
                        for e in range(2):
                            m = 2 * N + e
                            if m:
                                pe.wait_ge(state_done, 2 * PAIRS * (m - 1) + 2 * p + 2)
                            nc.tensor.matmul(o[GLA_C * e:GLA_C * (e + 1), :],
                                             qd[s][p][:, c0 + GLA_C * e:c0 + GLA_C * (e + 1)], S[m % RING][p][:, :],
                                             start=True, stop=False, skip_group_check=True)
                        for e in range(2):
                            h = 2 * p + e
                            mm = nc.tensor.matmul(o[:, e * GLA_DV:(e + 1) * GLA_DV], am[N % 2][:, h * P:(h + 1) * P],
                                                  vt[N % 2][:, h * GLA_DV:(h + 1) * GLA_DV],
                                                  start=False, stop=True, skip_group_check=True)
                    mm.then_inc(o_done, 1)

                def transposed_outputs(N):
                    pe.wait_ge(on_done, N + 1)
                    if N:
                        pe.wait_ge(mixed, N)
                    for j in range(3):
                        mm = nc.tensor.transpose(otps[:, j * P:(j + 1) * P], on[N % 2][:, j * P:(j + 1) * P], ident[:, :])
                    mm.then_inc(oT_done, 1)

                for g in range(NG):
                    s = g % 2
                    for n in range(ST):
                        N, cols = g * ST + n, slice(n * P, (n + 1) * P)
                        if n == 0:
                            pe.wait_ge(v_loaded[s], 16 * (g // 2 + 1))
                            pe.wait_ge(prep_done, PAIRS * (g + 1))
                        if N:
                            pe.wait_ge(v_copied, 3 * N)
                        for h in range(GLA_H):
                            mm = nc.tensor.transpose(vps[:, h * GLA_DV:(h + 1) * GLA_DV], v[s][:, h, cols],
                                                     ident[0:GLA_DV, 0:GLA_DV])
                        mm.then_inc(vT_done, 1)
                        if N:
                            pe.wait_ge(k_copied, N)
                        for p in range(PAIRS):
                            mm = nc.tensor.transpose(kps[:, p * KR:(p + 1) * KR], kte[s][p][:, cols], ident[0:KR, 0:KR])
                        mm.then_inc(kT_done, 1)
                        if N:
                            pe.wait_ge(masked, N)
                        for p in range(PAIRS):
                            mm = nc.tensor.matmul(aps[:, p * 2 * P:(p + 1) * 2 * P], kd[s][p][:, cols],
                                                  qpad[s][p][:, :, cols], start=True, stop=True)
                        mm.then_inc(attn_done, 1)
                        if N:
                            outputs(N - 1)
                        pe.wait_ge(v_copied, 3 * (N + 1))
                        pe.wait_ge(k_copied, N + 1)
                        for p in range(PAIRS):
                            if N:
                                pe.wait_ge(state_done, 4 * PAIRS * (N - 1) + 2 * PAIRS + 2 * p + 2)
                            nc.tensor.matmul(kvps[p][0:KR, 0:2 * W2], kt[:, p * KR:(p + 1) * KR],
                                             vz[:, :, p * W2:(p + 1) * W2], start=True, stop=True
                                             ).then_inc(kv_done, 1)
                        if N >= 2:
                            transposed_outputs(N - 2)
                        for x in pieces(g, n):
                            prep(*x)
                outputs(NS - 1)
                transposed_outputs(NS - 2)
                transposed_outputs(NS - 1)

            @block.scalar
            def _(act):
                def prep(g, p, part):
                    u = PAIRS * g + p
                    if part == 0:
                        act.wait_ge(z_done, u + 1)
                        if u:
                            act.wait_ge(la_done, u)
                        nc.scalar.activation(zabs[:, :], zps[0:KR, :], ACT.Abs, bias=bup[p][:, 0:1]).then_inc(abs_done, 1)
                        act.wait_ge(abs_done, u + 1)
                        nc.scalar.activation(zabs[:, :], zabs[:, :], ACT.Exp, scale=-1.0).then_inc(exp_done, 1)
                        act.wait_ge(exp_done, u + 1)
                        nc.scalar.activation(zabs[:, :], zabs[:, :], ACT.Ln, bias=1.0).then_inc(ln_done, 1)
                    else:
                        act.wait_ge(scan_done, u + 1)
                        if u:
                            act.wait_ge(prep_done, u)
                        gs = 1.0 / GLA_GATE
                        nc.scalar.activation(ep[:, :], b[:, :], ACT.Exp, scale=gs).then_inc(ep_done, 1)
                        nc.scalar.activation(em[:, :], b[:, :], ACT.Exp, scale=-gs).then_inc(em_done, 1)
                        act.wait_ge(tail_done, u + 1)
                        nc.scalar.activation(ee[:, :], tail[:, :], ACT.Exp, scale=gs).then_inc(ee_done, 1)
                act.wait_ge(pads, 2 * PAIRS)
                for p in range(PAIRS):
                    for e in range(2):
                        c = (2 * p + e) * GLA_DK
                        act.dma_start(bup[p][HB * e:HB * e + GLA_DK, :],
                                      b_alpha[0:1, c:c + GLA_DK].rearrange("a n -> n a")).then_inc(w_loaded, 16)
                act.wait_ge(w_loaded, 16 * 14)
                act.wait_ge(cleared, 10)
                for x in first_pieces():
                    prep(*x)

                def squares(N):
                    act.wait_ge(o_done, N + 1)
                    if N:
                        act.wait_ge(ms_done, N)
                    for h in range(GLA_H):
                        nc.scalar.activation(sqj[:, :], ops[:, h * GLA_DV:(h + 1) * GLA_DV], ACT.Square,
                                             accum_out=ss[:, h:h + 1]).then_inc(squared, 1)
                        act.wait_ge(squared, GLA_H * N + h + 1)

                for g in range(NG):
                    for n in range(ST):
                        N = g * ST + n
                        act.wait_ge(vT_done, N + 1)
                        if N >= 2:
                            act.wait_ge(o_done, N - 1)
                        nc.scalar.activation(vt[N % 2][:, :], vps[:, 0:GV], ACT.Copy).then_inc(v_copied, 1)
                        if N:
                            act.wait_ge(kv_done, PAIRS * N)
                        for e in range(2):
                            rows = slice(GLA_C * e, GLA_C * (e + 1))
                            nc.scalar.activation(vz[rows, e, :], vps[rows, 0:GV], ACT.Copy).then_inc(v_copied, 1)
                        act.wait_ge(kT_done, N + 1)
                        nc.scalar.activation(kt[:, :], kps[:, 0:PAIRS * KR], ACT.Copy).then_inc(k_copied, 1)
                        if N:
                            squares(N - 1)
                        for x in pieces(g, n):
                            prep(*x)
                squares(NS - 1)

            @block.vector
            def _(dve):
                def prep(g, p, part):
                    u, s = PAIRS * g + p, g % 2
                    if part == 0:
                        dve.wait_ge(z_done, u + 1)
                        dve.wait_ge(abs_done, u + 1)
                        if u:
                            dve.wait_ge(scan_done, u)
                        nc.vector.tensor_scalar(la[:, :], zps[0:KR, :], bup[p][:, 0:1], 0.0, ALU.add, ALU.min
                                                ).then_inc(min_done, 1)
                        dve.wait_ge(min_done, u + 1)
                        dve.wait_ge(ln_done, u + 1)
                        nc.vector.tensor_tensor(la[:, :], la[:, :], zabs[:, :], ALU.subtract).then_inc(la_done, 1)
                        dve.wait_ge(la_done, u + 1)
                        if u:
                            dve.wait_ge(em_done, u)
                            dve.wait_ge(tail_done, u)
                        nc.vector.tensor_tensor_scan(b[:, :], keep[:, :], la[:, :], 0.0, ALU.mult, ALU.add
                                                     ).then_inc(scan_done, 1)
                        dve.wait_ge(scan_done, u + 1)
                        if u:
                            dve.wait_ge(ee_done, u)
                        bc = b[:, :].rearrange("p (n c) -> p n c", c=GLA_C)
                        nc.vector.tensor_tensor(tail[:, :].rearrange("p (n c) -> p n c", c=GLA_C),
                                                bc[:, :, GLA_C - 1:GLA_C].to_broadcast([KR, GT // GLA_C, GLA_C]), bc,
                                                ALU.subtract).then_inc(tail_done, 1)
                    else:
                        dve.wait_ge(ep_done, u + 1)
                        if g >= 2:
                            dve.wait_ge(o_done, ST * (g - 1))
                            dve.wait_ge(attn_done, ST * (g - 1))
                        nc.vector.scalar_tensor_tensor(qd[s][p][:, :], q[s][p][:, :], GLA_DK ** -0.5, ep[:, :],
                                                       ALU.mult, ALU.mult).then_inc(qd_done, 1)
                        dve.wait_ge(qd_done, u + 1)
                        for e in range(2):
                            rows = slice(HB * e, HB * e + GLA_DK)
                            nc.vector.tensor_copy(qpad[s][p][rows, e, :], qd[s][p][rows, :]).then_inc(qpad_done, 1)
                dve.wait_ge(cleared, 10)
                dve.wait_ge(w_loaded, 16 * 14)
                dve.wait_ge(qk_loaded[0], QK_DMAS)
                for x in first_pieces():
                    prep(*x)

                def normed(N):
                    dve.wait_ge(squared, GLA_H * (N + 1))
                    nc.vector.tensor_scalar(ms[:, :], ss[:, :], 1.0 / GLA_DV, EPS, ALU.mult, ALU.add).then_inc(ms_done, 1)
                    dve.wait_ge(rstd_done, N + 1)
                    if N >= 2:
                        dve.wait_ge(oT_done, N - 1)
                    nc.vector.tensor_tensor(on[N % 2][:, :].rearrange("p (h d) -> p h d", d=GLA_DV),
                                            ops[:, 0:GV].rearrange("p (h d) -> p h d", d=GLA_DV),
                                            rstd[:, :].unsqueeze(2).to_broadcast([P, GLA_H, GLA_DV]), ALU.mult
                                            ).then_inc(on_done, 1)

                def gated(N):
                    g, c0 = N // ST, (N % ST) * P
                    dve.wait_ge(oT_done, N + 1)
                    dve.wait_ge(gate_ready, 3 * (g + 1))
                    if N:
                        dve.wait_ge(mix_lo, N)
                    nc.vector.tensor_tensor(mx[:, :, :], otps[:, 0:3 * P].rearrange("p (j t) -> p j t", t=P),
                                            gate[g % 2][:, :, c0:c0 + P], ALU.mult).then_inc(mixed, 1)

                for g in range(NG):
                    s = g % 2
                    if g + 1 < NG:
                        dve.wait_ge(qk_loaded[(g + 1) % 2], QK_DMAS * ((g + 1) // 2 + 1))
                    for n in range(ST):
                        N = g * ST + n
                        dve.wait_ge(attn_done, N + 1)
                        if N >= 2:
                            dve.wait_ge(o_done, N - 1)
                        nc.vector.tensor_tensor(am[N % 2][:, :], aps[:, :], gla_mask[:, :, :].rearrange("p h t -> p (h t)"),
                                                ALU.mult).then_inc(masked, 1)
                        if N:
                            normed(N - 1)
                        if n == 0:
                            dve.wait_ge(prep_done, PAIRS * (g + 1))
                        for e in range(2):
                            m = 2 * N + e
                            for p in range(PAIRS):
                                if e == 0:
                                    dve.wait_ge(kv_done, PAIRS * N + p + 1)
                                if m:
                                    dve.wait_ge(state_done, 2 * PAIRS * (m - 1) + 2 * p + 2)
                                for a in range(2):
                                    rows = slice(HB * a, HB * a + GLA_DK)
                                    cols = slice(a * GLA_DV, (a + 1) * GLA_DV)
                                    nc.vector.scalar_tensor_tensor(
                                        S[(m + 1) % RING][p][rows, cols], S[m % RING][p][rows, cols],
                                        dec[s][p][rows, 2 * n + e:2 * n + e + 1],
                                        kvps[p][rows, e * W2 + a * GLA_DV:e * W2 + (a + 1) * GLA_DV],
                                        ALU.mult, ALU.add).then_inc(state_done, 1)
                        if N >= 2:
                            gated(N - 2)
                        for x in pieces(g, n):
                            prep(*x)
                normed(NS - 1)
                gated(NS - 2)
                gated(NS - 1)

            @block.gpsimd
            def _(pool):
                for p in range(PAIRS):
                    pool.memset(wup[p][:, :], 0.0).then_inc(pads, 1)
                    pool.memset(bup[p][:, :], 0.0).then_inc(pads, 1)
                for s in range(2):
                    for p in range(PAIRS):
                        pool.memset(q[s][p][:, :], 0.0).then_inc(cleared, 1)
                        pool.memset(kk[s][p][:, :], 0.0).then_inc(cleared, 1)
                for p in range(PAIRS):
                    pool.memset(qpad[0][p][:, :, :], 0.0)
                    pool.memset(qpad[1][p][:, :, :], 0.0)
                    for r in range(RING):
                        pool.memset(S[r][p][:, :], 0.0)
                pool.memset(vz[:, :, :], 0.0)
                pool.memset(zero[:, :, :], 0.0)
                pool.memset(half[:, :], -0.5)
                pool.memset(keep[:, :], 1.0).then_inc(cleared, 1)
                pool.wait_ge(cleared, 9)
                pool.memset(keep[:, :].rearrange("p (n c) -> p n c", c=GLA_C)[:, :, 0:1], 0.0).then_inc(cleared, 1)
                pool.wait_ge(cleared, 10)

                def prep(g, p, part):
                    u, s = PAIRS * g + p, g % 2
                    if part == 0:
                        return
                    if p == 0:
                        pool.wait_ge(qk_loaded[s], QK_DMAS * (g // 2 + 1))
                    if g >= 2:
                        pool.wait_ge(attn_done, ST * (g - 1))
                        pool.wait_ge(kT_done, ST * (g - 1))
                        pool.wait_ge(state_done, 4 * PAIRS * ST * (g - 1))
                    pool.wait_ge(em_done, u + 1)
                    nc.gpsimd.tensor_tensor(kd[s][p][:, :], kk[s][p][:, :], em[:, :], ALU.mult).then_inc(k_decayed, 1)
                    pool.wait_ge(ee_done, u + 1)
                    nc.gpsimd.tensor_tensor(kte[s][p][:, :], kk[s][p][:, :], ee[:, :], ALU.mult).then_inc(k_decayed, 1)
                    pool.wait_ge(k_decayed, 2 * u + 2)
                    pool.wait_ge(qpad_done, 2 * u + 2)
                    nc.gpsimd.tensor_copy(dec[s][p][:, :].unsqueeze(2),
                                          ep[:, :].rearrange("p (n c) -> p n c", c=GLA_C)[:, :, GLA_C - 1:GLA_C]
                                          ).then_inc(prep_done, 1)

                def gates(g):
                    s = g % 2
                    pool.wait_ge(w_loaded, 16 * 14)
                    pool.wait_ge(gate_loaded[s], 16 * (g // 2 + 1))
                    for j in range(3):
                        nc.gpsimd.tensor_scalar(gate[s][:, j, :], gate[s][:, j, :], gn[:, j:j + 1], 1.0,
                                                ALU.mult, ALU.mult).then_inc(gate_ready, 1)
                for x in first_pieces():
                    prep(*x)
                gates(0)

                def rstds(N):
                    pool.wait_ge(ms_done, N + 1)
                    if N:
                        pool.wait_ge(on_done, N)
                    nc.gpsimd.tensor_tensor(rstd[:, :], ms[:, :], half[:, :], ALU.pow).then_inc(rstd_done, 1)

                def split(N):
                    pool.wait_ge(mixed, N + 1)
                    if N >= 2:
                        pool.wait_ge(stored[N % 2], 32 * (N // 2))
                    nc.gpsimd.tensor_tensor(mst[N % 2][HI][:, :, :], mx[:, :, :], zero[:, :, :], ALU.add
                                            ).then_inc(mix_hi, 1)
                    pool.wait_ge(mix_hi, N + 1)
                    nc.gpsimd.tensor_tensor(mst[N % 2][LO][:, :, :], mx[:, :, :], mst[N % 2][HI][:, :, :].bitcast(F32),
                                            ALU.subtract).then_inc(mix_lo, 1)
                for g in range(NG):
                    for n in range(ST):
                        N = g * ST + n
                        if N:
                            rstds(N - 1)
                        if N >= 2:
                            split(N - 2)
                        if n == 3 and g + 1 < NG:
                            gates(g + 1)
                        for x in pieces(g, n):
                            prep(*x)
                rstds(NS - 1)
                split(NS - 2)
                split(NS - 1)


class Ring:

    def __init__(self, it, per):
        self.it, self.per = it, per

    def at(self, n):
        return self.it * self.per + n


def softmax_attention(nc, scr, ident, ident_b, mask, fox):
    tag = "fox" if fox else "att"
    W = T if fox else M
    NB = W // P
    NG = T // CH
    ROUNDS = (FOX_H if fox else MEM_H) // 2
    SCALE = DH ** -0.5
    QT = CH // P
    PT = 4
    DEPTH = PT - 1 if fox else PT - 2
    AUX = DH

    def score_units(hd, g):
        for i in range(CH // P):
            if fox:
                for c in range(g + 1):
                    yield hd, g, i, c, CH if c < g else P * (i + 1)
            else:
                yield hd, g, i, 0, W

    def key_units(hd, g):
        for j in range(4 * (g + 1) if fox else NB):
            yield hd, g, j, max(0, j - 4 * g) if fox else 0

    turns = [(0, g) for g in range(NG)] + [(1, g) for g in reversed(range(NG))]
    keys_of = lambda g: CH * (g + 1) if fox else W
    ctx = ExitStack()
    with ctx:
        k = Pools(nc, ctx, tag)
        qa = [k.sb(f"qa{e}", [P, T], F32R) for e in range(2)]
        qb = [k.sb(f"qb{e}", [P, T], F32R) for e in range(2)] if fox else qa
        ka, kb = ([k.sb(f"{n}{e}", [P, W], F32R) for e in range(2)] for n in ("ka", "kb"))
        v = [k.sb(f"v{e}", [P, NB, 2 * DH], F32R) for e in range(2)]
        prob = [k.sb(f"prob{b}", [P, QT, W]) for b in range(2)]
        pT = [[k.sb(f"pT{b}{i}", [P, CH], F32R) for i in (HI, LO)] for b in range(PT)]
        nmax = [k.sb(f"nmax{b}", [P, CH // P, 4]) for b in range(2)]
        nm = [k.sb(f"nm{b}", [P, CH // P]) for b in range(2)]
        rsum = [k.sb(f"rsum{b}", [P, CH // P]) for b in range(2)]
        rinv = [k.sb(f"rinv{b}", [P, CH // P]) for b in range(2)]
        gate = [k.sb(f"gate{b}", [DH, CH]) for b in range(2)]
        low, o1 = k.sb("low", [DH, CH]), k.sb("o1", [DH, CH])
        o2 = [k.sb(f"o2{b}", [DH, CH]) for b in range(2)]
        zero = k.sb("zero", [DH, CH])
        om = [[k.sb(f"om{b}{i}", [DH, CH], F32R) for i in (HI, LO)] for b in range(2)]
        sps = [k.ps(f"sps{b}", [P, CH]) for b in range(2)]
        tps = [k.ps(f"tps{b}", [P, CH]) for b in range(3)]
        ops = [k.ps(f"ops{b}", [P, CH]) for b in range(2)]
        rps = k.ps("rps", [P, CH])
        names = ("zeroed0 zeroed1 filled0 filled1 piece_loaded0 piece_loaded1 piece_loaded2 piece_loaded3 second_loaded "
                 "gate_loaded0 gate_loaded1 scored negated maxed expd transposed pt_hi pt_lo "
                 "weighed inverted spread low_done added scaled gated o_hi o_lo stored0 stored1 sp_goes").split()
        (zeroed0, zeroed1, filled0, filled1, piece_loaded0, piece_loaded1, piece_loaded2, piece_loaded3, second_loaded,
         gate_loaded0, gate_loaded1, scored, negated, maxed, expd, transposed, pt_hi, pt_lo,
         weighed, inverted, spread, low_done, added, scaled, gated, o_hi, o_lo, stored0, stored1, sp_goes) = map(k.sem, names)
        gate_loaded, stored = (gate_loaded0, gate_loaded1), (stored0, stored1)
        zeroed, filled = (zeroed0, zeroed1), (filled0, filled1)
        FILLS = 2 if fox else 1
        piece_loaded = (piece_loaded0, piece_loaded1, piece_loaded2, piece_loaded3)

        n_scores = sum(len(list(score_units(*t))) for t in turns)
        n_keys = sum(len(list(key_units(*t))) for t in turns)
        n_turns = len(turns)
        def loads_of(g):
            return 9 if fox else 6 if g == 0 else 2
        LOADS = sum(map(loads_of, range(NG)))

        def at_turn(t):
            return (sum(len(list(score_units(*x))) for x in turns[:t]),
                    sum(len(list(key_units(*x))) for x in turns[:t]))

        def plan(t, last):
            units = list(key_units(*turns[t]))
            ahead = [] if last and t + 1 == n_turns else list(score_units(*turns[(t + 1) % n_turns]))
            done, tiles, out = 0, 0, []
            for m in range(len(units)):
                upto = min(len(ahead), -(-len(ahead) * (m + 1) * 4 // (3 * len(units))))
                ready = (done if fox and m + 1 < len(units) else upto) * QT // len(ahead) if ahead else 0
                out.append((units[m], list(range(done, upto)), list(range(tiles, ready))))
                done, tiles = upto, ready
            return ahead, out

        def fill(eng, e):
            low = slice(AUX, P)
            if fox:
                eng.memset(kb[e][low, :].bitcast(F32), 0.0).then_inc(zeroed[e], 1)
                eng.memset(qb[e][low, :].bitcast(F32), 1.0).then_inc(filled[e], 1)
                eng.wait_ge(zeroed[e], 1 + e)
                eng.memset(kb[e][AUX:AUX + 4, :].bitcast(F32), 1.0).then_inc(filled[e], 1)
            else:
                eng.memset(kb[e][low, :].bitcast(F32), 0.0).then_inc(filled[e], 1)

        def ends(t, m):
            return t >= 1 and m == (3 if fox else 1)

        def rounds(eng, round_):
            with eng.Fori(0, ROUNDS - 1) as r:
                round_(r, False)
            round_(ROUNDS - 1, True)

        with nc.Block() as block:
            @block.sync
            def _(sp):

                def load_head(r, e):
                    qt = r + (0 if fox else 3)
                    rows = slice(DH * e, DH * (e + 1))
                    top, bottom = slice(0, DH), slice(DH, P)
                    for g in range(NG):
                        cols = slice(CH * g, CH * (g + 1))

                        def part(tile, i):
                            return scr.split[bass.ds(tile, 1), i, rows, cols].rearrange("a p t -> (a p) t")
                        loads = [(qa[e][top, cols], part(qt, HI)), (qa[e][bottom, cols], part(qt, LO))]
                        if fox:
                            head, blocks = bass.ds(2 * r + e, 1), slice(4 * g, 4 * g + 4)
                            loads += [(ka[e][top, cols], part(r + 5, LO)), (ka[e][bottom, cols], part(r + 5, HI)),
                                      (qb[e][top, cols], part(qt, HI)), (kb[e][top, cols], part(r + 5, HI)),
                                      (qb[e][AUX + 2:AUX + 4, cols],
                                       scr.crow[0:2, head, cols].rearrange("i a t -> (i a) t")),
                                      (kb[e][AUX:AUX + 2, cols],
                                       scr.crow[2:4, head, cols].rearrange("i a t -> (i a) t")),
                                      (v[e][:, blocks, :],
                                       scr.fox_v[head, :, blocks, :].rearrange("a p b c -> (a p) b c"))]
                        elif g == 0:
                            def key(i):
                                return scr.mem_k[bass.ds(r, 1), i, rows, :].rearrange("a p t -> (a p) t")
                            loads += [(ka[e][top, :], key(LO)), (ka[e][bottom, :], key(HI)), (kb[e][top, :], key(HI)),
                                      (v[e][:, :, :],
                                       scr.mem_v[bass.ds(2 * r + e, 1)].rearrange("a p b c -> (a p) b c"))]
                        for dst, src in loads:
                            sp.dma_start(dst.bitcast(F32), src).then_inc(second_loaded if e else piece_loaded[g], 16)

                def load_gate(r, t):
                    e, g = turns[t]
                    src = scr.gates[bass.ds(r + (3 if fox else 6), 1), DH * e:DH * (e + 1), g * CH:(g + 1) * CH]
                    sp.dma_start(gate[t % 2][:, :], src.rearrange("a p t -> (a p) t")).then_inc(gate_loaded[t % 2], 16)
                sp.wait_ge(filled[0], FILLS)
                load_head(0, 0)
                load_gate(0, 0)
                load_gate(0, 1)
                sp.wait_ge(filled[1], FILLS)
                load_head(0, 1)

                def round_(r, last):
                    for t, (e, g) in enumerate(turns):
                        sp.wait_ge(o_lo, r * n_turns + t + 1)
                        sp.sem_inc(sp_goes, 1)
                        for i in (HI, LO):
                            dst = scr.mix[i, 4 * g:4 * g + 4, DH * e:DH * (e + 1), bass.ds(r + (3 if fox else 6), 1), :]
                            sp.dma_start(dst.rearrange("a p b t -> p a (b t)"),
                                         om[t % 2][i][:, :].rearrange("p (a t) -> p a t", t=P).bitcast(F32)
                                         ).then_inc(stored[t % 2], 16)
                        if t + 2 < n_turns:
                            load_gate(r, t + 2)
                        elif not last:
                            load_gate(r + 1, t + 2 - n_turns)
                        if not last and t + 1 in (n_turns // 2, n_turns):
                            load_head(r + 1, e)
                rounds(sp, round_)
                for b in range(2):
                    sp.wait_ge(stored[b], 16 * ROUNDS * n_turns)

            @block.tensor
            def _(pe):
                def round_(r, last, prologue=False):
                    S, K, G, E = Ring(r, n_scores), Ring(r, n_keys), Ring(r, n_turns), Ring(r, QT * n_turns)

                    def scores(u, n):
                        e, g, i, c, w = u
                        if i == 0 and c == 0 and e == 0:
                            pe.wait_ge(piece_loaded[g], (r + 1 + n // n_scores) * 16 * loads_of(g))
                        if n == n_scores // 2:
                            pe.wait_ge(second_loaded, (r + 1) * 16 * LOADS)
                        if n >= 2:
                            pe.wait_ge(negated, S.at(n - 1))
                        qcols = slice((4 * g + i) * P, (4 * g + i + 1) * P)
                        wide = max(w, 2 * P)
                        kcols = slice(c * CH, c * CH + wide)
                        diagonal = fox and c == g
                        nc.tensor.matmul(sps[n % 2][:, 0:wide], qa[e][:, qcols], ka[e][:, kcols],
                                         start=True, stop=False)
                        if diagonal:
                            nc.tensor.matmul(sps[n % 2][:, w - P:w], ident_b[:, :], mask[:, :],
                                             start=False, stop=False, skip_group_check=True)
                        mm = nc.tensor.matmul(sps[n % 2][:, 0:wide], qb[e][:, qcols], kb[e][:, kcols],
                                              start=False, stop=True)
                        mm.then_inc(scored, 1)

                    def transposes(u, n, t, q0):
                        e, g, j, i0 = u
                        pe.wait_ge(pt_lo, K.at(n - 2 if n >= 3 else 0))
                        for i in range(i0, QT):
                            if q0:
                                pe.wait_ge(expd, E.at(QT * t + i + 1))
                            mm = nc.tensor.transpose(tps[n % 3][:, i * P:(i + 1) * P],
                                                     prob[t % 2][:, i, j * P:(j + 1) * P], ident[:, :])
                        mm.then_inc(transposed, 1)

                    def weigh(u, n, t, first, last):
                        e, g, j, i0 = u
                        if first:
                            pe.wait_ge(added, G.at(max(t - 1, 0)))
                        for i in (HI, LO):
                            if i == HI:
                                pe.wait_ge(pt_hi, K.at(n + 1))
                            else:
                                pe.wait_ge(pt_lo, K.at(n + 1))
                            mm = nc.tensor.matmul(ops[t % 2][:, i0 * P:CH], v[e][:, j, :], pT[n % PT][i][:, i0 * P:CH],
                                                  start=(first and i == HI), stop=(last and i == LO),
                                                  skip_group_check=True)
                        mm.then_inc(weighed, 1)

                    def spread_sums(t):
                        pe.wait_ge(inverted, G.at(t + 1))
                        pe.wait_ge(scaled, G.at(t))
                        for i in range(4):
                            mm = nc.tensor.matmul(rps[0:DH, i * P:(i + 1) * P],
                                                  rinv[t % 2][:, i:i + 1].to_broadcast([P, DH]), ident[:, :],
                                                  start=True, stop=True)
                        mm.then_inc(spread, 1)

                    if prologue:
                        for n, u in enumerate(score_units(*turns[0])):
                            scores(u, n)
                        return
                    waiting = []
                    for t in range(n_turns):
                        k0, s1 = at_turn(t)[1], at_turn(t + 1)[0]
                        ahead, steps = plan(t, last)
                        for m, (u, made, _) in enumerate(steps):
                            transposes(u, k0 + m, t, m == 0)
                            for a in made:
                                scores(ahead[a], s1 + a)
                            waiting.append((u, k0 + m, t, m == 0, m == len(steps) - 1))
                            if len(waiting) > DEPTH:
                                weigh(*waiting.pop(0))
                            if ends(t, m):
                                spread_sums(t - 1)
                    for x in waiting:
                        weigh(*x)
                    spread_sums(n_turns - 1)
                round_(0, False, prologue=True)
                rounds(pe, round_)

            @block.scalar
            def _(act):
                def round_(r, last, prologue=False):
                    K, G, E = Ring(r, n_keys), Ring(r, n_turns), Ring(r, QT * n_turns)

                    def exponentials(t, i):
                        w = keys_of(turns[t % n_turns][1]) - (CH - P * (i + 1) if fox else 0)
                        act.wait_ge(maxed, E.at(QT * t + i + 1))
                        nc.scalar.activation(prob[t % 2][:, i, 0:w], prob[t % 2][:, i, 0:w], ACT.Exp,
                                             bias=nm[t % 2][:, i:i + 1], scale=-1.0,
                                             accum_out=rsum[t % 2][:, i:i + 1]).then_inc(expd, 1)

                    def pt_high(u, n):
                        e, g, j, i0 = u
                        act.wait_ge(transposed, K.at(n + 1))
                        act.wait_ge(weighed, K.at(max(n - PT + 1, 0)))
                        nc.scalar.activation(pT[n % PT][HI][:, i0 * P:CH], tps[n % 3][:, i0 * P:CH], ACT.Copy
                                             ).then_inc(pt_hi, 1)

                    def low_half(t):
                        act.wait_ge(weighed, K.at(at_turn(t + 1)[1]))
                        act.wait_ge(added, G.at(t))
                        nc.scalar.activation(low[:, :], ops[t % 2][DH:P, :], ACT.Copy).then_inc(low_done, 1)

                    if prologue:
                        for i in range(QT):
                            exponentials(0, i)
                        return
                    for t in range(n_turns):
                        k0 = at_turn(t)[1]
                        for m, (u, _, tiles) in enumerate(plan(t, last)[1]):
                            pt_high(u, k0 + m)
                            for i in tiles:
                                exponentials(t + 1, i)
                            if ends(t, m):
                                low_half(t - 1)
                    low_half(n_turns - 1)
                round_(0, False, prologue=True)
                rounds(act, round_)

            @block.vector
            def _(dve):
                fill(nc.vector, 0)

                def round_(r, last, prologue=False):
                    S, K, G, E = Ring(r, n_scores), Ring(r, n_keys), Ring(r, n_turns), Ring(r, QT * n_turns)

                    def negate(u, n, t):
                        e, g, i, c, w = u
                        dve.wait_ge(scored, S.at(n + 1))
                        if t >= 1 and i == 0 and c == 0:
                            dve.wait_ge(transposed, K.at(at_turn(t - 1)[1]))
                        nc.vector.tensor_scalar(prob[t % 2][:, i, c * CH:c * CH + w], sps[n % 2][:, 0:w], -SCALE, None,
                                                ALU.mult, ALU.min, accum_out=nmax[t % 2][:, i, c:c + 1]
                                                ).then_inc(negated, 1)
                        if c == (g if fox else 0):
                            dve.wait_ge(negated, S.at(n + 1))
                            nc.vector.tensor_reduce(nm[t % 2][:, i:i + 1], nmax[t % 2][:, i, 0:c + 1], AX.X, ALU.min
                                                    ).then_inc(maxed, 1)

                    def pt_low(u, n):
                        e, g, j, i0 = u
                        dve.wait_ge(pt_hi, K.at(n + 1))
                        nc.vector.tensor_tensor(pT[n % PT][LO][:, i0 * P:CH], tps[n % 3][:, i0 * P:CH],
                                                pT[n % PT][HI][:, i0 * P:CH].bitcast(F32), ALU.subtract
                                                ).then_inc(pt_lo, 1)

                    def invert(t):
                        dve.wait_ge(expd, E.at(QT * (t + 1)))
                        dve.wait_ge(spread, G.at(max(t - 1, 0)))
                        nc.vector.reciprocal(rinv[t % 2][:, :], rsum[t % 2][:, :]).then_inc(inverted, 1)

                    def scale(t):
                        dve.wait_ge(scaled, G.at(t))
                        dve.wait_ge(low_done, G.at(t + 1))
                        nc.vector.tensor_tensor(o1[:, :], ops[t % 2][0:DH, :], low[:, :], ALU.add).then_inc(added, 1)
                        dve.wait_ge(added, G.at(t + 1))
                        dve.wait_ge(spread, G.at(t + 1))
                        dve.wait_ge(o_lo, G.at(max(t - 1, 0)))
                        nc.vector.tensor_tensor(o2[t % 2][:, :], rps[0:DH, :], o1[:, :], ALU.mult).then_inc(scaled, 1)

                    if prologue:
                        for n, u in enumerate(score_units(*turns[0])):
                            negate(u, n, 0)
                        return
                    for t in range(n_turns):
                        k0, s1 = at_turn(t)[1], at_turn(t + 1)[0]
                        ahead, steps = plan(t, last)
                        invert(t)
                        for m, (u, made, _) in enumerate(steps):
                            for a in made:
                                negate(ahead[a], s1 + a, t + 1)
                            pt_low(u, k0 + m)
                            if ends(t, m):
                                scale(t - 1)
                    scale(n_turns - 1)
                round_(0, False, prologue=True)
                rounds(dve, round_)

            @block.gpsimd
            def _(pool):
                pool.memset(zero[:, :], 0.0).then_inc(zeroed[1], 1)
                pool.wait_ge(zeroed[1], 1)
                fill(pool, 1)
                with pool.Fori(0, ROUNDS) as r:
                    G = Ring(r, n_turns)
                    for t in range(n_turns):
                        b = t % 2
                        pool.wait_ge(gate_loaded[b], 16 * (r * (n_turns // 2) + t // 2 + 1))
                        pool.wait_ge(scaled, G.at(t + 1))
                        nc.gpsimd.tensor_tensor(o2[b][:, :], o2[b][:, :], gate[b][:, :], ALU.mult).then_inc(gated, 1)
                        pool.wait_ge(gated, G.at(t + 1))
                        pool.wait_ge(stored[b], 32 * (r * (n_turns // 2) + t // 2))
                        nc.gpsimd.tensor_tensor(om[b][HI][:, :], o2[b][:, :], zero[:, :], ALU.add).then_inc(o_hi, 1)
                        pool.wait_ge(o_hi, G.at(t + 1))
                        nc.gpsimd.tensor_tensor(om[b][LO][:, :], o2[b][:, :], om[b][HI][:, :].bitcast(F32),
                                                ALU.subtract).then_inc(o_lo, 1)




def project_out(nc, scr, out, x, w_out, final_norm_g):
    x_t = x[0].rearrange("(t p) d -> t p d", p=P)
    out_t = out[0].rearrange("(t p) d -> t p d", p=P)
    NC = D // CH
    RAW = 4
    ctx = ExitStack()
    with ctx:
        k = Pools(nc, ctx, "out")
        g = k.sb("g", [P, D])
        w_raw = [k.sb(f"wraw{s}", [P, D]) for s in range(RAW)]
        w = [k.sb(f"w{i}", [P, MIX_T, D], F32R) for i in (HI, LO)]
        mix = [[k.sb(f"mix{s}{i}", [P, MIX_T, P], F32R) for i in (HI, LO)] for s in range(2)]
        xin, y, o = ([k.sb(f"{n}{s}", [P, D]) for s in range(2)] for n in ("x", "y", "o"))
        junk = k.sb("junk", [P, D])
        st = k.sb("st", [P, 4])
        yps = [k.ps(f"yps{s}", [P, NC, CH]) for s in range(2)]
        names = ("g_loaded w_loaded0 w_loaded1 w_loaded2 w_loaded3 w_hi w_lo mix_loaded0 mix_loaded1 x_loaded0 x_loaded1 projected added "
                 "squared mean_done filled rstd_done normed stored0 stored1 sp_goes").split()
        (g_loaded, w_loaded0, w_loaded1, w_loaded2, w_loaded3, w_hi, w_lo, mix_loaded0, mix_loaded1, x_loaded0, x_loaded1, projected, added,
         squared, mean_done, filled, rstd_done, normed, stored0, stored1, sp_goes) = map(k.sem, names)
        w_loaded, mix_loaded = (w_loaded0, w_loaded1, w_loaded2, w_loaded3), (mix_loaded0, mix_loaded1)
        x_loaded, stored = (x_loaded0, x_loaded1), (stored0, stored1)
        with nc.Block() as block:
            @block.sync
            def _(sp):
                def load(t, s):
                    for i in (HI, LO):
                        sp.dma_start(mix[s][i][:, :, :].bitcast(F32),
                                     scr.mix[i, bass.ds(t, 1)].rearrange("a p k t -> (a p) k t")
                                     ).then_inc(mix_loaded[s], 16)
                    sp.dma_start(xin[s][:, :], x_t[bass.ds(t, 1)].rearrange("a p d -> (a p) d")
                                 ).then_inc(x_loaded[s], 16)
                for kk in range(MIX_T):
                    if kk >= RAW:
                        sp.wait_ge(w_lo, kk - RAW + 1)
                    sp.dma_start(w_raw[kk % RAW][:, :], w_out[0, kk * P:(kk + 1) * P, :]
                                 ).then_inc(w_loaded[kk % RAW], 16)
                    if kk == 1:
                        load(0, 0)
                load(1, 1)
                sp.dma_start(g[:, :], final_norm_g.rearrange("(a d) -> a d", a=1)[0].partition_broadcast(P)
                             ).then_inc(g_loaded, 16)
                with sp.Fori(1, TT // 2) as h:
                    for s in range(2):
                        t = 2 * h + s
                        sp.wait_ge(projected, t - 1)
                        sp.sem_inc(sp_goes, 1)
                        sp.wait_ge(added, t - 1)
                        sp.sem_inc(sp_goes, 1)
                        load(t, s)

            @block.tensor
            def _(pe):
                def tile(h, s, first):
                    t = 2 * h + s
                    pe.wait_ge(mix_loaded[s], 32 * (h + 1))
                    if not first:
                        pe.wait_ge(added, t - 1)
                    for kk in range(MIX_T):
                        if first and s == 0:
                            pe.wait_ge(w_lo, kk + 1)
                        for n, (a, b) in enumerate(PASSES):
                            for c in range(NC):
                                mm = nc.tensor.matmul(yps[s][:, c, :], mix[s][a][:, kk, :],
                                                      w[b][:, kk, c * CH:(c + 1) * CH],
                                                      start=(kk == 0 and n == 0), stop=(kk == MIX_T - 1 and n == 2))
                    mm.then_inc(projected, 1)
                for s in range(2):
                    tile(0, s, True)
                with pe.Fori(1, TT // 2) as h:
                    for s in range(2):
                        tile(h, s, False)

            @block.vector
            def _(dve):
                for kk in range(MIX_T):
                    dve.wait_ge(w_hi, kk + 1)
                    nc.vector.tensor_tensor(w[LO][:, kk, :], w_raw[kk % RAW][:, :], w[HI][:, kk, :].bitcast(F32),
                                            ALU.subtract).then_inc(w_lo, 1)
                dve.wait_ge(g_loaded, 16)
                with dve.Fori(0, TT // 2) as h:
                    for s in range(2):
                        t = 2 * h + s
                        dve.wait_ge(x_loaded[s], 16 * (h + 1))
                        dve.wait_ge(projected, t + 1)
                        nc.vector.tensor_tensor(y[s][:, :], yps[s][:, :, :].rearrange("p c n -> p (c n)"), xin[s][:, :],
                                                ALU.add).then_inc(added, 1)
                        dve.wait_ge(squared, t + 1)
                        nc.vector.tensor_scalar(st[:, 1:2], st[:, 0:1], 1.0 / D, EPS, ALU.mult, ALU.add
                                                ).then_inc(mean_done, 1)
                        dve.wait_ge(rstd_done, t + 1)
                        dve.wait_ge(stored[s], 16 * h)
                        nc.vector.scalar_tensor_tensor(o[s][:, :], y[s][:, :], st[:, 3:4], g[:, :], ALU.mult, ALU.mult
                                                       ).then_inc(normed, 1)

            @block.gpsimd
            def _(pool):
                pool.memset(st[:, 2:3], -0.5).then_inc(filled, 1)
                pool.wait_ge(filled, 1)
                with pool.Fori(0, TT // 2) as h:
                    for s in range(2):
                        pool.wait_ge(mean_done, 2 * h + s + 1)
                        nc.gpsimd.tensor_tensor(st[:, 3:4], st[:, 1:2], st[:, 2:3], ALU.pow).then_inc(rstd_done, 1)

            @block.scalar
            def _(act):
                for kk in range(MIX_T):
                    act.wait_ge(w_loaded[kk % RAW], 16 * (kk // RAW + 1))
                    nc.scalar.activation(w[HI][:, kk, :], w_raw[kk % RAW][:, :], ACT.Copy).then_inc(w_hi, 1)
                with act.Fori(0, TT // 2) as h:
                    for s in range(2):
                        t = 2 * h + s
                        act.wait_ge(added, t + 1)
                        nc.scalar.activation(junk[:, :], y[s][:, :], ACT.Square, accum_out=st[:, 0:1]).then_inc(squared, 1)
                        act.wait_ge(normed, t + 1)
                        act.dma_start(out_t[bass.ds(t, 1)].rearrange("a p d -> (a p) d"), o[s][:, :]
                                      ).then_inc(stored[s], 16)
                for s in range(2):
                    act.wait_ge(stored[s], 16 * (TT // 2))


def hymba_block(nc, out, x, mem, norm_g, w_cols, w_tok, w_alpha_up, b_alpha, b_forget, gla_norm_g, mem_norm_g,
                w_mem_kv, w_out, final_norm_g):
    scr = Scratch(nc)
    ctx = ExitStack()
    with ctx:
        k = Pools(nc, ctx, "all")
        ident, ident_b, fox_mask, gla_mask = constants(nc, k)
        h_ctx = ExitStack()
        with h_ctx:
            steps_ctx = ExitStack()
            with steps_ctx:
                tokens = TokenStage(nc, h_ctx, steps_ctx, scr, ident, x, norm_g, w_tok)
                memory_keys_values(nc, scr, ident, tokens, mem, mem_norm_g, w_mem_kv)
                kh = Pools(nc, h_ctx, "h")
                hT = [kh.sb(f"T{i}", [P, KT, T], F32R) for i in (HI, LO)]
                fglr = kh.sb("fglr", [P, TT, FGLR])
                project_tokens(nc, scr, tokens, hT, fglr)
            project_columns(nc, scr, ident, tokens, hT, fglr, w_cols, b_forget)
        gated_linear_attention(nc, scr, ident, gla_mask, w_alpha_up, b_alpha, gla_norm_g)
        softmax_attention(nc, scr, ident, ident_b, fox_mask, fox=False)
        softmax_attention(nc, scr, ident, ident_b, fox_mask, fox=True)
        project_out(nc, scr, out, x, w_out, final_norm_g)


_OUTS = [((1, T, D), "float32")]


def laid_out(inputs):
    import numpy as np

    a = {n: np.ascontiguousarray(inputs[n]) for n in (
        "x", "mem", "norm_g", "w_alpha_up", "b_alpha", "b_forget", "gla_norm_g", "mem_norm_g", "w_mem_kv",
        "w_out", "final_norm_g")}
    w = np.ascontiguousarray(inputs["w_in"])[0].reshape(KT, P, -1)
    starts = ([F_Q + P * i for i in range(3)] + [M_Q + P * i for i in range(2)] + [F_K + P * i for i in range(3)]
              + [G_GATE + P * i for i in range(3)] + [F_GATE + P * i for i in range(3)]
              + [M_GATE + P * i for i in range(2)] + [G_Q + P * i for i in range(6)])
    a["w_cols"] = np.ascontiguousarray(np.stack([w[:, :, c:c + P].transpose(1, 0, 2) for c in starts]))
    tok = np.concatenate([w[:, :, F_V:F_V + 384], w[:, :, F_FG:F_FG + FOX_H], w[:, :, G_LR:G_LR + GLA_R]], axis=2)
    a["w_tok"] = np.ascontiguousarray(tok.transpose(1, 0, 2))
    return a


def kernel(**inputs):
    import numpy as np
    import concourse.bacc as bacc
    from concourse.bass_utils import run_bass_kernel_spmd

    nc = bacc.Bacc("TRN2", target_bir_lowering=False, num_devices=1)
    arrays, args = {}, {}
    for name, a in laid_out(inputs).items():
        arrays[f"in_{name}"] = a
        args[name] = nc.dram_tensor(f"in_{name}", a.shape, mybir.dt.from_np(a.dtype), kind="ExternalInput").ap()
    shape, dtype = _OUTS[0]
    out = nc.dram_tensor("out_0", shape, mybir.dt.from_np(np.dtype(dtype)), kind="ExternalOutput").ap()
    hymba_block(nc, out=out, **args)
    r = run_bass_kernel_spmd(nc, [arrays], core_ids=[0])
    return r.results[0]["out_0"]
```

```python
import concourse.bass as bass
from concourse import mybir
from contextlib import ExitStack

F32 = mybir.dt.float32
F32R = mybir.dt.float32r
BF16 = mybir.dt.bfloat16
ALU = mybir.AluOpType
ACT = mybir.ActivationFunctionType
AX = mybir.AxisListType

P = 128
D = 1024
T = 2048
M = 256
KT = D // P
TT = T // P
EPS = 1e-6
CH = 512
NCH = T // CH

GLA_H, GLA_DK, GLA_DV, GLA_R, GLA_C, GLA_GATE = 4, 48, 96, 16, 64, 16.0
FOX_H, DH = 6, 64
MEM_H = 4
MIX_T = 8

TOK_C = FOX_H * DH + FOX_H + GLA_R
FGLR = FOX_H + GLA_R
NSPLIT, NGATE, NRAW = 8, 8, 6
NCOL = NSPLIT + NGATE + NRAW

IN = [192, 192, 384, 16, 384, 384, 384, 384, 6, 384, 256, 256]
OFF = [sum(IN[:i]) for i in range(len(IN) + 1)]
G_Q, G_K, G_V, G_LR, G_GATE, F_Q, F_K, F_V, F_FG, F_GATE, M_Q, M_GATE = OFF[:-1]

HI, LO = 0, 1
PASSES = [(HI, HI), (HI, LO), (LO, HI)]


class Scratch:

    def __init__(self, nc):
        def dram(name, shape, dt):
            return nc.dram_tensor(name, shape, dt).ap()
        self.split = dram("scr_split", [NSPLIT, 2, P, T], F32)
        self.gates = dram("scr_gates", [NGATE, P, T], F32)
        self.raw = dram("scr_raw", [NRAW * P, T], F32)
        self.fox_v = dram("scr_fox_v", [FOX_H, P, TT, 2 * DH], F32)
        self.mem_k = dram("scr_mem_k", [2, 2, P, M], F32)
        self.mem_v = dram("scr_mem_v", [MEM_H, P, 2, 2 * DH], F32)
        self.lr = dram("scr_lr", [GLA_R, T], F32)
        self.crow = dram("scr_crow", [4, FOX_H, T], F32)
        self.mix = dram("scr_mix", [2, TT, P, MIX_T, P], F32)


class Pools:

    def __init__(self, nc, ctx, tag, clears=False):
        self.nc, self.ctx, self.tag = nc, ctx, tag
        self.cleared = [] if clears else None
        if clears:
            ctx.callback(self.clear)

    def clear(self):
        self.nc.clear_and_free_semaphores(self.cleared)
        self.nc.all_engine_barrier()

    def sb(self, name, shape, dt=F32):
        return self.ctx.enter_context(self.nc.sbuf_tensor(f"{self.tag}_{name}", shape, dt))

    def ps(self, name, shape, dt=F32):
        return self.ctx.enter_context(self.nc.psum_tensor(f"{self.tag}_{name}", shape, dt))

    def sem(self, name):
        if self.cleared is None:
            return self.ctx.enter_context(self.nc.semaphore(f"{self.tag}_{name}"))
        sem = self.nc.alloc_semaphore(f"{self.tag}_{name}")
        self.cleared.append(sem)
        return sem


class Constants:

    MADE = 9

    def __init__(self, nc, ctx):
        k = Pools(nc, ctx, "all")
        self.ident = k.sb("ident", [P, P])
        self.ident_b = k.sb("ident_b", [P, P], BF16)
        self.fox_mask = k.sb("fox_mask", [P, P], BF16)
        self.gla_mask = k.sb("gla_mask", [P, 4, P])
        self.made = k.sem("made")

    def make(self, pool):
        made, fox_mask, gla_mask = self.made, self.fox_mask, self.gla_mask
        pool.memset(self.ident[:, :], 0.0).then_inc(made, 1)
        pool.memset(self.ident_b[:, :], 0.0).then_inc(made, 1)
        pool.memset(fox_mask[:, :], 0.0).then_inc(made, 1)
        pool.memset(gla_mask[:, :, :], 1.0).then_inc(made, 1)
        pool.wait_ge(made, 4)
        for m in (self.ident, self.ident_b):
            pool.affine_select(out=m[:, :], in_=m[:, :], compare_op=ALU.not_equal, fill=1.0,
                               base=0, pattern=[[-1, P]], channel_multiplier=1).then_inc(made, 1)
        pool.affine_select(out=fox_mask[:, :], in_=fox_mask[:, :], compare_op=ALU.is_ge, fill=-1e38,
                           base=0, pattern=[[-1, P]], channel_multiplier=1).then_inc(made, 1)
        pool.affine_select(out=gla_mask[:, :, :], in_=gla_mask[:, :, :], compare_op=ALU.is_ge, fill=0.0,
                           base=0, pattern=[[0, 4], [1, P]], channel_multiplier=-1).then_inc(made, 1)
        pool.wait_ge(made, 8)
        pool.memset(gla_mask[0:GLA_C, :, GLA_C:P], 0.0).then_inc(made, 1)
        pool.wait_ge(made, 9)


def memory_keys_values(nc, scr, consts, tokens, mem, mem_norm_g, w_mem_kv):
    ident = consts.ident
    MT = M // P
    KV = 2 * MEM_H * DH
    QUARTERS = 4
    QK = KT // QUARTERS
    ctx = ExitStack()
    with ctx:
        k = Pools(nc, ctx, "mem", clears=True)
        x, g, xn, sq = k.sb("x", [P, MT, D]), k.sb("g", [P, D]), k.sb("xn", [P, MT, D]), k.sb("sq", [P, D])
        xT = [k.sb(f"xT{i}", [P, KT, M], F32R) for i in (HI, LO)]
        w = k.sb("w", [P, KT, KV])
        wp = [k.sb(f"w{i}", [P, KT, KV], F32R) for i in (HI, LO)]
        kst = [k.sb(f"k{i}", [P, MT, M], F32R) for i in (HI, LO)]
        vst = k.sb("v", [P, MT, MEM_H, 2, DH], F32R)
        ss, ms, rstd, half = (k.sb(n, [P, MT]) for n in ("ss", "ms", "rstd", "half"))
        tps = [k.ps(f"tps{i}", [P, 4, P]) for i in range(2)]
        kps, vps = k.ps("kps", [P, MT, M]), k.ps("vps", [P, MT, M])
        x_loaded0, x_loaded1, g_loaded, w_loaded0, w_loaded1, filled, squared, mean_done, rstd_done, normed = map(
            k.sem, "x_loaded0 x_loaded1 g_loaded w_loaded0 w_loaded1 filled squared mean_done rstd_done normed".split())
        transposed, hi_done, lo_done, w_hi, w_lo, k_done, v_done, ev_hi, ev_lo, stored = map(
            k.sem, "transposed hi_done lo_done w_hi w_lo k_done v_done ev_hi ev_lo stored".split())

        x_loaded, w_loaded = (x_loaded0, x_loaded1), (w_loaded0, w_loaded1)
        half_k = KT // 2

        def columns(i):
            t, c = divmod(i, 2)
            return slice(4 * c, 4 * c + 4), slice(t * P, (t + 1) * P)

        with nc.Block() as block:
            @block.sync
            def _(sp):
                for t in range(MT):
                    sp.dma_start(x[:, t, :], mem[0, t * P:(t + 1) * P, :]).then_inc(x_loaded[t], 16)
                sp.dma_start(g[:, :], mem_norm_g[0].partition_broadcast(P)).then_inc(g_loaded, 16)
                for n in range(2):
                    ks = slice(half_k * n, half_k * (n + 1))
                    sp.dma_start(w[:, ks, :], w_mem_kv[0].rearrange("(k p) n -> p k n", p=P)[:, ks, :]
                                 ).then_inc(w_loaded[n], 16)
                tokens.first_loads(sp)
                sp.wait_ge(ev_lo, 1)
                for i in range(MT):
                    for part in (HI, LO):
                        sp.dma_start(scr.mem_k[i, part], kst[part][:, i, :].bitcast(F32)).then_inc(stored, 16)
                for t in range(MT):
                    sp.wait_ge(ev_lo, t + 2)
                    sp.dma_start(scr.mem_v[:, :, t, :].rearrange("h p c -> p h c"),
                                 vst[:, t, :, :, :].rearrange("p h a c -> p h (a c)").bitcast(F32)).then_inc(stored, 16)
                sp.wait_ge(stored, 16 * 3 * MT)

            @block.scalar
            def _(act):
                for t in range(MT):
                    act.wait_ge(x_loaded[t], 16)
                    if t:
                        act.wait_ge(squared, t)
                    nc.scalar.activation(sq[:, :], x[:, t, :], ACT.Square,
                                         accum_out=ss[:, t:t + 1]).then_inc(squared, 1)

                def weights_high(q):
                    act.wait_ge(w_loaded[2 * q // QUARTERS], 16)
                    ks = slice(QK * q, QK * (q + 1))
                    nc.scalar.activation(wp[HI][:, ks, :], w[:, ks, :], ACT.Copy).then_inc(w_hi, 1)

                for i in range(2 * MT):
                    if i % 2 == 0:
                        weights_high(i)
                        weights_high(i + 1)
                    act.wait_ge(transposed, i + 1)
                    ks, cols = columns(i)
                    nc.scalar.activation(xT[HI][:, ks, cols], tps[i % 2][:, :, :], ACT.Copy).then_inc(hi_done, 1)
                tokens.squares(act, 0, 0)
                act.wait_ge(k_done, MT)
                nc.scalar.activation(kst[HI][:, :, :], kps[:, :, :], ACT.Copy).then_inc(ev_hi, 1)
                tokens.high_part(act, 0, 0)
                tokens.squares(act, 0, 1)
                act.wait_ge(v_done, MT)
                for t in range(MT):
                    nc.scalar.activation(vst[:, t, :, HI, :], vps[:, t, :].rearrange("p (h c) -> p h c", c=DH),
                                         ACT.Copy).then_inc(ev_hi, 1)

            @block.vector
            def _(dve):
                dve.wait_ge(squared, MT)
                nc.vector.tensor_scalar(ms[:, :], ss[:, :], 1.0 / D, EPS, ALU.mult, ALU.add).then_inc(mean_done, 1)
                dve.wait_ge(g_loaded, 16)
                dve.wait_ge(rstd_done, 1)
                for t in range(MT):
                    dve.wait_ge(x_loaded[t], 16)
                    nc.vector.scalar_tensor_tensor(xn[:, t, :], x[:, t, :], rstd[:, t:t + 1], g[:, :],
                                                   ALU.mult, ALU.mult).then_inc(normed, 1)

                def weights_low(q):
                    dve.wait_ge(w_hi, q + 1)
                    ks = slice(QK * q, QK * (q + 1))
                    nc.vector.tensor_tensor(wp[LO][:, ks, :], w[:, ks, :], wp[HI][:, ks, :].bitcast(F32),
                                            ALU.subtract).then_inc(w_lo, 1)

                for i in range(2 * MT):
                    if i % 2 == 0:
                        weights_low(i)
                        weights_low(i + 1)
                    dve.wait_ge(hi_done, i + 1)
                    ks, cols = columns(i)
                    nc.vector.tensor_tensor(xT[LO][:, ks, cols], tps[i % 2][:, :, :], xT[HI][:, ks, cols].bitcast(F32),
                                            ALU.subtract).then_inc(lo_done, 1)
                tokens.normalise(dve, 0, 0)
                dve.wait_ge(ev_hi, 1)
                nc.vector.tensor_tensor(kst[LO][:, :, :], kps[:, :, :], kst[HI][:, :, :].bitcast(F32),
                                        ALU.subtract).then_inc(ev_lo, 1)
                tokens.low_part(dve, 0, 0)
                tokens.normalise(dve, 0, 1)
                dve.wait_ge(ev_hi, 1 + MT)
                for t in range(MT):
                    nc.vector.tensor_tensor(vst[:, t, :, LO, :], vps[:, t, :].rearrange("p (h c) -> p h c", c=DH),
                                            vst[:, t, :, HI, :].bitcast(F32), ALU.subtract).then_inc(ev_lo, 1)

            @block.gpsimd
            def _(pool):
                consts.make(pool)
                pool.memset(half[:, :], -0.5).then_inc(filled, 1)
                pool.memset(tokens.half[:, :], -0.5).then_inc(filled, 1)
                pool.wait_ge(filled, 2)
                pool.wait_ge(mean_done, 1)
                nc.gpsimd.tensor_tensor(rstd[:, :], ms[:, :], half[:, :], ALU.pow).then_inc(rstd_done, 1)
                for kk in range(KT):
                    tokens.split_weights(pool, kk)
                    if kk == KT // 2 - 1:
                        tokens.rstds(pool, 0, 0)
                    if kk == KT - 2:
                        tokens.rstds(pool, 0, 1)

            @block.tensor
            def _(pe):
                pe.wait_ge(consts.made, consts.MADE)
                for i in range(2 * MT):
                    t, c = divmod(i, 2)
                    pe.wait_ge(normed, t + 1)
                    if i >= 2:
                        pe.wait_ge(lo_done, i - 1)
                    for j in range(4):
                        kk = 4 * c + j
                        mm = nc.tensor.transpose(tps[c][:, j, :], xn[:, t, kk * P:(kk + 1) * P], ident[:, :])
                    mm.then_inc(transposed, 1)
                pe.wait_ge(lo_done, 2 * MT)
                for i in range(MT):
                    for kk in range(KT):
                        pe.wait_ge(w_lo, kk // QK + 1)
                        for n, (a, b) in enumerate(PASSES):
                            mm = nc.tensor.matmul(kps[:, i, :], wp[a][:, kk, i * P:(i + 1) * P], xT[b][:, kk, :],
                                                  start=(kk == 0 and n == 0), stop=(kk == KT - 1 and n == 2))
                    mm.then_inc(k_done, 1)
                tokens.transposes(pe, 0, 0, first=True)
                for t in range(MT):
                    for kk in range(KT):
                        for n, (a, b) in enumerate(PASSES):
                            mm = nc.tensor.matmul(vps[:, t, :], xT[a][:, kk, t * P:(t + 1) * P],
                                                  wp[b][:, kk, M:2 * M],
                                                  start=(kk == 0 and n == 0), stop=(kk == KT - 1 and n == 2))
                    mm.then_inc(v_done, 1)


class TokenStage:

    RAW = 4

    def __init__(self, nc, ctx, ctx_steps, scr, ident, x, norm_g, w_tok):
        self.nc, self.scr, self.ident, self.norm_g, self.w_tok = nc, scr, ident, norm_g, w_tok
        self.x_t = x[0].rearrange("(t p) d -> t p d", p=P)
        k = Pools(nc, ctx, "tok")
        self.g = k.sb("g", [P, D])
        self.xin = [k.sb(f"xin{s}", [P, D]) for s in range(2)]
        self.xn = k.sb("xn", [P, D])
        self.ssq, self.mean, self.rstd, self.half = (k.sb(n, [P, 1]) for n in ("ssq", "mean", "rstd", "half"))
        self.raws = k.sb("wraw", [P, T])
        self.w_raw = [self.raws[:, TOK_C * s:TOK_C * (s + 1)] for s in range(self.RAW)]
        self.w = [k.sb(f"w{i}", [P, KT, TOK_C], F32R) for i in (HI, LO)]
        self.slot = [[k.sb(f"slot{s}{i}", [P, KT, P], F32R) for i in (HI, LO)] for s in range(2)]
        self.cols_loaded = [k.sem(f"cols_loaded{s}") for s in range(2)]
        k = Pools(nc, ctx_steps, "tok", clears=True)
        self.tps = [k.ps(f"tps{c}", [P, 4, P]) for c in range(2)]
        self.junk = k.ps("junk", [P, 2 * CH])
        (self.g_loaded, self.w_hi, self.w_lo, self.squared, self.mean_done, self.rstd_done, self.normed,
         self.transposed, self.hi_done, self.lo_done) = map(
            k.sem, "g_loaded w_hi w_lo squared mean_done rstd_done normed transposed hi_done lo_done".split())
        self.x_loaded = [k.sem(f"x_loaded{s}") for s in range(2)]
        self.w_loaded = [k.sem(f"w_loaded{s}") for s in range(self.RAW)]

    def first_loads(self, sp):
        for t in range(2):
            sp.dma_start(self.xin[t][:, :], self.x_t[t]).then_inc(self.x_loaded[t], 16)
            if t == 0:
                sp.dma_start(self.g[:, :], self.norm_g[0].partition_broadcast(P)).then_inc(self.g_loaded, 16)
        for kk in range(KT):
            if kk >= self.RAW:
                sp.wait_ge(self.w_lo, kk - self.RAW + 1)
            sp.dma_start(self.w_raw[kk % self.RAW][:, :], self.w_tok[:, kk, :]
                         ).then_inc(self.w_loaded[kk % self.RAW], 16)

    def split_weights(self, pool, kk):
        raw, hi = self.w_raw[kk % self.RAW], self.w[HI][:, kk, :]
        pool.wait_ge(self.w_loaded[kk % self.RAW], 16 * (kk // self.RAW + 1))
        pool.tensor_scalar(hi, raw[:, :], 1.0, 1.0, ALU.mult, ALU.mult).then_inc(self.w_hi, 1)
        pool.wait_ge(self.w_hi, kk + 1)
        pool.tensor_tensor(self.w[LO][:, kk, :], raw[:, :], hi.bitcast(F32), ALU.subtract).then_inc(self.w_lo, 1)

    def squares(self, act, h, s):
        t = 2 * h + s
        act.wait_ge(self.x_loaded[s], 16 * (h + 1))
        act.wait_ge(self.mean_done, t)
        act.activation(self.junk[:, :], self.xin[s][:, :], ACT.Square, accum_out=self.ssq[:, :]
                       ).then_inc(self.squared, 1)

    def rstds(self, pool, h, s):
        t = 2 * h + s
        pool.wait_ge(self.mean_done, t + 1)
        pool.wait_ge(self.normed, t)
        pool.tensor_tensor(self.rstd[:, :], self.mean[:, :], self.half[:, :], ALU.pow).then_inc(self.rstd_done, 1)

    def normalise(self, dve, h, s):
        t = 2 * h + s
        dve.wait_ge(self.squared, t + 1)
        dve.tensor_scalar(self.mean[:, :], self.ssq[:, :], 1.0 / D, EPS, ALU.mult, ALU.add).then_inc(self.mean_done, 1)
        dve.wait_ge(self.transposed, 2 * t)
        dve.wait_ge(self.g_loaded, 16)
        dve.wait_ge(self.rstd_done, t + 1)
        dve.scalar_tensor_tensor(self.xn[:, :], self.xin[s][:, :], self.rstd[:, :], self.g[:, :],
                                 ALU.mult, ALU.mult).then_inc(self.normed, 1)

    def transposes(self, pe, h, s, first=False):
        t = 2 * h + s
        pe.wait_ge(self.normed, t + 1)
        for c in range(2):
            if not first:
                pe.wait_ge(self.lo_done, 2 * t - 1 + c)
            for j in range(4):
                kk = 4 * c + j
                mm = pe.transpose(self.tps[c][:, j, :], self.xn[:, kk * P:(kk + 1) * P], self.ident[:, :])
            mm.then_inc(self.transposed, 1)

    def high_part(self, act, h, s):
        t = 2 * h + s
        for c in range(2):
            act.wait_ge(self.transposed, 2 * t + c + 1)
            act.activation(self.slot[s][HI][:, 4 * c:4 * c + 4, :], self.tps[c][:, :, :], ACT.Copy
                           ).then_inc(self.hi_done, 1)

    def low_part(self, dve, h, s):
        t = 2 * h + s
        for c in range(2):
            dve.wait_ge(self.hi_done, 2 * t + c + 1)
            dve.tensor_tensor(self.slot[s][LO][:, 4 * c:4 * c + 4, :], self.tps[c][:, :, :],
                              self.slot[s][HI][:, 4 * c:4 * c + 4, :].bitcast(F32), ALU.subtract
                              ).then_inc(self.lo_done, 1)


def project_tokens(nc, scr, tk, hT, fglr, w_cols):
    V = FOX_H * DH
    slot, w = tk.slot, tk.w
    ctx = ExitStack()
    with ctx:
        k = Pools(nc, ctx, "tok2", clears=True)
        vst = [k.sb(f"vst{s}", [P, FOX_H, 2, DH], F32R) for s in range(2)]
        mps = [k.ps(f"mps{s}", [P, CH]) for s in range(2)]
        (kept_hi, kept_lo, multiplied, v_hi, v_lo, v_stored0, v_stored1, pool_goes, act_goes) = map(
            k.sem, "kept_hi kept_lo multiplied v_hi v_lo v_stored0 v_stored1 pool_goes act_goes".split())
        v_stored = (v_stored0, v_stored1)

        def steps(eng, step):
            for t in (0, 1):
                step(0, t, True, True)
            with eng.Fori(1, TT // 2 - 1) as h:
                for s in range(2):
                    step(h, s, True, True)
            step(TT // 2 - 1, 0, True, False)
            step(TT // 2 - 1, 1, False, False)

        with nc.Block() as block:
            @block.sync
            def _(sp):
                def store(t, s):
                    sp.wait_ge(v_lo, t + 1)
                    sp.dma_start(scr.fox_v[:, :, bass.ds(t, 1), :].rearrange("h p a c -> p h (a c)"),
                                 vst[s][:, :, :, :].rearrange("p h a c -> p h (a c)").bitcast(F32)
                                 ).then_inc(v_stored[s], 16)

                def step(h, s, _, more):
                    t = 2 * h + s
                    if more:
                        sp.wait_ge(tk.normed, t + 1)
                        sp.dma_start(tk.xin[s][:, :], tk.x_t[bass.ds(t + 2, 1)].rearrange("a p d -> (a p) d")
                                     ).then_inc(tk.x_loaded[s], 16)
                    if not (isinstance(h, int) and t == 0):
                        store(t - 1, 1 - s)
                steps(sp, step)
                for s in range(2):
                    if s:
                        sp.wait_ge(tk.normed, TT)
                    sp.dma_start(tk.xin[s][:, :], w_cols[s].rearrange("p k c -> p (k c)")
                                 ).then_inc(tk.cols_loaded[s], 16)
                store(TT - 1, 1)
                for s in range(2):
                    sp.wait_ge(v_stored[s], 16 * TT // 2)

            @block.scalar
            def _(act):
                def keep_high(h, s):
                    t = 2 * h + s
                    act.wait_ge(tk.hi_done, 2 * t + 2)
                    act.sem_inc(act_goes, 1)
                    nc.scalar.activation(hT[HI][:, :, bass.ds(t * P, P)], slot[s][HI][:, :, :].bitcast(F32), ACT.Copy
                                         ).then_inc(kept_hi, 1)
                keep_high(0, 0)

                def step(h, s, one_more, two_more):
                    t = 2 * h + s
                    if one_more:
                        act.wait_ge(multiplied, t)
                        act.wait_ge(kept_hi, t)
                        act.wait_ge(kept_lo, t)
                        tk.high_part(nc.scalar, h + s, 1 - s)
                    if two_more:
                        tk.squares(nc.scalar, h + 1, s)
                    if one_more:
                        keep_high(h + s, 1 - s)
                    act.wait_ge(multiplied, t + 1)
                    act.wait_ge(v_stored[s], 16 * h)
                    nc.scalar.activation(vst[s][:, :, HI, :], mps[s][:, 0:V].rearrange("p (h c) -> p h c", c=DH),
                                         ACT.Copy).then_inc(v_hi, 1)
                steps(act, step)

            @block.vector
            def _(dve):
                def step(h, s, one_more, two_more):
                    t = 2 * h + s
                    if one_more:
                        tk.low_part(nc.vector, h + s, 1 - s)
                    if two_more:
                        tk.normalise(nc.vector, h + 1, s)
                    dve.wait_ge(v_hi, t + 1)
                    nc.vector.tensor_copy(fglr[:, bass.ds(t, 1), :].rearrange("p a c -> p (a c)"),
                                          mps[s][:, V:TOK_C])
                    nc.vector.tensor_tensor(vst[s][:, :, LO, :], mps[s][:, 0:V].rearrange("p (h c) -> p h c", c=DH),
                                            vst[s][:, :, HI, :].bitcast(F32), ALU.subtract).then_inc(v_lo, 1)
                steps(dve, step)

            @block.gpsimd
            def _(pool):
                def keep_low(h, s):
                    t = 2 * h + s
                    pool.wait_ge(tk.lo_done, 2 * t + 2)
                    pool.sem_inc(pool_goes, 1)
                    nc.gpsimd.tensor_copy(hT[LO][:, :, bass.ds(t * P, P)], slot[s][LO][:, :, :].bitcast(F32)
                                          ).then_inc(kept_lo, 1)
                keep_low(0, 0)

                def step(h, s, one_more, two_more):
                    if two_more:
                        tk.rstds(nc.gpsimd, h + 1, s)
                    if one_more:
                        keep_low(h + s, 1 - s)
                steps(pool, step)
                pool.wait_ge(kept_lo, TT)

            @block.tensor
            def _(pe):
                def step(h, s, one_more, _):
                    t = 2 * h + s
                    if one_more:
                        tk.transposes(nc.tensor, h + s, 1 - s)
                    pe.wait_ge(tk.lo_done, 2 * t + 2)
                    if isinstance(h, int) and h == 0:
                        pe.wait_ge(tk.w_lo, KT)
                    else:
                        pe.wait_ge(v_lo, t - 1)
                    for kk in range(KT):
                        for n, (a, b) in enumerate(PASSES):
                            mm = nc.tensor.matmul(mps[s][:, 0:TOK_C], slot[s][a][:, kk, :], w[b][:, kk, :],
                                                  start=(kk == 0 and n == 0), stop=(kk == KT - 1 and n == 2))
                    mm.then_inc(multiplied, 1)
                steps(pe, step)


def project_columns(nc, scr, ident, tk, hT, fglr, w_cols, b_forget):
    R = 8
    ctx = ExitStack()
    with ctx:
        k = Pools(nc, ctx, "col")
        w_raw = [tile[:, :].rearrange("p (k c) -> p k c", c=P) for tile in tk.xin]
        w = tk.slot
        both = [tile[:, :, :].rearrange("p k c -> p (k c)") for tile in tk.w]
        stage = [[both[i][:, T + CH * s:T + CH * (s + 1)] for i in (HI, LO)] for s in range(2)]
        plain = [tk.xn[:, CH * s:CH * (s + 1)] for s in range(2)]
        rT = k.sb("rT", [FGLR, T])
        f = rT[0:FOX_H, :]
        a = tk.raws[0:FOX_H, :]
        parts = [both[i][0:FOX_H, 0:T] for i in (HI, LO)]
        bf = k.sb("bf", [FOX_H, 1])
        cps = [k.ps(f"cps{c}", [P, CH]) for c in range(NCH)]
        rps = k.ps("rps", [P, T])
        (w_hi, w_lo, projected, hi_done, bank_free, gate_done, raw_done,
         stored0, stored1, rows_loaded, rows_t, rows_copied, act_rows, dve_rows, pool_rows, rows_stored,
         pool_goes) = map(
            k.sem, ("w_hi w_lo projected hi_done bank_free gate_done raw_done "
                    "stored0 stored1 rows_loaded rows_t rows_copied act_rows dve_rows pool_rows rows_stored "
                    "pool_goes").split())
        w_loaded, stored = tk.cols_loaded, (stored0, stored1)
        split_st = 16 * 2 * 2
        plain_st = 16 * 2
        base_plain = NSPLIT * split_st

        with nc.Block() as block:
            @block.sync
            def _(sp):
                def load_next(j, s):
                    sp.wait_ge(w_lo, j + 1)
                    sp.dma_start(w_raw[s][:, :, :],
                                 w_cols[bass.ds(j + 2, 1)].rearrange("a p k c -> (a p) k c")
                                 ).then_inc(w_loaded[s], 16)

                def store_split(j):
                    for c in range(NCH):
                        sp.wait_ge(bank_free, 4 * j + c + 5)
                        for i in (HI, LO):
                            dst = scr.split[bass.ds(j, 1), i, :, c * CH:(c + 1) * CH]
                            sp.dma_start(dst.rearrange("a p t -> (a p) t"), stage[c % 2][i][:, :].bitcast(F32)
                                         ).then_inc(stored[c % 2], 16)

                def store_plain(j, dst, first):
                    for c in range(NCH):
                        sp.wait_ge(bank_free, 4 * j + c + 5)
                        d = dst[bass.ds(j - first, 1), :, c * CH:(c + 1) * CH].rearrange("a p t -> (a p) t")
                        sp.dma_start(d, plain[c % 2][:, :]).then_inc(stored[c % 2], 16)

                with sp.Fori(0, NSPLIT // 2) as h:
                    for s in range(2):
                        load_next(2 * h + s, s)
                        store_split(2 * h + s)
                with sp.Fori(NSPLIT // 2, (NSPLIT + NGATE) // 2) as h:
                    for s in range(2):
                        load_next(2 * h + s, s)
                        store_plain(2 * h + s, scr.gates, NSPLIT)
                raw = scr.raw.rearrange("(a p) t -> a p t", p=P)
                with sp.Fori((NSPLIT + NGATE) // 2, NCOL // 2 - 1) as h:
                    for s in range(2):
                        load_next(2 * h + s, s)
                        store_plain(2 * h + s, raw, NSPLIT + NGATE)
                store_plain(NCOL - 2, raw, NSPLIT + NGATE)
                store_plain(NCOL - 1, raw, NSPLIT + NGATE)
                for s in range(2):
                    sp.wait_ge(stored[s], base_plain + (NGATE + NRAW) * plain_st)

            @block.gpsimd
            def _(pool):
                def split(h, s):
                    j = 2 * h + s
                    pool.wait_ge(w_loaded[s], 16 * (h + 1))
                    pool.sem_inc(pool_goes, 1)
                    nc.gpsimd.tensor_scalar(w[s][HI][:, :, :], w_raw[s][:, :, :], 1.0, 1.0, ALU.mult, ALU.mult
                                            ).then_inc(w_hi, 1)
                    pool.wait_ge(w_hi, j + 1)
                    nc.gpsimd.tensor_tensor(w[s][LO][:, :, :], w_raw[s][:, :, :], w[s][HI][:, :, :].bitcast(F32),
                                            ALU.subtract).then_inc(w_lo, 1)
                split(0, 0)
                pool.dma_start(bf[:, :], b_forget.rearrange("a h -> h a")).then_inc(rows_loaded, 16)
                split(0, 1)
                pool.wait_ge(rows_copied, 1)
                pool.dma_start(scr.lr, rT[FOX_H:FGLR, :]).then_inc(rows_stored, 16)
                pool.wait_ge(dve_rows, 4)
                nc.gpsimd.tensor_scalar(f, f, float(R), 1.0, ALU.mult, ALU.mult).then_inc(pool_rows, 1)
                pool.wait_ge(pool_rows, 1)
                nc.gpsimd.tensor_copy(parts[HI][:, :], f).then_inc(pool_rows, 1)
                pool.wait_ge(pool_rows, 2)
                nc.gpsimd.tensor_tensor(parts[LO][:, :], f, parts[HI][:, :].bitcast(F32), ALU.subtract
                                        ).then_inc(pool_rows, 1)
                pool.wait_ge(pool_rows, 3)
                for i in (HI, LO):
                    pool.dma_start(scr.crow[i], parts[i][:, :].bitcast(F32)).then_inc(rows_stored, 16)
                pool.wait_ge(rows_stored, 48)
                for i in (HI, LO):
                    nc.gpsimd.tensor_scalar(parts[i][:, :], parts[i][:, :].bitcast(F32), -1.0, 1.0,
                                            ALU.mult, ALU.mult).then_inc(pool_rows, 1)
                pool.wait_ge(pool_rows, 5)
                for i in (HI, LO):
                    pool.dma_start(scr.crow[2 + i], parts[i][:, :].bitcast(F32)).then_inc(rows_stored, 16)
                pool.wait_ge(rows_stored, 80)
                with pool.Fori(1, NCOL // 2) as h:
                    for s in range(2):
                        pool.wait_ge(projected, 4 * (2 * h + s - 1))
                        split(h, s)

            @block.tensor
            def _(pe):
                for t in range(TT):
                    mm = nc.tensor.transpose(rps[0:FGLR, t * P:(t + 1) * P], fglr[:, t, :], ident[:, :])
                mm.then_inc(rows_t, 1)
                with pe.Fori(0, NCOL // 2) as h:
                    for s in range(2):
                        j = 2 * h + s
                        pe.wait_ge(w_lo, j + 1)
                        for c in range(NCH):
                            pe.wait_ge(bank_free, 4 * j + c + 1)
                            for kk in range(KT):
                                for n, (a_, b_) in enumerate(PASSES):
                                    mm = nc.tensor.matmul(cps[c][:, :], w[s][a_][:, kk, :],
                                                          hT[b_][:, kk, c * CH:(c + 1) * CH],
                                                          start=(kk == 0 and n == 0), stop=(kk == KT - 1 and n == 2))
                            mm.then_inc(projected, 1)

            @block.scalar
            def _(act):
                act.wait_ge(rows_t, 1)
                nc.scalar.activation(rT[:, :], rps[0:FGLR, :], ACT.Copy).then_inc(rows_copied, 1)
                act.wait_ge(dve_rows, 1)
                nc.scalar.activation(a[:, :], f, ACT.Abs).then_inc(act_rows, 1)
                act.wait_ge(act_rows, 1)
                nc.scalar.activation(a[:, :], a[:, :], ACT.Exp, scale=-1.0).then_inc(act_rows, 1)
                act.wait_ge(act_rows, 2)
                nc.scalar.activation(a[:, :], a[:, :], ACT.Ln, bias=1.0).then_inc(act_rows, 1)

                with act.Fori(0, NSPLIT // 2) as h:
                    for s in range(2):
                        for c in range(NCH):
                            j = 2 * h + s
                            act.wait_ge(projected, 4 * j + c + 1)
                            act.wait_ge(stored[c % 2], j * split_st + (c // 2) * 32)
                            nc.scalar.activation(stage[c % 2][HI][:, :], cps[c][:, :], ACT.Copy).then_inc(hi_done, 1)
                act.wait_ge(bank_free, 4 * NSPLIT + 4)
                with act.Fori(NSPLIT // 2, (NSPLIT + NGATE) // 2) as h:
                    for s in range(2):
                        for c in range(NCH):
                            j = 2 * h + s
                            act.wait_ge(projected, 4 * j + c + 1)
                            act.wait_ge(stored[c % 2], base_plain + (j - NSPLIT) * plain_st + (c // 2) * 16)
                            nc.scalar.activation(plain[c % 2][:, :], cps[c][:, :], ACT.Silu).then_inc(bank_free, 1)

            @block.vector
            def _(dve):
                dve.sem_inc(bank_free, 4)
                dve.wait_ge(rows_copied, 1)
                dve.wait_ge(rows_loaded, 16)
                nc.vector.tensor_scalar(f, rT[0:FOX_H, :], bf[:, 0:1], None, ALU.add).then_inc(dve_rows, 1)
                dve.wait_ge(dve_rows, 1)
                dve.wait_ge(act_rows, 3)
                nc.vector.scalar_tensor_tensor(f, f, 0.0, a[:, :], ALU.min, ALU.subtract
                                               ).then_inc(dve_rows, 1)
                dve.wait_ge(dve_rows, 2)
                nc.vector.memset(a[:, :], -3e38).then_inc(dve_rows, 1)
                dve.wait_ge(dve_rows, 3)
                nc.vector.tensor_tensor_scan(f, f, a[:, :], 0.0, ALU.add, ALU.max).then_inc(dve_rows, 1)
                with dve.Fori(0, NSPLIT // 2) as h:
                    for s in range(2):
                        for c in range(NCH):
                            j = 2 * h + s
                            dve.wait_ge(hi_done, 4 * j + c + 1)
                            nc.vector.tensor_tensor(stage[c % 2][LO][:, :], cps[c][:, :],
                                                    stage[c % 2][HI][:, :].bitcast(F32), ALU.subtract
                                                    ).then_inc(bank_free, 1)
                dve.wait_ge(bank_free, 4 * (NSPLIT + NGATE) + 4)
                with dve.Fori((NSPLIT + NGATE) // 2, NCOL // 2) as h:
                    for s in range(2):
                        for c in range(NCH):
                            j = 2 * h + s
                            dve.wait_ge(projected, 4 * j + c + 1)
                            dve.wait_ge(stored[c % 2], base_plain + (j - NSPLIT) * plain_st + (c // 2) * 16)
                            nc.vector.tensor_copy(plain[c % 2][:, :], cps[c][:, :]).then_inc(bank_free, 1)




def gated_linear_attention(nc, scr, ident, gla_mask, w_alpha_up, b_alpha, gla_norm_g, next_stages):
    NG, GT = T // CH, CH
    NS = T // P
    ST = CH // P
    HB = 64
    KR = HB + GLA_DK
    W2 = 2 * GLA_DV
    GV = GLA_H * GLA_DV
    RING = 6
    PAIRS = 2
    QKW = GLA_H * GLA_DK
    ctx = ExitStack()
    with ctx:
        k = Pools(nc, ctx, "gla")
        pair_tiles = lambda name, shape, dt=F32: [[k.sb(f"{name}{s}{p}", shape, dt) for p in range(PAIRS)]
                                                  for s in range(2)]
        q, kk = pair_tiles("q", [KR, GT]), pair_tiles("k", [KR, GT])
        qd, kd, kte = (pair_tiles(n, [KR, GT]) for n in ("qd", "kd", "kte"))
        qpad = pair_tiles("qpad", [KR, 2, GT])
        dec = pair_tiles("dec", [KR, GT // GLA_C])
        v = [k.sb(f"v{s}", [GLA_DV, GLA_H, GT]) for s in range(2)]
        lr = [k.sb(f"lr{s}", [GLA_R, GT]) for s in range(2)]
        gate = [k.sb(f"gate{s}", [P, 3, GT]) for s in range(2)]
        keep = k.sb("keep", [KR, GT])
        zabs, la, b, tail, ep, em, ee = (k.sb(n, [KR, GT]) for n in "zabs la b tail ep em ee".split())
        wup = [k.sb(f"wup{p}", [GLA_R, KR]) for p in range(PAIRS)]
        bup = [k.sb(f"bup{p}", [KR, 1]) for p in range(PAIRS)]
        gn = k.sb("gn", [P, 3])
        vt = [k.sb(f"vt{s}", [P, GV]) for s in range(2)]
        vz = k.sb("vz", [P, 2, GV])
        kt = k.sb("kt", [P, PAIRS * KR])
        am = [k.sb(f"am{s}", [P, GLA_H * P]) for s in range(2)]
        S = [[k.sb(f"S{r}{p}", [KR, W2]) for p in range(PAIRS)] for r in range(RING)]
        sqj = k.sb("sqj", [P, GLA_DV])
        ss, ms, rstd, half = (k.sb(n, [P, GLA_H]) for n in ("ss", "ms", "rstd", "half"))
        on = [k.sb(f"on{s}", [P, GV]) for s in range(2)]
        mx = k.sb("mx", [P, 3, P])
        mst = [[k.sb(f"mst{s}{i}", [P, 3, P], F32R) for i in (HI, LO)] for s in range(2)]
        zps = k.ps("zps", [P, CH])
        vps = k.ps("vps", [P, CH])
        kps = k.ps("kps", [P, CH])
        aps = k.ps("aps", [P, CH])
        kvps = [k.ps(f"kvps{p}", [P, CH]) for p in range(PAIRS)]
        ops = k.ps("ops", [P, CH])
        otps = k.ps("otps", [P, CH])
        (k_decayed, qpad_done, pads, w_loaded, gn_loaded, lr_loaded0, lr_loaded1, qk_cleared, cleared, filled,
         qk_loaded0, qk_loaded1, v_loaded0, v_loaded1, gate_loaded0, gate_loaded1, z_done, abs_done,
         min_done, exp_done, ln_done, la_done, scan_done, ep_done, em_done, tail_done, ee_done, qd_done, prep_done,
         gate_ready) = map(
            k.sem, ("k_decayed qpad_done pads w_loaded gn_loaded lr_loaded0 lr_loaded1 qk_cleared cleared filled "
                    "qk_loaded0 qk_loaded1 v_loaded0 v_loaded1 gate_loaded0 gate_loaded1 z_done "
                    "abs_done min_done exp_done ln_done la_done scan_done ep_done em_done tail_done ee_done qd_done "
                    "prep_done gate_ready").split())
        (vT_done, kT_done, attn_done, kv_done, o_done, oT_done, v_copied, k_copied, masked, state_done, squared,
         ms_done, rstd_done, on_done, mixed, mix_hi, mix_lo, stored0, stored1) = map(
            k.sem, ("vT_done kT_done attn_done kv_done o_done oT_done v_copied k_copied masked state_done squared "
                    "ms_done rstd_done on_done mixed mix_hi mix_lo stored0 stored1").split())
        qk_loaded, v_loaded = (qk_loaded0, qk_loaded1), (v_loaded0, v_loaded1)
        gate_loaded = (gate_loaded0, gate_loaded1)
        stored, lr_loaded = (stored0, stored1), (lr_loaded0, lr_loaded1)
        QK_DMAS = 16 * 4 * PAIRS

        def pieces(g, n):
            if g + 1 < NG:
                for piece in ((0,), (1, 2), (3,), ())[n]:
                    yield g + 1, piece // 2, piece % 2

        def first_pieces():
            for p in range(PAIRS):
                for part in range(2):
                    yield 0, p, part

        with nc.Block() as block:
            @block.sync
            def _(sp):
                def load_qk(g):
                    s, cols = g % 2, slice(g * GT, (g + 1) * GT)
                    if g >= 2:
                        sp.wait_ge(prep_done, PAIRS * (g - 1))
                    sp.dma_start(lr[s][:, :], scr.lr[:, cols]).then_inc(lr_loaded[s], 16)
                    if g < 2:
                        sp.wait_ge(qk_cleared, 2 * PAIRS * (g + 1))
                    for p in range(PAIRS):
                        for e in range(2):
                            r = (2 * p + e) * GLA_DK
                            rows = slice(HB * e, HB * e + GLA_DK)
                            sp.dma_start(q[s][p][rows, :], scr.raw[r:r + GLA_DK, cols]).then_inc(qk_loaded[s], 16)
                            sp.dma_start(kk[s][p][rows, :], scr.raw[QKW + r:QKW + r + GLA_DK, cols]
                                         ).then_inc(qk_loaded[s], 16)

                def load_v(g):
                    s, cols = g % 2, slice(g * GT, (g + 1) * GT)
                    if g >= 2:
                        sp.wait_ge(vT_done, ST * (g - 1))
                    sp.dma_start(v[s][:, :, :], scr.raw[2 * QKW:2 * QKW + GV, cols].rearrange("(h d) t -> d h t", d=GLA_DV)
                                 ).then_inc(v_loaded[s], 16)

                def load_gate(g):
                    s, cols = g % 2, slice(g * GT, (g + 1) * GT)
                    if g >= 2:
                        sp.wait_ge(mixed, ST * (g - 1))
                    sp.dma_start(gate[s][:, :, :], scr.gates[0:3, :, cols].rearrange("j p t -> p j t")
                                 ).then_inc(gate_loaded[s], 16)

                def store(N):
                    sp.wait_ge(mix_lo, N + 1)
                    for i in (HI, LO):
                        sp.dma_start(scr.mix[i, N, :, 0:3, :], mst[N % 2][i][:, :, :].bitcast(F32)
                                     ).then_inc(stored[N % 2], 16)
                sp.wait_ge(pads, 2 * PAIRS)
                for p in range(PAIRS):
                    for e in range(2):
                        c = (2 * p + e) * GLA_DK
                        sp.dma_start(wup[p][:, HB * e:HB * e + GLA_DK], w_alpha_up[0, :, c:c + GLA_DK]
                                     ).then_inc(w_loaded, 16)
                load_qk(0)
                ch = 0
                while ch < GV:
                    n = min(P - ch % P, GLA_DV - ch % GLA_DV)
                    sp.dma_start(gn[ch % P:ch % P + n, ch // P:ch // P + 1],
                                 gla_norm_g[0:1, ch % GLA_DV:ch % GLA_DV + n].rearrange("a n -> n a")
                                 ).then_inc(gn_loaded, 16)
                    ch += n
                load_v(0)
                load_gate(0)
                load_qk(1)
                load_v(1)
                load_gate(1)
                for stage in next_stages:
                    stage.first_loads(sp)
                for g in range(NG):
                    for n in range(ST):
                        if g * ST + n >= 2:
                            store(g * ST + n - 2)
                        if n == 0 and g + 2 < NG:
                            load_qk(g + 2)
                        if n == 0 and 2 <= g + 1 < NG:
                            load_v(g + 1)
                        if n == 2 and 2 <= g + 1 < NG:
                            load_gate(g + 1)
                store(NS - 2)
                store(NS - 1)
                for s in range(2):
                    sp.wait_ge(stored[s], 16 * NS)

            @block.tensor
            def _(pe):
                def prep(g, p, part):
                    u = PAIRS * g + p
                    if part:
                        return
                    if p == 0:
                        pe.wait_ge(lr_loaded[g % 2], 16 * (g // 2 + 1))
                    if u:
                        pe.wait_ge(min_done, u)
                        pe.wait_ge(abs_done, u)
                    nc.tensor.matmul(zps[0:KR, :], wup[p][:, :], lr[g % 2][:, :], start=True, stop=True
                                     ).then_inc(z_done, 1)
                pe.wait_ge(cleared, 2)
                pe.wait_ge(w_loaded, 16 * 8)
                for x in first_pieces():
                    prep(*x)

                def outputs(N):
                    s, c0 = (N // ST) % 2, (N % ST) * P
                    if N:
                        pe.wait_ge(on_done, N)
                    pe.wait_ge(masked, N + 1)
                    for p in range(PAIRS):
                        o = ops[:, p * W2:(p + 1) * W2]
                        for e in range(2):
                            m = 2 * N + e
                            if m:
                                pe.wait_ge(state_done, 2 * PAIRS * (m - 1) + 2 * p + 2)
                            nc.tensor.matmul(o[GLA_C * e:GLA_C * (e + 1), :],
                                             qd[s][p][:, c0 + GLA_C * e:c0 + GLA_C * (e + 1)], S[m % RING][p][:, :],
                                             start=True, stop=False, skip_group_check=True)
                        for e in range(2):
                            h = 2 * p + e
                            mm = nc.tensor.matmul(o[:, e * GLA_DV:(e + 1) * GLA_DV], am[N % 2][:, h * P:(h + 1) * P],
                                                  vt[N % 2][:, h * GLA_DV:(h + 1) * GLA_DV],
                                                  start=False, stop=True, skip_group_check=True)
                    mm.then_inc(o_done, 1)

                def transposed_outputs(N):
                    pe.wait_ge(on_done, N + 1)
                    if N:
                        pe.wait_ge(mixed, N)
                    for j in range(3):
                        mm = nc.tensor.transpose(otps[:, j * P:(j + 1) * P], on[N % 2][:, j * P:(j + 1) * P], ident[:, :])
                    mm.then_inc(oT_done, 1)

                for g in range(NG):
                    s = g % 2
                    for n in range(ST):
                        N, cols = g * ST + n, slice(n * P, (n + 1) * P)
                        if n == 0:
                            pe.wait_ge(v_loaded[s], 16 * (g // 2 + 1))
                            pe.wait_ge(prep_done, PAIRS * (g + 1))
                            pe.wait_ge(filled, 1)
                        if N:
                            pe.wait_ge(v_copied, 3 * N)
                        for h in range(GLA_H):
                            mm = nc.tensor.transpose(vps[:, h * GLA_DV:(h + 1) * GLA_DV], v[s][:, h, cols],
                                                     ident[0:GLA_DV, 0:GLA_DV])
                        mm.then_inc(vT_done, 1)
                        if N:
                            pe.wait_ge(k_copied, N)
                        for p in range(PAIRS):
                            mm = nc.tensor.transpose(kps[:, p * KR:(p + 1) * KR], kte[s][p][:, cols], ident[0:KR, 0:KR])
                        mm.then_inc(kT_done, 1)
                        if N:
                            pe.wait_ge(masked, N)
                        for p in range(PAIRS):
                            mm = nc.tensor.matmul(aps[:, p * 2 * P:(p + 1) * 2 * P], kd[s][p][:, cols],
                                                  qpad[s][p][:, :, cols], start=True, stop=True)
                        mm.then_inc(attn_done, 1)
                        if N:
                            outputs(N - 1)
                        pe.wait_ge(v_copied, 3 * (N + 1))
                        pe.wait_ge(k_copied, N + 1)
                        for p in range(PAIRS):
                            if N:
                                pe.wait_ge(state_done, 4 * PAIRS * (N - 1) + 2 * PAIRS + 2 * p + 2)
                            nc.tensor.matmul(kvps[p][0:KR, 0:2 * W2], kt[:, p * KR:(p + 1) * KR],
                                             vz[:, :, p * W2:(p + 1) * W2], start=True, stop=True
                                             ).then_inc(kv_done, 1)
                        if N >= 2:
                            transposed_outputs(N - 2)
                        for x in pieces(g, n):
                            prep(*x)
                outputs(NS - 1)
                transposed_outputs(NS - 2)
                transposed_outputs(NS - 1)

            @block.scalar
            def _(act):
                def prep(g, p, part):
                    u = PAIRS * g + p
                    if part == 0:
                        act.wait_ge(z_done, u + 1)
                        if u:
                            act.wait_ge(la_done, u)
                        nc.scalar.activation(zabs[:, :], zps[0:KR, :], ACT.Abs, bias=bup[p][:, 0:1]).then_inc(abs_done, 1)
                        act.wait_ge(abs_done, u + 1)
                        nc.scalar.activation(zabs[:, :], zabs[:, :], ACT.Exp, scale=-1.0).then_inc(exp_done, 1)
                        act.wait_ge(exp_done, u + 1)
                        nc.scalar.activation(zabs[:, :], zabs[:, :], ACT.Ln, bias=1.0).then_inc(ln_done, 1)
                    else:
                        act.wait_ge(scan_done, u + 1)
                        if u:
                            act.wait_ge(prep_done, u)
                        gs = 1.0 / GLA_GATE
                        nc.scalar.activation(ep[:, :], b[:, :], ACT.Exp, scale=gs).then_inc(ep_done, 1)
                        nc.scalar.activation(em[:, :], b[:, :], ACT.Exp, scale=-gs).then_inc(em_done, 1)
                        act.wait_ge(tail_done, u + 1)
                        nc.scalar.activation(ee[:, :], tail[:, :], ACT.Exp, scale=gs).then_inc(ee_done, 1)
                act.wait_ge(pads, 2 * PAIRS)
                for p in range(PAIRS):
                    for e in range(2):
                        c = (2 * p + e) * GLA_DK
                        act.dma_start(bup[p][HB * e:HB * e + GLA_DK, :],
                                      b_alpha[0:1, c:c + GLA_DK].rearrange("a n -> n a")).then_inc(w_loaded, 16)
                act.wait_ge(w_loaded, 16 * 8)
                act.wait_ge(cleared, 2)
                for x in first_pieces():
                    prep(*x)

                def squares(N):
                    act.wait_ge(o_done, N + 1)
                    if N:
                        act.wait_ge(ms_done, N)
                    for h in range(GLA_H):
                        nc.scalar.activation(sqj[:, :], ops[:, h * GLA_DV:(h + 1) * GLA_DV], ACT.Square,
                                             accum_out=ss[:, h:h + 1]).then_inc(squared, 1)
                        act.wait_ge(squared, GLA_H * N + h + 1)

                act.wait_ge(filled, 1)
                for g in range(NG):
                    for n in range(ST):
                        N = g * ST + n
                        act.wait_ge(vT_done, N + 1)
                        if N >= 2:
                            act.wait_ge(o_done, N - 1)
                        nc.scalar.activation(vt[N % 2][:, :], vps[:, 0:GV], ACT.Copy).then_inc(v_copied, 1)
                        if N:
                            act.wait_ge(kv_done, PAIRS * N)
                        for e in range(2):
                            rows = slice(GLA_C * e, GLA_C * (e + 1))
                            nc.scalar.activation(vz[rows, e, :], vps[rows, 0:GV], ACT.Copy).then_inc(v_copied, 1)
                        act.wait_ge(kT_done, N + 1)
                        nc.scalar.activation(kt[:, :], kps[:, 0:PAIRS * KR], ACT.Copy).then_inc(k_copied, 1)
                        if N:
                            squares(N - 1)
                        for x in pieces(g, n):
                            prep(*x)
                squares(NS - 1)

            @block.vector
            def _(dve):
                def prep(g, p, part):
                    u, s = PAIRS * g + p, g % 2
                    if part == 0:
                        dve.wait_ge(z_done, u + 1)
                        dve.wait_ge(abs_done, u + 1)
                        if u:
                            dve.wait_ge(scan_done, u)
                        nc.vector.tensor_scalar(la[:, :], zps[0:KR, :], bup[p][:, 0:1], 0.0, ALU.add, ALU.min
                                                ).then_inc(min_done, 1)
                        dve.wait_ge(min_done, u + 1)
                        dve.wait_ge(ln_done, u + 1)
                        nc.vector.tensor_tensor(la[:, :], la[:, :], zabs[:, :], ALU.subtract).then_inc(la_done, 1)
                        dve.wait_ge(la_done, u + 1)
                        if u:
                            dve.wait_ge(em_done, u)
                            dve.wait_ge(tail_done, u)
                        nc.vector.tensor_tensor_scan(b[:, :], keep[:, :], la[:, :], 0.0, ALU.mult, ALU.add
                                                     ).then_inc(scan_done, 1)
                        dve.wait_ge(scan_done, u + 1)
                        if u:
                            dve.wait_ge(ee_done, u)
                        bc = b[:, :].rearrange("p (n c) -> p n c", c=GLA_C)
                        nc.vector.tensor_tensor(tail[:, :].rearrange("p (n c) -> p n c", c=GLA_C),
                                                bc[:, :, GLA_C - 1:GLA_C].to_broadcast([KR, GT // GLA_C, GLA_C]), bc,
                                                ALU.subtract).then_inc(tail_done, 1)
                    else:
                        dve.wait_ge(qk_loaded[s], QK_DMAS * (g // 2 + 1))
                        dve.wait_ge(ep_done, u + 1)
                        if g >= 2:
                            dve.wait_ge(o_done, ST * (g - 1))
                            dve.wait_ge(attn_done, ST * (g - 1))
                        nc.vector.scalar_tensor_tensor(qd[s][p][:, :], q[s][p][:, :], GLA_DK ** -0.5, ep[:, :],
                                                       ALU.mult, ALU.mult).then_inc(qd_done, 1)
                        dve.wait_ge(qd_done, u + 1)
                        if not u:
                            dve.wait_ge(filled, 1)
                        for e in range(2):
                            rows = slice(HB * e, HB * e + GLA_DK)
                            nc.vector.tensor_copy(qpad[s][p][rows, e, :], qd[s][p][rows, :]).then_inc(qpad_done, 1)
                for s in range(2):
                    for p in range(PAIRS):
                        nc.vector.memset(q[s][p][:, :], 0.0).then_inc(qk_cleared, 1)
                        nc.vector.memset(kk[s][p][:, :], 0.0).then_inc(qk_cleared, 1)
                dve.wait_ge(cleared, 2)
                dve.wait_ge(w_loaded, 16 * 8)
                for x in first_pieces():
                    prep(*x)
                for stage in next_stages:
                    stage.first_fill(nc.vector)

                def means(N):
                    dve.wait_ge(squared, GLA_H * (N + 1))
                    nc.vector.tensor_scalar(ms[:, :], ss[:, :], 1.0 / GLA_DV, EPS, ALU.mult, ALU.add).then_inc(ms_done, 1)

                def normed(N):
                    dve.wait_ge(rstd_done, N + 1)
                    if N >= 2:
                        dve.wait_ge(oT_done, N - 1)
                    nc.vector.tensor_tensor(on[N % 2][:, :].rearrange("p (h d) -> p h d", d=GLA_DV),
                                            ops[:, 0:GV].rearrange("p (h d) -> p h d", d=GLA_DV),
                                            rstd[:, :].unsqueeze(2).to_broadcast([P, GLA_H, GLA_DV]), ALU.mult
                                            ).then_inc(on_done, 1)

                def gated(N):
                    g, c0 = N // ST, (N % ST) * P
                    dve.wait_ge(oT_done, N + 1)
                    dve.wait_ge(gate_ready, 3 * (g + 1))
                    if N:
                        dve.wait_ge(mix_lo, N)
                    nc.vector.tensor_tensor(mx[:, :, :], otps[:, 0:3 * P].rearrange("p (j t) -> p j t", t=P),
                                            gate[g % 2][:, :, c0:c0 + P], ALU.mult).then_inc(mixed, 1)

                for g in range(NG):
                    s = g % 2
                    for n in range(ST):
                        N = g * ST + n
                        dve.wait_ge(attn_done, N + 1)
                        if N >= 2:
                            dve.wait_ge(o_done, N - 1)
                        nc.vector.tensor_tensor(am[N % 2][:, :], aps[:, :], gla_mask[:, :, :].rearrange("p h t -> p (h t)"),
                                                ALU.mult).then_inc(masked, 1)
                        if N:
                            means(N - 1)
                        if n == 0:
                            dve.wait_ge(prep_done, PAIRS * (g + 1))
                        for e in range(2):
                            m = 2 * N + e
                            for p in range(PAIRS):
                                if e == 0:
                                    dve.wait_ge(kv_done, PAIRS * N + p + 1)
                                if m:
                                    dve.wait_ge(state_done, 2 * PAIRS * (m - 1) + 2 * p + 2)
                                for a in range(2):
                                    rows = slice(HB * a, HB * a + GLA_DK)
                                    cols = slice(a * GLA_DV, (a + 1) * GLA_DV)
                                    nc.vector.scalar_tensor_tensor(
                                        S[(m + 1) % RING][p][rows, cols], S[m % RING][p][rows, cols],
                                        dec[s][p][rows, 2 * n + e:2 * n + e + 1],
                                        kvps[p][rows, e * W2 + a * GLA_DV:e * W2 + (a + 1) * GLA_DV],
                                        ALU.mult, ALU.add).then_inc(state_done, 1)
                        if N:
                            normed(N - 1)
                        if N >= 2:
                            gated(N - 2)
                        for x in pieces(g, n):
                            prep(*x)
                means(NS - 1)
                normed(NS - 1)
                gated(NS - 2)
                gated(NS - 1)

            @block.gpsimd
            def _(pool):
                for p in range(PAIRS):
                    pool.memset(wup[p][:, :], 0.0).then_inc(pads, 1)
                    pool.memset(bup[p][:, :], 0.0).then_inc(pads, 1)
                pool.memset(keep[:, :], 1.0).then_inc(cleared, 1)
                pool.wait_ge(cleared, 1)
                pool.memset(keep[:, :].rearrange("p (n c) -> p n c", c=GLA_C)[:, :, 0:1], 0.0).then_inc(cleared, 1)
                pool.wait_ge(cleared, 2)
                for p in range(PAIRS):
                    pool.memset(qpad[0][p][:, :, :], 0.0)
                    pool.memset(qpad[1][p][:, :, :], 0.0)
                    for r in range(RING):
                        pool.memset(S[r][p][:, :], 0.0)
                pool.memset(vz[:, :, :], 0.0)
                pool.memset(half[:, :], -0.5).then_inc(filled, 1)
                pool.wait_ge(filled, 1)

                def prep(g, p, part):
                    u, s = PAIRS * g + p, g % 2
                    if part == 0:
                        return
                    if p == 0:
                        pool.wait_ge(qk_loaded[s], QK_DMAS * (g // 2 + 1))
                    if g >= 2:
                        pool.wait_ge(attn_done, ST * (g - 1))
                        pool.wait_ge(kT_done, ST * (g - 1))
                        pool.wait_ge(state_done, 4 * PAIRS * ST * (g - 1))
                    pool.wait_ge(em_done, u + 1)
                    nc.gpsimd.tensor_tensor(kd[s][p][:, :], kk[s][p][:, :], em[:, :], ALU.mult).then_inc(k_decayed, 1)
                    pool.wait_ge(ee_done, u + 1)
                    nc.gpsimd.tensor_tensor(kte[s][p][:, :], kk[s][p][:, :], ee[:, :], ALU.mult).then_inc(k_decayed, 1)
                    pool.wait_ge(k_decayed, 2 * u + 2)
                    pool.wait_ge(qpad_done, 2 * u + 2)
                    nc.gpsimd.tensor_copy(dec[s][p][:, :].unsqueeze(2),
                                          ep[:, :].rearrange("p (n c) -> p n c", c=GLA_C)[:, :, GLA_C - 1:GLA_C]
                                          ).then_inc(prep_done, 1)

                def gates(g):
                    s = g % 2
                    pool.wait_ge(gn_loaded, 16 * 6)
                    pool.wait_ge(gate_loaded[s], 16 * (g // 2 + 1))
                    for j in range(3):
                        nc.gpsimd.tensor_scalar(gate[s][:, j, :], gate[s][:, j, :], gn[:, j:j + 1], 1.0,
                                                ALU.mult, ALU.mult).then_inc(gate_ready, 1)
                for x in first_pieces():
                    prep(*x)
                gates(0)

                def rstds(N):
                    pool.wait_ge(ms_done, N + 1)
                    if N:
                        pool.wait_ge(on_done, N)
                    nc.gpsimd.tensor_tensor(rstd[:, :], ms[:, :], half[:, :], ALU.pow).then_inc(rstd_done, 1)

                def split(N):
                    pool.wait_ge(mixed, N + 1)
                    if N >= 2:
                        pool.wait_ge(stored[N % 2], 32 * (N // 2))
                    nc.gpsimd.tensor_scalar(mst[N % 2][HI][:, :, :], mx[:, :, :], 1.0, 1.0, ALU.mult, ALU.mult
                                            ).then_inc(mix_hi, 1)
                    pool.wait_ge(mix_hi, N + 1)
                    nc.gpsimd.tensor_tensor(mst[N % 2][LO][:, :, :], mx[:, :, :], mst[N % 2][HI][:, :, :].bitcast(F32),
                                            ALU.subtract).then_inc(mix_lo, 1)
                for g in range(NG):
                    for n in range(ST):
                        N = g * ST + n
                        if N:
                            rstds(N - 1)
                        if N >= 2:
                            split(N - 2)
                        if n == 3 and g + 1 < NG:
                            gates(g + 1)
                        for x in pieces(g, n):
                            prep(*x)
                rstds(NS - 1)
                split(NS - 2)
                split(NS - 1)


class Ring:

    def __init__(self, it, per):
        self.it, self.per = it, per

    def at(self, n):
        return self.it * self.per + n


class HeadTiles:

    def __init__(self, nc, ctx, scr, fox, e=0):
        self.scr, self.fox, self.e = scr, fox, e
        self.FILLS = 2 if fox else 1
        k = Pools(nc, ctx, f"{'fox' if fox else 'att'}{e}")
        W = T if fox else M
        self.qa = k.sb("qa", [P, T], F32R)
        self.qb = k.sb("qb", [P, T], F32R) if fox else self.qa
        self.ka, self.kb = k.sb("ka", [P, W], F32R), k.sb("kb", [P, W], F32R)
        self.v = k.sb("v", [P, W // P, 2 * DH], F32R)
        self.zeroed, self.filled = k.sem("zeroed"), k.sem("filled")
        self.pieces = 1 if e else NCH
        self.loaded = [k.sem(f"loaded{g}") for g in range(self.pieces)]

    def loads_of(self, g):
        return 9 if self.fox else 6 if g == 0 else 2

    def first_fill(self, eng):
        low = slice(DH, P)
        if self.fox:
            eng.memset(self.kb[low, :].bitcast(F32), 0.0).then_inc(self.zeroed, 1)
            eng.memset(self.qb[low, :].bitcast(F32), 1.0).then_inc(self.filled, 1)
            eng.wait_ge(self.zeroed, 1)
            eng.memset(self.kb[DH:DH + 4, :].bitcast(F32), 1.0).then_inc(self.filled, 1)
        else:
            eng.memset(self.kb[low, :].bitcast(F32), 0.0).then_inc(self.filled, 1)

    def first_loads(self, sp):
        sp.wait_ge(self.filled, self.FILLS)
        for g in range(self.pieces):
            self.load_qk(sp, 0, g)
            self.load_v(sp, 0, g)

    def send(self, sp, g, dst, src):
        sp.dma_start(dst.bitcast(F32), src).then_inc(self.loaded[g], 16)

    def load_v(self, sp, r, g):
        head, v, scr = bass.ds(2 * r + self.e, 1), self.v, self.scr
        if self.fox:
            n = TT // self.pieces
            blocks = slice(n * g, n * (g + 1))
            self.send(sp, g, v[:, blocks, :], scr.fox_v[head, :, blocks, :].rearrange("a p b c -> (a p) b c"))
        elif g == 0:
            self.send(sp, g, v[:, :, :], scr.mem_v[head].rearrange("a p b c -> (a p) b c"))

    def load_qk(self, sp, r, g):
        scr, fox, e, qa, qb, ka, kb = self.scr, self.fox, self.e, self.qa, self.qb, self.ka, self.kb
        qt = r + (0 if fox else 3)
        rows = slice(DH * e, DH * (e + 1))
        top, bottom = slice(0, DH), slice(DH, P)
        w = T // self.pieces
        cols = slice(w * g, w * (g + 1))

        def part(tile, i):
            return scr.split[bass.ds(tile, 1), i, rows, cols].rearrange("a p t -> (a p) t")
        loads = [(qa[top, cols], part(qt, HI)), (qa[bottom, cols], part(qt, LO))]
        if fox:
            head = bass.ds(2 * r + e, 1)
            loads += [(ka[top, cols], part(r + 5, LO)), (ka[bottom, cols], part(r + 5, HI)),
                      (qb[top, cols], part(qt, HI)), (kb[top, cols], part(r + 5, HI)),
                      (qb[DH + 2:DH + 4, cols], scr.crow[0:2, head, cols].rearrange("i a t -> (i a) t")),
                      (kb[DH:DH + 2, cols], scr.crow[2:4, head, cols].rearrange("i a t -> (i a) t"))]
        elif g == 0:
            def key(i):
                return scr.mem_k[bass.ds(r, 1), i, rows, :].rearrange("a p t -> (a p) t")
            loads += [(ka[top, :], key(LO)), (ka[bottom, :], key(HI)), (kb[top, :], key(HI))]
        for dst, src in loads:
            self.send(sp, g, dst, src)



def softmax_attention(nc, scr, ident, ident_b, mask, first, next_stages):
    fox = first.fox
    tag = "fox" if fox else "att"
    W = T if fox else M
    NB = W // P
    NG = T // CH
    ROUNDS = (FOX_H if fox else MEM_H) // 2
    SCALE = DH ** -0.5
    QT = CH // P
    PT = 4
    DEPTH = PT - 1 if fox else PT - 3
    AUX = DH

    def score_units(hd, g):
        for i in range(CH // P):
            if fox:
                for c in range(g + 1):
                    yield hd, g, i, c, CH if c < g else P * (i + 1)
            else:
                yield hd, g, i, 0, W

    def key_units(hd, g):
        for j in range(4 * (g + 1) if fox else NB):
            yield hd, g, j, max(0, j - 4 * g) if fox else 0

    turns = [(0, g) for g in range(NG)] + [(1, g) for g in reversed(range(NG))]
    keys_of = lambda g: CH * (g + 1) if fox else W
    ctx = ExitStack()
    with ctx:
        k = Pools(nc, ctx, tag)
        second = HeadTiles(nc, ctx, scr, fox, e=1)
        heads = (first, second)
        qa, qb, ka, kb, v = ([getter(x) for x in heads] for getter in (
            lambda x: x.qa, lambda x: x.qb, lambda x: x.ka, lambda x: x.kb, lambda x: x.v))
        prob = [k.sb(f"prob{b}", [P, QT, W]) for b in range(2)]
        pT = [[k.sb(f"pT{b}{i}", [P, CH], F32R) for i in (HI, LO)] for b in range(PT)]
        nmax = [k.sb(f"nmax{b}", [P, CH // P, 4]) for b in range(2)]
        nm = [k.sb(f"nm{b}", [P, CH // P]) for b in range(2)]
        rsum = [k.sb(f"rsum{b}", [P, CH // P]) for b in range(2)]
        rinv = [k.sb(f"rinv{b}", [P, CH // P]) for b in range(2)]
        gate = [k.sb(f"gate{b}", [DH, CH]) for b in range(2)]
        low = k.sb("low", [DH, CH])
        scale = [k.sb(f"scale{b}", [DH, CH]) for b in range(2)]
        o = [k.sb(f"o{b}", [DH, CH]) for b in range(2)]
        om = [[k.sb(f"om{b}{i}", [DH, CH], F32R) for i in (HI, LO)] for b in range(2)]
        sps = [k.ps(f"sps{b}", [P, CH]) for b in range(2)]
        tps = [k.ps(f"tps{b}", [P, CH]) for b in range(3)]
        ops = [k.ps(f"ops{b}", [P, CH]) for b in range(2)]
        rps = k.ps("rps", [P, CH])
        names = ("pool_goes gate_scaled gate_loaded0 gate_loaded1 scored negated maxed expd transposed pt_hi pt_lo "
                 "weighed inverted spread low_done added scaled gated o_hi o_lo stored0 stored1 sp_goes").split()
        (pool_goes, gate_scaled, gate_loaded0, gate_loaded1, scored, negated, maxed, expd, transposed, pt_hi, pt_lo,
         weighed, inverted, spread, low_done, added, scaled, gated, o_hi, o_lo, stored0, stored1, sp_goes) = map(k.sem, names)
        gate_loaded, stored = (gate_loaded0, gate_loaded1), (stored0, stored1)

        n_scores = sum(len(list(score_units(*t))) for t in turns)
        n_keys = sum(len(list(key_units(*t))) for t in turns)
        n_turns = len(turns)

        def at_turn(t):
            return (sum(len(list(score_units(*x))) for x in turns[:t]),
                    sum(len(list(key_units(*x))) for x in turns[:t]))

        def plan(t, last):
            units = list(key_units(*turns[t]))
            ahead = [] if last and t + 1 == n_turns else list(score_units(*turns[(t + 1) % n_turns]))
            done, tiles, out = 0, 0, []
            for m in range(len(units)):
                upto = min(len(ahead), -(-len(ahead) * (m + 1) * (4 if fox else 3) // (3 * len(units))))
                ready = (done if fox and m + 1 < len(units) else upto) * QT // len(ahead) if ahead else 0
                out.append((units[m], list(range(done, upto)), list(range(tiles, ready))))
                done, tiles = upto, ready
            return ahead, out

        def ends(t, m):
            return t >= 1 and m == (3 if fox else 1)

        def rounds(eng, round_):
            with eng.Fori(0, ROUNDS - 1) as r:
                round_(r, False)
            round_(ROUNDS - 1, True)

        with nc.Block() as block:
            @block.sync
            def _(sp):
                def load_gate(r, t):
                    e, g = turns[t]
                    src = scr.gates[bass.ds(r + (3 if fox else 6), 1), DH * e:DH * (e + 1), g * CH:(g + 1) * CH]
                    sp.dma_start(gate[t % 2][:, :], src.rearrange("a p t -> (a p) t")).then_inc(gate_loaded[t % 2], 16)
                load_gate(0, 0)
                load_gate(0, 1)
                second.first_loads(sp)
                for stage in next_stages:
                    stage.first_loads(sp)

                def round_(r, last):
                    for t, (e, g) in enumerate(turns):
                        sp.wait_ge(o_lo, r * n_turns + t + 1)
                        sp.sem_inc(sp_goes, 1)
                        for i in (HI, LO):
                            dst = scr.mix[i, 4 * g:4 * g + 4, DH * e:DH * (e + 1), bass.ds(r + (3 if fox else 6), 1), :]
                            sp.dma_start(dst.rearrange("a p b t -> p a (b t)"),
                                         om[t % 2][i][:, :].rearrange("p (a t) -> p a t", t=P).bitcast(F32)
                                         ).then_inc(stored[t % 2], 16)
                        if t + 2 < n_turns:
                            load_gate(r, t + 2)
                        elif not last:
                            load_gate(r + 1, t + 2 - n_turns)
                        if not last and t + 2 in (n_turns // 2, n_turns):
                            sp.wait_ge(scored, r * n_scores + at_turn(t + 2)[0])
                            sp.sem_inc(sp_goes, 1)
                            for piece in range(heads[e].pieces):
                                heads[e].load_qk(sp, r + 1, piece)
                        if not last and t + 1 in (n_turns // 2, n_turns):
                            for piece in range(heads[e].pieces):
                                heads[e].load_v(sp, r + 1, piece)
                rounds(sp, round_)
                for b in range(2):
                    sp.wait_ge(stored[b], 16 * ROUNDS * n_turns)

            @block.tensor
            def _(pe):
                def round_(r, last, prologue=False):
                    S, K, G, E = Ring(r, n_scores), Ring(r, n_keys), Ring(r, n_turns), Ring(r, QT * n_turns)

                    def scores(u, n):
                        e, g, i, c, w = u
                        if i == 0 and c == 0 and e == 0:
                            pe.wait_ge(first.loaded[g], (r + 1 + n // n_scores) * 16 * first.loads_of(g))
                        if n == n_scores // 2:
                            pe.wait_ge(second.loaded[0], (r + 1) * 16 * second.loads_of(0))
                        if n >= 2:
                            pe.wait_ge(negated, S.at(n - 1))
                        qcols = slice((4 * g + i) * P, (4 * g + i + 1) * P)
                        wide = max(w, 2 * P)
                        kcols = slice(c * CH, c * CH + wide)
                        diagonal = fox and c == g
                        nc.tensor.matmul(sps[n % 2][:, 0:wide], qa[e][:, qcols], ka[e][:, kcols],
                                         start=True, stop=False)
                        if diagonal:
                            nc.tensor.matmul(sps[n % 2][:, w - P:w], ident_b[:, :], mask[:, :],
                                             start=False, stop=False, skip_group_check=True)
                        mm = nc.tensor.matmul(sps[n % 2][:, 0:wide], qb[e][:, qcols], kb[e][:, kcols],
                                              start=False, stop=True)
                        mm.then_inc(scored, 1)

                    def transposes(u, n, t, q0):
                        e, g, j, i0 = u
                        pe.wait_ge(pt_lo, K.at(n - 2 if n >= 3 else 0))
                        for i in range(i0, QT):
                            if q0:
                                pe.wait_ge(expd, E.at(QT * t + i + 1))
                            mm = nc.tensor.transpose(tps[n % 3][:, i * P:(i + 1) * P],
                                                     prob[t % 2][:, i, j * P:(j + 1) * P], ident[:, :])
                        mm.then_inc(transposed, 1)

                    def weigh(u, n, t, first, last):
                        e, g, j, i0 = u
                        if first:
                            pe.wait_ge(added, G.at(max(t - 1, 0)))
                        for i in (HI, LO):
                            if i == HI:
                                pe.wait_ge(pt_hi, K.at(n + 1))
                            else:
                                pe.wait_ge(pt_lo, K.at(n + 1))
                            mm = nc.tensor.matmul(ops[t % 2][:, i0 * P:CH], v[e][:, j, :], pT[n % PT][i][:, i0 * P:CH],
                                                  start=(first and i == HI), stop=(last and i == LO),
                                                  skip_group_check=True)
                        mm.then_inc(weighed, 1)

                    def spread_sums(t):
                        pe.wait_ge(inverted, G.at(t + 1))
                        pe.wait_ge(scaled, G.at(t))
                        for i in range(4):
                            mm = nc.tensor.matmul(rps[0:DH, i * P:(i + 1) * P],
                                                  rinv[t % 2][:, i:i + 1].to_broadcast([P, DH]), ident[:, :],
                                                  start=True, stop=True)
                        mm.then_inc(spread, 1)

                    if prologue:
                        for n, u in enumerate(score_units(*turns[0])):
                            scores(u, n)
                        return
                    waiting = []
                    for t in range(n_turns):
                        k0, s1 = at_turn(t)[1], at_turn(t + 1)[0]
                        ahead, steps = plan(t, last)
                        for m, (u, made, _) in enumerate(steps):
                            transposes(u, k0 + m, t, m == 0)
                            for a in made:
                                scores(ahead[a], s1 + a)
                            waiting.append((u, k0 + m, t, m == 0, m == len(steps) - 1))
                            if len(waiting) > DEPTH:
                                weigh(*waiting.pop(0))
                            if ends(t, m):
                                spread_sums(t - 1)
                    for x in waiting:
                        weigh(*x)
                    spread_sums(n_turns - 1)
                round_(0, False, prologue=True)
                rounds(pe, round_)

            @block.scalar
            def _(act):
                def round_(r, last, prologue=False):
                    K, G, E = Ring(r, n_keys), Ring(r, n_turns), Ring(r, QT * n_turns)

                    def exponentials(t, i):
                        w = keys_of(turns[t % n_turns][1]) - (CH - P * (i + 1) if fox else 0)
                        act.wait_ge(maxed, E.at(QT * t + i + 1))
                        nc.scalar.activation(prob[t % 2][:, i, 0:w], prob[t % 2][:, i, 0:w], ACT.Exp,
                                             bias=nm[t % 2][:, i:i + 1], scale=-1.0,
                                             accum_out=rsum[t % 2][:, i:i + 1]).then_inc(expd, 1)

                    def pt_high(u, n):
                        e, g, j, i0 = u
                        act.wait_ge(transposed, K.at(n + 1))
                        act.wait_ge(weighed, K.at(max(n - PT + 1, 0)))
                        nc.scalar.activation(pT[n % PT][HI][:, i0 * P:CH], tps[n % 3][:, i0 * P:CH], ACT.Copy
                                             ).then_inc(pt_hi, 1)

                    def low_half(t):
                        act.wait_ge(weighed, K.at(at_turn(t + 1)[1]))
                        act.wait_ge(added, G.at(t))
                        nc.scalar.activation(low[:, :], ops[t % 2][DH:P, :], ACT.Copy).then_inc(low_done, 1)
                        act.wait_ge(spread, G.at(t + 1))
                        act.wait_ge(o_lo, G.at(max(t - 1, 0)))
                        nc.scalar.activation(scale[t % 2][:, :], rps[0:DH, :], ACT.Copy).then_inc(scaled, 1)

                    if prologue:
                        for i in range(QT):
                            exponentials(0, i)
                        return
                    for t in range(n_turns):
                        k0 = at_turn(t)[1]
                        for m, (u, _, tiles) in enumerate(plan(t, last)[1]):
                            pt_high(u, k0 + m)
                            for i in tiles:
                                exponentials(t + 1, i)
                            if ends(t, m):
                                low_half(t - 1)
                    low_half(n_turns - 1)
                round_(0, False, prologue=True)
                rounds(act, round_)

            @block.vector
            def _(dve):
                def round_(r, last, prologue=False):
                    S, K, G, E = Ring(r, n_scores), Ring(r, n_keys), Ring(r, n_turns), Ring(r, QT * n_turns)

                    def negate(u, n, t):
                        e, g, i, c, w = u
                        dve.wait_ge(scored, S.at(n + 1))
                        if t >= 1 and i == 0 and c == 0:
                            dve.wait_ge(transposed, K.at(at_turn(t - 1)[1]))
                        nc.vector.tensor_scalar(prob[t % 2][:, i, c * CH:c * CH + w], sps[n % 2][:, 0:w], -SCALE, None,
                                                ALU.mult, ALU.min, accum_out=nmax[t % 2][:, i, c:c + 1]
                                                ).then_inc(negated, 1)
                        if c == (g if fox else 0):
                            dve.wait_ge(negated, S.at(n + 1))
                            nc.vector.tensor_reduce(nm[t % 2][:, i:i + 1], nmax[t % 2][:, i, 0:c + 1], AX.X, ALU.min
                                                    ).then_inc(maxed, 1)

                    def pt_low(u, n):
                        e, g, j, i0 = u
                        dve.wait_ge(pt_hi, K.at(n + 1))
                        nc.vector.tensor_tensor(pT[n % PT][LO][:, i0 * P:CH], tps[n % 3][:, i0 * P:CH],
                                                pT[n % PT][HI][:, i0 * P:CH].bitcast(F32), ALU.subtract
                                                ).then_inc(pt_lo, 1)

                    def invert(t):
                        dve.wait_ge(expd, E.at(QT * (t + 1)))
                        dve.wait_ge(spread, G.at(max(t - 1, 0)))
                        nc.vector.reciprocal(rinv[t % 2][:, :], rsum[t % 2][:, :]).then_inc(inverted, 1)

                    def add(t):
                        dve.wait_ge(low_done, G.at(t + 1))
                        dve.wait_ge(o_lo, G.at(max(t - 1, 0)))
                        nc.vector.tensor_tensor(o[t % 2][:, :], ops[t % 2][0:DH, :], low[:, :], ALU.add
                                                ).then_inc(added, 1)

                    if prologue:
                        for n, u in enumerate(score_units(*turns[0])):
                            negate(u, n, 0)
                        return
                    for t in range(n_turns):
                        k0, s1 = at_turn(t)[1], at_turn(t + 1)[0]
                        ahead, steps = plan(t, last)
                        invert(t)
                        for m, (u, made, _) in enumerate(steps):
                            for a in made:
                                negate(ahead[a], s1 + a, t + 1)
                            pt_low(u, k0 + m)
                            if ends(t, m):
                                add(t - 1)
                    add(n_turns - 1)
                round_(0, False, prologue=True)
                rounds(dve, round_)

            @block.gpsimd
            def _(pool):
                second.first_fill(pool)
                pool.wait_ge(second.filled, second.FILLS)

                def round_(r, last):
                    G = Ring(r, n_turns)

                    def gated_output(t):
                        b = t % 2
                        pool.wait_ge(gate_loaded[b], 16 * (r * (n_turns // 2) + t // 2 + 1))
                        pool.wait_ge(scaled, G.at(t + 1))
                        nc.gpsimd.tensor_tensor(gate[b][:, :], scale[b][:, :], gate[b][:, :], ALU.mult
                                                ).then_inc(gate_scaled, 1)
                        pool.wait_ge(gate_scaled, G.at(t + 1))
                        pool.wait_ge(added, G.at(t + 1))
                        nc.gpsimd.tensor_tensor(o[b][:, :], o[b][:, :], gate[b][:, :], ALU.mult).then_inc(gated, 1)
                        pool.wait_ge(gated, G.at(t + 1))
                        pool.wait_ge(stored[b], 32 * (r * (n_turns // 2) + t // 2))
                        pool.sem_inc(pool_goes, 1)
                        nc.gpsimd.tensor_scalar(om[b][HI][:, :], o[b][:, :], 1.0, 1.0, ALU.mult, ALU.mult).then_inc(o_hi, 1)
                        pool.wait_ge(o_hi, G.at(t + 1))
                        nc.gpsimd.tensor_tensor(om[b][LO][:, :], o[b][:, :], om[b][HI][:, :].bitcast(F32),
                                                ALU.subtract).then_inc(o_lo, 1)
                    for t in range(n_turns):
                        for m, (u, _, _) in enumerate(plan(t, last)[1]):
                            if ends(t, m):
                                gated_output(t - 1)
                    gated_output(n_turns - 1)
                rounds(pool, round_)




class OutWeights:

    RAW = 3

    def __init__(self, nc, ctx, w_out, final_norm_g):
        self.w_out, self.final_norm_g = w_out, final_norm_g
        k = Pools(nc, ctx, "outw")
        self.g = k.sb("g", [P, D])
        self.raw = [k.sb(f"raw{s}", [P, D]) for s in range(self.RAW)]
        self.loaded, self.g_loaded = [k.sem(f"loaded{s}") for s in range(self.RAW)], k.sem("g_loaded")

    def load(self, sp, kk):
        sp.dma_start(self.raw[kk % self.RAW][:, :], self.w_out[0, kk * P:(kk + 1) * P, :]
                     ).then_inc(self.loaded[kk % self.RAW], 16)

    def first_loads(self, sp):
        for kk in range(self.RAW):
            self.load(sp, kk)
        sp.dma_start(self.g[:, :], self.final_norm_g.rearrange("(a d) -> a d", a=1)[0].partition_broadcast(P)
                     ).then_inc(self.g_loaded, 16)


def project_out(nc, scr, out, x, weights):
    x_t = x[0].rearrange("(t p) d -> t p d", p=P)
    out_t = out[0].rearrange("(t p) d -> t p d", p=P)
    NC = D // CH
    RAW, w_raw, g = weights.RAW, weights.raw, weights.g
    ctx = ExitStack()
    with ctx:
        k = Pools(nc, ctx, "out")
        w = [k.sb(f"w{i}", [P, MIX_T, D], F32R) for i in (HI, LO)]
        mix = [[k.sb(f"mix{s}{i}", [P, MIX_T, P], F32R) for i in (HI, LO)] for s in range(2)]
        xin, y, o = ([k.sb(f"{n}{s}", [P, D]) for s in range(2)] for n in ("x", "y", "o"))
        junk = k.sb("junk", [P, D])
        st = k.sb("st", [P, 4])
        yps = [k.ps(f"yps{s}", [P, NC, CH]) for s in range(2)]
        names = ("w_hi w_lo mix_loaded0 mix_loaded1 x_loaded0 x_loaded1 projected added "
                 "squared mean_done filled rstd_done normed stored0 stored1 sp_goes").split()
        (w_hi, w_lo, mix_loaded0, mix_loaded1, x_loaded0, x_loaded1, projected, added,
         squared, mean_done, filled, rstd_done, normed, stored0, stored1, sp_goes) = map(k.sem, names)
        w_loaded, mix_loaded = weights.loaded, (mix_loaded0, mix_loaded1)
        x_loaded, stored = (x_loaded0, x_loaded1), (stored0, stored1)
        with nc.Block() as block:
            @block.sync
            def _(sp):
                def load(t, s):
                    for i in (HI, LO):
                        sp.dma_start(mix[s][i][:, :, :].bitcast(F32),
                                     scr.mix[i, bass.ds(t, 1)].rearrange("a p k t -> (a p) k t")
                                     ).then_inc(mix_loaded[s], 16)
                    sp.dma_start(xin[s][:, :], x_t[bass.ds(t, 1)].rearrange("a p d -> (a p) d")
                                 ).then_inc(x_loaded[s], 16)
                load(0, 0)
                for kk in range(RAW, MIX_T):
                    sp.wait_ge(w_lo, kk - RAW + 1)
                    weights.load(sp, kk)
                load(1, 1)
                with sp.Fori(1, TT // 2) as h:
                    for s in range(2):
                        t = 2 * h + s
                        sp.wait_ge(projected, t - 1)
                        sp.sem_inc(sp_goes, 1)
                        sp.wait_ge(added, t - 1)
                        sp.sem_inc(sp_goes, 1)
                        load(t, s)

            @block.tensor
            def _(pe):
                def tile(h, s, first):
                    t = 2 * h + s
                    pe.wait_ge(mix_loaded[s], 32 * (h + 1))
                    if not first:
                        pe.wait_ge(added, t - 1)
                    for kk in range(MIX_T):
                        if first and s == 0:
                            pe.wait_ge(w_lo, kk + 1)
                        for n, (a, b) in enumerate(PASSES):
                            for c in range(NC):
                                mm = nc.tensor.matmul(yps[s][:, c, :], mix[s][a][:, kk, :],
                                                      w[b][:, kk, c * CH:(c + 1) * CH],
                                                      start=(kk == 0 and n == 0), stop=(kk == MIX_T - 1 and n == 2))
                    mm.then_inc(projected, 1)
                for s in range(2):
                    tile(0, s, True)
                with pe.Fori(1, TT // 2) as h:
                    for s in range(2):
                        tile(h, s, False)

            @block.vector
            def _(dve):
                for kk in range(MIX_T):
                    dve.wait_ge(w_hi, kk + 1)
                    nc.vector.tensor_tensor(w[LO][:, kk, :], w_raw[kk % RAW][:, :], w[HI][:, kk, :].bitcast(F32),
                                            ALU.subtract).then_inc(w_lo, 1)
                dve.wait_ge(weights.g_loaded, 16)
                with dve.Fori(0, TT // 2) as h:
                    for s in range(2):
                        t = 2 * h + s
                        dve.wait_ge(x_loaded[s], 16 * (h + 1))
                        dve.wait_ge(projected, t + 1)
                        nc.vector.tensor_tensor(y[s][:, :], yps[s][:, :, :].rearrange("p c n -> p (c n)"), xin[s][:, :],
                                                ALU.add).then_inc(added, 1)
                        dve.wait_ge(squared, t + 1)
                        nc.vector.tensor_scalar(st[:, 1:2], st[:, 0:1], 1.0 / D, EPS, ALU.mult, ALU.add
                                                ).then_inc(mean_done, 1)
                        dve.wait_ge(rstd_done, t + 1)
                        dve.wait_ge(stored[s], 16 * h)
                        nc.vector.scalar_tensor_tensor(o[s][:, :], y[s][:, :], st[:, 3:4], g[:, :], ALU.mult, ALU.mult
                                                       ).then_inc(normed, 1)

            @block.gpsimd
            def _(pool):
                pool.memset(st[:, 2:3], -0.5).then_inc(filled, 1)
                pool.wait_ge(filled, 1)
                with pool.Fori(0, TT // 2) as h:
                    for s in range(2):
                        pool.wait_ge(mean_done, 2 * h + s + 1)
                        nc.gpsimd.tensor_tensor(st[:, 3:4], st[:, 1:2], st[:, 2:3], ALU.pow).then_inc(rstd_done, 1)

            @block.scalar
            def _(act):
                for kk in range(MIX_T):
                    act.wait_ge(w_loaded[kk % RAW], 16 * (kk // RAW + 1))
                    nc.scalar.activation(w[HI][:, kk, :], w_raw[kk % RAW][:, :], ACT.Copy).then_inc(w_hi, 1)
                with act.Fori(0, TT // 2) as h:
                    for s in range(2):
                        t = 2 * h + s
                        act.wait_ge(added, t + 1)
                        nc.scalar.activation(junk[:, :], y[s][:, :], ACT.Square, accum_out=st[:, 0:1]).then_inc(squared, 1)
                        act.wait_ge(normed, t + 1)
                        act.dma_start(out_t[bass.ds(t, 1)].rearrange("a p d -> (a p) d"), o[s][:, :]
                                      ).then_inc(stored[s], 16)
                for s in range(2):
                    act.wait_ge(stored[s], 16 * (TT // 2))


def hymba_block(nc, out, x, mem, norm_g, w_cols, w_tok, w_alpha_up, b_alpha, b_forget, gla_norm_g, mem_norm_g,
                w_mem_kv, w_out, final_norm_g):
    scr = Scratch(nc)
    ctx = ExitStack()
    with ctx:
        consts = Constants(nc, ctx)
        ident, ident_b, fox_mask, gla_mask = consts.ident, consts.ident_b, consts.fox_mask, consts.gla_mask
        h_ctx = ExitStack()
        with h_ctx:
            steps_ctx = ExitStack()
            with steps_ctx:
                tokens = TokenStage(nc, h_ctx, steps_ctx, scr, ident, x, norm_g, w_tok)
                memory_keys_values(nc, scr, consts, tokens, mem, mem_norm_g, w_mem_kv)
                kh = Pools(nc, h_ctx, "h")
                hT = [kh.sb(f"T{i}", [P, KT, T], F32R) for i in (HI, LO)]
                fglr = kh.sb("fglr", [P, TT, FGLR])
                project_tokens(nc, scr, tokens, hT, fglr, w_cols)
            project_columns(nc, scr, ident, tokens, hT, fglr, w_cols, b_forget)
        weights_out = OutWeights(nc, ctx, w_out, final_norm_g)
        fox_head, att_ctx = HeadTiles(nc, ctx, scr, fox=True), ExitStack()
        with att_ctx:
            att_head = HeadTiles(nc, att_ctx, scr, fox=False)
            gated_linear_attention(nc, scr, ident, gla_mask, w_alpha_up, b_alpha, gla_norm_g, (att_head, fox_head))
            softmax_attention(nc, scr, ident, ident_b, fox_mask, att_head, (weights_out,))
        softmax_attention(nc, scr, ident, ident_b, fox_mask, fox_head, ())
        project_out(nc, scr, out, x, weights_out)


_OUTS = [((1, T, D), "float32")]


def laid_out(inputs):
    import numpy as np

    a = {n: np.ascontiguousarray(inputs[n]) for n in (
        "x", "mem", "norm_g", "w_alpha_up", "b_alpha", "b_forget", "gla_norm_g", "mem_norm_g", "w_mem_kv",
        "w_out", "final_norm_g")}
    w = np.ascontiguousarray(inputs["w_in"])[0].reshape(KT, P, -1)
    starts = ([F_Q + P * i for i in range(3)] + [M_Q + P * i for i in range(2)] + [F_K + P * i for i in range(3)]
              + [G_GATE + P * i for i in range(3)] + [F_GATE + P * i for i in range(3)]
              + [M_GATE + P * i for i in range(2)] + [G_Q + P * i for i in range(6)])
    a["w_cols"] = np.ascontiguousarray(np.stack([w[:, :, c:c + P].transpose(1, 0, 2) for c in starts]))
    tok = np.concatenate([w[:, :, F_V:F_V + 384], w[:, :, F_FG:F_FG + FOX_H], w[:, :, G_LR:G_LR + GLA_R]], axis=2)
    a["w_tok"] = np.ascontiguousarray(tok.transpose(1, 0, 2))
    return a


def kernel(**inputs):
    import numpy as np
    import concourse.bacc as bacc
    from concourse.bass_utils import run_bass_kernel_spmd

    nc = bacc.Bacc("TRN2", target_bir_lowering=False, num_devices=1)
    arrays, args = {}, {}
    for name, a in laid_out(inputs).items():
        arrays[f"in_{name}"] = a
        args[name] = nc.dram_tensor(f"in_{name}", a.shape, mybir.dt.from_np(a.dtype), kind="ExternalInput").ap()
    shape, dtype = _OUTS[0]
    out = nc.dram_tensor("out_0", shape, mybir.dt.from_np(np.dtype(dtype)), kind="ExternalOutput").ap()
    hymba_block(nc, out=out, **args)
    r = run_bass_kernel_spmd(nc, [arrays], core_ids=[0])
    return r.results[0]["out_0"]
```
